# Optimizing a Trainium2 kernel written in Bass

```python
import jax, jax.numpy as jnp
from jax import lax
import numpy as np

D_MODEL = 2048
BATCH = 1
SEQ = 256
DEPTH = 1

EPS = 1e-6
SSD_WIDTH = D_MODEL // 2
SSD_HEAD_DIM = 64
SSD_HEADS = SSD_WIDTH // SSD_HEAD_DIM
SSD_GROUPS = 2
SSD_STATE = 128
SSD_CONV = 4
SSD_CHUNK = 128
ATT_WIDTH = D_MODEL - SSD_WIDTH
ATT_HEAD_DIM = 128
ATT_HEADS = ATT_WIDTH // ATT_HEAD_DIM
ATT_KV_HEADS = 4
IDX_HEADS = 16
IDX_HEAD_DIM = 64
IDX_TOPK_MAX = 256
Q_BLOCK = 128
D_FF = 4 * D_MODEL
MIX_WIDTH = SSD_WIDTH + ATT_WIDTH
DT_COL_SCALE = 0.1

N_Z = SSD_WIDTH
N_BC = SSD_GROUPS * SSD_STATE
CONV_CH = SSD_WIDTH + 2 * N_BC
N_DT = SSD_HEADS
N_Q = ATT_HEADS * ATT_HEAD_DIM
N_KV = ATT_KV_HEADS * ATT_HEAD_DIM
N_QI = IDX_HEADS * IDX_HEAD_DIM
N_KI = IDX_HEAD_DIM
N_WI = IDX_HEADS
IN_SIZES = (N_Z, CONV_CH, N_DT, N_Q, N_KV, N_KV, N_QI, N_KI, N_WI)
IN_WIDTH = N_Z + CONV_CH + N_DT + N_Q + 2 * N_KV + N_QI + N_KI + N_WI


def _split(t, sizes):
    pts = [int(v) for v in np.cumsum(sizes)[:-1]]
    return jnp.split(t, pts, axis=-1)

def rmsnorm(x, g):
    xf = x.astype(jnp.float32)
    y = xf * lax.rsqrt(jnp.mean(xf * xf, axis=-1, keepdims=True) + EPS)
    return (y * g.astype(jnp.float32)).astype(x.dtype)

def causal_dwconv(u, w, bias):
    ch = u.shape[-1]
    out = lax.conv_general_dilated(
        u, w[:, None, :], window_strides=(1,), padding=((SSD_CONV - 1, 0),),
        dimension_numbers=("NWC", "WIO", "NWC"), feature_group_count=ch)
    return out + bias

def ssd_chunked(xs, dt, a, bm, cm):
    b, l, h, p = xs.shape
    g, n = bm.shape[-2:]
    r = h // g
    q = SSD_CHUNK
    c = l // q
    xdt = (xs * dt[..., None]).reshape(b, c, q, g, r, p)
    adt = (dt * a).reshape(b, c, q, g, r)
    bm = bm.reshape(b, c, q, g, n)
    cm = cm.reshape(b, c, q, g, n)
    a_cum = jnp.cumsum(adt, axis=2)
    seg = a_cum[:, :, :, None] - a_cum[:, :, None, :]
    causal = jnp.tril(jnp.ones((q, q), dtype=bool))[None, None, :, :, None, None]
    decay = jnp.exp(jnp.where(causal, seg, -jnp.inf))
    cb = jnp.einsum("bclgn,bcsgn->bclsg", cm, bm)
    y_diag = jnp.einsum("bclsg,bclsgr,bcsgrp->bclgrp", cb, decay, xdt)
    decay_state = jnp.exp(a_cum[:, :, -1:] - a_cum)
    states = jnp.einsum("bcsgn,bcsgr,bcsgrp->bcgrpn", bm, decay_state, xdt)
    chunk_decay = jnp.exp(a_cum[:, :, -1])

    def step(carry, inp):
        st, dec = inp
        return carry * dec[..., None, None] + st, carry

    init = jnp.zeros((b, g, r, p, n), dtype=xs.dtype)
    _, prev = lax.scan(step, init, (jnp.swapaxes(states, 0, 1), jnp.swapaxes(chunk_decay, 0, 1)))
    prev = jnp.swapaxes(prev, 0, 1)
    y_off = jnp.einsum("bclgn,bcgrpn,bclgr->bclgrp", cm, prev, jnp.exp(a_cum))
    return (y_diag + y_off).reshape(b, l, h, p)

def dsa_attention(q, k, v, q_idx, k_idx, w_idx):
    b, l = q.shape[:2]
    topk = min(IDX_TOPK_MAX, l // 4)
    qb = min(Q_BLOCK, l)
    nb = l // qb
    rep = ATT_HEADS // ATT_KV_HEADS
    key_pos = jnp.arange(l)

    def to_blocks(t):
        return jnp.swapaxes(t.reshape(b, nb, qb, *t.shape[2:]), 0, 1)

    def one_block(args):
        q_b, qi_b, wi_b, start = args
        t_pos = start + jnp.arange(qb)
        s = jnp.einsum("bqhd,bsd->bqhs", qi_b, k_idx) * (IDX_HEAD_DIM ** -0.5)
        score = jnp.einsum("bqhs,bqh->bqs", jax.nn.relu(s), wi_b).astype(jnp.float32)
        admissible = key_pos[None, :] <= t_pos[:, None]
        score = jnp.where(admissible[None], score, -jnp.inf)
        _, sel = lax.top_k(score, topk)
        sel_ok = sel <= t_pos[None, :, None]
        k_sel = jax.vmap(lambda kk, ii: kk[ii])(k, sel)
        v_sel = jax.vmap(lambda vv, ii: vv[ii])(v, sel)
        qg = q_b.reshape(b, qb, ATT_KV_HEADS, rep, ATT_HEAD_DIM)
        logits = jnp.einsum("bqhgd,bqkhd->bqhgk", qg, k_sel).astype(jnp.float32) * (ATT_HEAD_DIM ** -0.5)
        logits = jnp.where(sel_ok[:, :, None, None, :], logits, -jnp.inf)
        prob = jax.nn.softmax(logits, axis=-1).astype(v.dtype)
        o = jnp.einsum("bqhgk,bqkhd->bqhgd", prob, v_sel)
        return o.reshape(b, qb, ATT_HEADS * ATT_HEAD_DIM)

    starts = jnp.arange(nb, dtype=jnp.int32) * qb
    out = lax.map(one_block, (to_blocks(q), to_blocks(q_idx), to_blocks(w_idx), starts))
    return jnp.swapaxes(out, 0, 1).reshape(b, l, ATT_HEADS * ATT_HEAD_DIM)

def hybrid_layer(x, g_mix, w_in, conv_w, conv_b, dt_bias, a_log, d_skip, g_ssd,
                 g_q, g_k, g_kidx, w_out, g_mlp, w_up, w_down):
    b, l, _ = x.shape
    h = rmsnorm(x, g_mix) @ w_in
    z, xbc, dt, q, k, v, qi, ki, wi = _split(h, IN_SIZES)

    xbc = jax.nn.silu(causal_dwconv(xbc, conv_w, conv_b))
    xs, bm, cm = _split(xbc, (SSD_WIDTH, N_BC, N_BC))
    xs_f = xs.astype(jnp.float32).reshape(b, l, SSD_HEADS, SSD_HEAD_DIM)
    dt_f = jax.nn.softplus(dt.astype(jnp.float32) + dt_bias.astype(jnp.float32))
    a = -jnp.exp(a_log.astype(jnp.float32))
    y = ssd_chunked(xs_f, dt_f, a,
                    bm.astype(jnp.float32).reshape(b, l, SSD_GROUPS, SSD_STATE),
                    cm.astype(jnp.float32).reshape(b, l, SSD_GROUPS, SSD_STATE))
    y = y + d_skip.astype(jnp.float32)[:, None] * xs_f
    y = y.reshape(b, l, SSD_WIDTH) * jax.nn.silu(z.astype(jnp.float32))
    yg = y.reshape(b, l, SSD_GROUPS, SSD_WIDTH // SSD_GROUPS)
    yg = yg * lax.rsqrt(jnp.mean(yg * yg, axis=-1, keepdims=True) + EPS)
    y_ssd = (yg.reshape(b, l, SSD_WIDTH) * g_ssd.astype(jnp.float32)).astype(x.dtype)

    q = rmsnorm(q.reshape(b, l, ATT_HEADS, ATT_HEAD_DIM), g_q)
    k = rmsnorm(k.reshape(b, l, ATT_KV_HEADS, ATT_HEAD_DIM), g_k)
    v = v.reshape(b, l, ATT_KV_HEADS, ATT_HEAD_DIM)
    qi = qi.reshape(b, l, IDX_HEADS, IDX_HEAD_DIM)
    ki = rmsnorm(ki, g_kidx)
    wi = wi * (IDX_HEADS ** -0.5)
    y_att = dsa_attention(q, k, v, qi, ki, wi)

    x = x + jnp.concatenate([y_ssd, y_att], axis=-1) @ w_out

    u = rmsnorm(x, g_mlp) @ w_up
    return x + jnp.square(jax.nn.relu(u)) @ w_down

def first_inputs(seed: int = 0) -> dict:
    key = jax.random.key(seed)
    ks = jax.random.split(key, 20)
    f32 = jnp.float32
    nrm = lambda k, shape, s: jax.random.normal(k, shape, f32) * s
    gain = lambda k, shape: 1.0 + 0.02 * jax.random.normal(k, shape, f32)

    x = jax.random.normal(ks[0], (BATCH, SEQ, D_MODEL), f32)
    col_scale = jnp.ones((IN_WIDTH,), f32).at[N_Z + CONV_CH:N_Z + CONV_CH + N_DT].set(DT_COL_SCALE)
    w_in = nrm(ks[1], (DEPTH, D_MODEL, IN_WIDTH), D_MODEL ** -0.5) * col_scale
    conv_w = nrm(ks[2], (DEPTH, SSD_CONV, CONV_CH), SSD_CONV ** -0.5)
    conv_b = nrm(ks[3], (DEPTH, CONV_CH), 0.01)
    u = jax.random.uniform(ks[4], (DEPTH, SSD_HEADS), f32)
    dt0 = jnp.exp(u * (jnp.log(0.1) - jnp.log(0.001)) + jnp.log(0.001))
    dt_bias = dt0 + jnp.log(-jnp.expm1(-dt0))
    a_log = jnp.log(jax.random.uniform(ks[5], (DEPTH, SSD_HEADS), f32, 1.0, 16.0))
    d_skip = 1.0 + 0.1 * jax.random.normal(ks[6], (DEPTH, SSD_HEADS), f32)
    return {
        "x": x,
        "g_mix": gain(ks[7], (DEPTH, D_MODEL)),
        "w_in": w_in,
        "conv_w": conv_w,
        "conv_b": conv_b,
        "dt_bias": dt_bias,
        "a_log": a_log,
        "d_skip": d_skip,
        "g_ssd": gain(ks[8], (DEPTH, SSD_WIDTH)),
        "g_q": gain(ks[9], (DEPTH, ATT_HEAD_DIM)),
        "g_k": gain(ks[10], (DEPTH, ATT_HEAD_DIM)),
        "g_kidx": gain(ks[11], (DEPTH, IDX_HEAD_DIM)),
        "w_out": nrm(ks[12], (DEPTH, MIX_WIDTH, D_MODEL), MIX_WIDTH ** -0.5),
        "g_mlp": gain(ks[13], (DEPTH, D_MODEL)),
        "w_up": nrm(ks[14], (DEPTH, D_MODEL, D_FF), D_MODEL ** -0.5),
        "w_down": nrm(ks[15], (DEPTH, D_FF, D_MODEL), D_FF ** -0.5),
    }

def first_block(x, g_mix, w_in, conv_w, conv_b, dt_bias, a_log, d_skip, g_ssd,
              g_q, g_k, g_kidx, w_out, g_mlp, w_up, w_down):
    for i in range(DEPTH):
        x = hybrid_layer(x, g_mix[i], w_in[i], conv_w[i], conv_b[i], dt_bias[i], a_log[i],
                         d_skip[i], g_ssd[i], g_q[i], g_k[i], g_kidx[i], w_out[i],
                         g_mlp[i], w_up[i], w_down[i])
    return x


N_MIXERS = 4
FOX_HEADS = 16
FOX_HEAD_DIM = D_MODEL // FOX_HEADS
LRU_WIDTH = 2688
LRU_BLOCKS = 16
LRU_BLOCK_DIM = LRU_WIDTH // LRU_BLOCKS
CONV_WIDTH = 4
LRU_C = 8.0
SB_HEADS = 16
SB_HEAD_DIM = D_MODEL // SB_HEADS
MLSTM_HEADS = 4
MLSTM_QK_DIM = D_MODEL // 2 // MLSTM_HEADS
MLSTM_V_DIM = D_MODEL // MLSTM_HEADS
MLSTM_CHUNK = 64
MLSTM_M_INIT = -1e30
D_FF_2 = 4 * D_MODEL


def _n_of(m):
    return (DEPTH - m + N_MIXERS - 1) // N_MIXERS

def rmsnorm_2(x, g):
    xf = x.astype(jnp.float32)
    y = xf * lax.rsqrt(jnp.mean(xf * xf, axis=-1, keepdims=True) + EPS)
    return (y * g.astype(jnp.float32)).astype(x.dtype)

def _heads(t, n_heads, d):
    b, s, _ = t.shape
    return t.reshape(b, s, n_heads, d).transpose(0, 2, 1, 3)

def _blocks_to_seq(out):
    nb, b, h, q, d = out.shape
    return out.transpose(1, 0, 3, 2, 4).reshape(b, nb * q, h * d)

def fox_attention(x, w_in, b_f, w_out):
    B, S, _ = x.shape
    H, dh = FOX_HEADS, FOX_HEAD_DIM
    proj = x @ w_in
    q, k, v, f_pre = jnp.split(proj, [D_MODEL, 2 * D_MODEL, 3 * D_MODEL], axis=-1)
    q, k, v = _heads(q, H, dh), _heads(k, H, dh), _heads(v, H, dh)
    log_f = jax.nn.log_sigmoid((f_pre + b_f).astype(jnp.float32)).transpose(0, 2, 1)
    cum = jnp.cumsum(log_f, axis=-1)
    nb = S // Q_BLOCK
    qb = q.reshape(B, H, nb, Q_BLOCK, dh).transpose(2, 0, 1, 3, 4)
    cb = cum.reshape(B, H, nb, Q_BLOCK).transpose(2, 0, 1, 3)
    pos_k = jnp.arange(S)
    scale = dh ** -0.5

    def block(args):
        i, q_i, c_i = args
        pos_q = i * Q_BLOCK + jnp.arange(Q_BLOCK)
        logits = jnp.einsum('bhqd,bhkd->bhqk', q_i, k).astype(jnp.float32) * scale
        logits = logits + c_i[..., :, None] - cum[..., None, :]
        logits = jnp.where(pos_k[None, :] <= pos_q[:, None], logits, -jnp.inf)
        p = jax.nn.softmax(logits, axis=-1)
        return jnp.einsum('bhqk,bhkd->bhqd', p.astype(v.dtype), v)

    out = lax.map(block, (jnp.arange(nb), qb, cb))
    return (_blocks_to_seq(out) @ w_out).astype(x.dtype)

def rglru_block(x, w_in, conv_w, conv_b, w_r, b_r, w_i, b_i, lam, w_out):
    B, S, _ = x.shape
    W, NB, bd = LRU_WIDTH, LRU_BLOCKS, LRU_BLOCK_DIM
    proj = x @ w_in
    gate, u = jnp.split(proj, [W], axis=-1)
    u_pad = jnp.pad(u, ((0, 0), (CONV_WIDTH - 1, 0), (0, 0)))
    u = conv_b + sum(u_pad[:, j:j + S, :] * conv_w[j] for j in range(CONV_WIDTH))
    ub = u.reshape(B, S, NB, bd)
    r = jax.nn.sigmoid((jnp.einsum('bsnd,nde->bsne', ub, w_r).reshape(B, S, W) + b_r).astype(jnp.float32))
    ig = jax.nn.sigmoid((jnp.einsum('bsnd,nde->bsne', ub, w_i).reshape(B, S, W) + b_i).astype(jnp.float32))
    log_a = LRU_C * r * jax.nn.log_sigmoid(lam.astype(jnp.float32))
    a = jnp.exp(log_a)
    bterm = jnp.sqrt(-jnp.expm1(2.0 * log_a)) * (ig * u.astype(jnp.float32))

    def combine(left, right):
        a1, b1 = left
        a2, b2 = right
        return a1 * a2, a2 * b1 + b2

    _, h = lax.associative_scan(combine, (a, bterm), axis=1)
    y = h * jax.nn.gelu(gate.astype(jnp.float32))
    return (y.astype(x.dtype) @ w_out).astype(x.dtype)

def stick_breaking_attention(x, w_in, w_out):
    B, S, _ = x.shape
    H, dh = SB_HEADS, SB_HEAD_DIM
    q, k, v = jnp.split(x @ w_in, 3, axis=-1)
    q, k, v = _heads(q, H, dh), _heads(k, H, dh), _heads(v, H, dh)
    nb = S // Q_BLOCK
    qb = q.reshape(B, H, nb, Q_BLOCK, dh).transpose(2, 0, 1, 3, 4)
    pos_k = jnp.arange(S)
    scale = dh ** -0.5

    def block(args):
        i, q_i = args
        pos_q = i * Q_BLOCK + jnp.arange(Q_BLOCK)
        strict = pos_k[None, :] < pos_q[:, None]
        z = jnp.einsum('bhqd,bhkd->bhqk', q_i, k).astype(jnp.float32) * scale
        log_beta = jax.nn.log_sigmoid(z)
        log_1mb = jnp.where(strict, jax.nn.log_sigmoid(-z), 0.0)
        after = lax.cumsum(log_1mb, axis=3, reverse=True) - log_1mb
        att = jnp.where(strict, jnp.exp(log_beta + after), 0.0)
        return jnp.einsum('bhqk,bhkd->bhqd', att.astype(v.dtype), v)

    out = lax.map(block, (jnp.arange(nb), qb))
    return (_blocks_to_seq(out) @ w_out).astype(x.dtype)

def mlstm_block(x, w_in, b_if, head_g, w_out):
    B, S, _ = x.shape
    H, dk, dv, L = MLSTM_HEADS, MLSTM_QK_DIM, MLSTM_V_DIM, MLSTM_CHUNK
    qk = H * dk
    proj = x @ w_in
    q, k, v, o_pre, g_pre = jnp.split(proj, [qk, 2 * qk, 2 * qk + D_MODEL, 2 * qk + 2 * D_MODEL], axis=-1)
    q, k, v = _heads(q, H, dk), _heads(k, H, dk) * (dk ** -0.5), _heads(v, H, dv)
    g_pre = g_pre.astype(jnp.float32).reshape(B, S, 2, H) + b_if.astype(jnp.float32)
    i_pre = g_pre[:, :, 0].transpose(0, 2, 1)
    log_f = jax.nn.log_sigmoid(g_pre[:, :, 1]).transpose(0, 2, 1)
    nc = S // L

    def chunks(t):
        return jnp.moveaxis(t.reshape(t.shape[:2] + (nc, L) + t.shape[3:]), 2, 0)

    causal = jnp.tril(jnp.ones((L, L), dtype=bool))

    def step(carry, xs):
        C, n, m = carry
        qc, kc, vc, lfc, ic = xs
        b = jnp.cumsum(lfc, axis=-1)
        g = b[..., -1]
        Dm = jnp.where(causal, b[..., :, None] - b[..., None, :] + ic[..., None, :], -jnp.inf)
        inter = b + m[..., None]
        m_t = jnp.maximum(inter, jnp.max(Dm, axis=-1))
        w_intra = jnp.exp(Dm - m_t[..., None])
        w_inter = jnp.exp(inter - m_t)
        s = jnp.einsum('bhtd,bhsd->bhts', qc, kc).astype(jnp.float32) * w_intra
        num = (w_inter[..., None] * jnp.einsum('bhtd,bhde->bhte', qc, C)
               + jnp.einsum('bhts,bhse->bhte', s, vc))
        den = w_inter * jnp.einsum('bhtd,bhd->bht', qc, n) + jnp.sum(s, axis=-1)
        h = num / jnp.maximum(jnp.abs(den), jnp.exp(-m_t))[..., None]
        wk = g[..., None] - b + ic
        m_new = jnp.maximum(g + m, jnp.max(wk, axis=-1))
        decay = jnp.exp(g + m - m_new)
        wk_e = jnp.exp(wk - m_new[..., None])
        C_new = decay[..., None, None] * C + jnp.einsum('bhs,bhsd,bhse->bhde', wk_e, kc, vc)
        n_new = decay[..., None] * n + jnp.einsum('bhs,bhsd->bhd', wk_e, kc)
        return (C_new, n_new, m_new), h

    init = (jnp.zeros((B, H, dk, dv), jnp.float32), jnp.zeros((B, H, dk), jnp.float32),
            jnp.full((B, H), MLSTM_M_INIT, jnp.float32))
    _, hs = lax.scan(step, init, (chunks(q), chunks(k), chunks(v), chunks(log_f), chunks(i_pre)))
    h = hs.transpose(1, 0, 3, 2, 4).reshape(B, S, H, dv)
    hn = rmsnorm_2(h, head_g.reshape(H, dv)).reshape(B, S, D_MODEL)
    y = jax.nn.sigmoid(o_pre.astype(jnp.float32)) * hn
    return (y.astype(x.dtype) @ w_out).astype(x.dtype)

def sqrelu_mlp(x, w1, w2):
    return (jnp.square(jax.nn.relu(x @ w1)) @ w2).astype(x.dtype)

def _dense(key, shape, fan_in):
    return jax.random.normal(key, shape, jnp.float32) * (fan_in ** -0.5)

def second_inputs(seed: int = 0) -> dict:
    key = jax.random.key(seed)
    ks = jax.random.split(key, 24)
    n0, n1, n2, n3 = _n_of(0), _n_of(1), _n_of(2), _n_of(3)
    D, W, NB, bd = D_MODEL, LRU_WIDTH, LRU_BLOCKS, LRU_BLOCK_DIM
    x = jax.random.normal(ks[0], (BATCH, SEQ, D), jnp.float32)
    norm_g = 1.0 + 0.02 * jax.random.normal(ks[1], (DEPTH, 4, D), jnp.float32)
    mlp_w1 = _dense(ks[2], (DEPTH, D, D_FF_2), D)
    mlp_w2 = _dense(ks[3], (DEPTH, D_FF_2, D), D_FF_2)
    fox_w_in = _dense(ks[4], (n0, D, 3 * D + FOX_HEADS), D)
    fox_b_f = 3.0 + 0.1 * jax.random.normal(ks[5], (n0, FOX_HEADS), jnp.float32)
    fox_w_out = _dense(ks[6], (n0, D, D), D)
    lru_w_in = _dense(ks[7], (n1, D, 2 * W), D)
    lru_conv_w = _dense(ks[8], (n1, CONV_WIDTH, W), CONV_WIDTH)
    lru_conv_b = 0.01 * jax.random.normal(ks[9], (n1, W), jnp.float32)
    lru_w_r = _dense(ks[10], (n1, NB, bd, bd), bd)
    lru_b_r = 0.01 * jax.random.normal(ks[11], (n1, W), jnp.float32)
    lru_w_i = _dense(ks[12], (n1, NB, bd, bd), bd)
    lru_b_i = 0.01 * jax.random.normal(ks[13], (n1, W), jnp.float32)
    a_c = jax.random.uniform(ks[14], (n1, W), jnp.float32, minval=0.9, maxval=0.999)
    p = a_c ** (1.0 / LRU_C)
    lru_lambda = jnp.log(p) - jnp.log1p(-p)
    lru_w_out = _dense(ks[15], (n1, W, D), W)
    sb_w_in = _dense(ks[16], (n2, D, 3 * D), D)
    sb_w_out = _dense(ks[17], (n2, D, D), D)
    mlstm_w_in = _dense(ks[18], (n3, D, 3 * D + 2 * MLSTM_HEADS), D)
    mlstm_b_if = jnp.stack([-1.0 + 0.1 * jax.random.normal(ks[19], (n3, MLSTM_HEADS), jnp.float32),
                            3.0 + 0.1 * jax.random.normal(ks[20], (n3, MLSTM_HEADS), jnp.float32)], axis=1)
    mlstm_head_g = 1.0 + 0.02 * jax.random.normal(ks[21], (n3, D), jnp.float32)
    mlstm_w_out = _dense(ks[22], (n3, D, D), D)
    return {'x': x, 'norm_g': norm_g, 'mlp_w1': mlp_w1, 'mlp_w2': mlp_w2,
            'fox_w_in': fox_w_in, 'fox_b_f': fox_b_f, 'fox_w_out': fox_w_out,
            'lru_w_in': lru_w_in, 'lru_conv_w': lru_conv_w, 'lru_conv_b': lru_conv_b,
            'lru_w_r': lru_w_r, 'lru_b_r': lru_b_r, 'lru_w_i': lru_w_i, 'lru_b_i': lru_b_i,
            'lru_lambda': lru_lambda, 'lru_w_out': lru_w_out,
            'sb_w_in': sb_w_in, 'sb_w_out': sb_w_out,
            'mlstm_w_in': mlstm_w_in, 'mlstm_b_if': mlstm_b_if, 'mlstm_head_g': mlstm_head_g,
            'mlstm_w_out': mlstm_w_out}

def second_block(x, norm_g, mlp_w1, mlp_w2, fox_w_in, fox_b_f, fox_w_out,
              lru_w_in, lru_conv_w, lru_conv_b, lru_w_r, lru_b_r, lru_w_i, lru_b_i,
              lru_lambda, lru_w_out, sb_w_in, sb_w_out,
              mlstm_w_in, mlstm_b_if, mlstm_head_g, mlstm_w_out):
    for i in range(DEPTH):
        m, j = i % N_MIXERS, i // N_MIXERS
        h = rmsnorm_2(x, norm_g[i, 0])
        if m == 0:
            h = fox_attention(h, fox_w_in[j], fox_b_f[j], fox_w_out[j])
        elif m == 1:
            h = rglru_block(h, lru_w_in[j], lru_conv_w[j], lru_conv_b[j], lru_w_r[j], lru_b_r[j],
                            lru_w_i[j], lru_b_i[j], lru_lambda[j], lru_w_out[j])
        elif m == 2:
            h = stick_breaking_attention(h, sb_w_in[j], sb_w_out[j])
        else:
            h = mlstm_block(h, mlstm_w_in[j], mlstm_b_if[j], mlstm_head_g[j], mlstm_w_out[j])
        x = x + rmsnorm_2(h, norm_g[i, 1])
        h = sqrelu_mlp(rmsnorm_2(x, norm_g[i, 2]), mlp_w1[i], mlp_w2[i])
        x = x + rmsnorm_2(h, norm_g[i, 3])
    return x


def setup_inputs(seed=0):
    out = dict(first_inputs(seed))
    for name, value in second_inputs(seed + 1).items():
        if name != "x":
            out[name + "_2"] = value
    return out


def reference(
    x, g_mix, w_in, conv_w, conv_b, dt_bias, a_log, d_skip, g_ssd, g_q, g_k, g_kidx, w_out,
    g_mlp, w_up, w_down, norm_g_2, mlp_w1_2, mlp_w2_2, fox_w_in_2, fox_b_f_2, fox_w_out_2,
    lru_w_in_2, lru_conv_w_2, lru_conv_b_2, lru_w_r_2, lru_b_r_2, lru_w_i_2, lru_b_i_2,
    lru_lambda_2, lru_w_out_2, sb_w_in_2, sb_w_out_2, mlstm_w_in_2, mlstm_b_if_2,
    mlstm_head_g_2, mlstm_w_out_2,
):
    x = first_block(
        x, g_mix, w_in, conv_w, conv_b, dt_bias, a_log, d_skip, g_ssd, g_q, g_k, g_kidx, w_out,
        g_mlp, w_up, w_down,
    )
    return second_block(
        x, norm_g_2, mlp_w1_2, mlp_w2_2, fox_w_in_2, fox_b_f_2, fox_w_out_2, lru_w_in_2,
        lru_conv_w_2, lru_conv_b_2, lru_w_r_2, lru_b_r_2, lru_w_i_2, lru_b_i_2, lru_lambda_2,
        lru_w_out_2, sb_w_in_2, sb_w_out_2, mlstm_w_in_2, mlstm_b_if_2, mlstm_head_g_2,
        mlstm_w_out_2,
    )


_drawn_inputs = setup_inputs


def setup_inputs(seed=0):
    import zlib

    import numpy as np

    out = dict(_drawn_inputs(seed))
    spreads = {}
    factors = {'conv_b': 6.945,
     'g_ssd': 12.521,
     'g_q': 8.0,
     'g_k': 8.0,
     'g_kidx': 4.6,
     'g_mlp': 3.274,
     'fox_b_f_2': 24.48,
     'norm_g_2': 8.0}
    for name, (base, spread) in spreads.items():
        noise = np.random.default_rng([zlib.crc32(name.encode()), seed]).standard_normal(out[name].shape)
        drawn = base * np.exp(spread * noise) if base else spread * noise
        out[name] = __import__('jax').numpy.asarray(drawn.astype(out[name].dtype))
    for name, factor in factors.items():
        out[name] = (out[name] * factor).astype(out[name].dtype)
    return out
```

```python
from contextlib import ExitStack

import concourse.bass as bass
from concourse import mybir

P = 128
TOK = 256
NT = TOK // P
D = 2048
KT = D // P
EPS = 1e-6
NEG = -1e30

SSD_W, HEADS_S, HD_S, GROUPS, STATE, TAPS = 1024, 16, 64, 2, 128, 4
HPG = HEADS_S // GROUPS
CONV_CH = SSD_W + 2 * GROUPS * STATE
HEADS_A, KV_A, HD = 8, 4, 128
HEADS_I, HD_I = 16, 64
TOPK = 64
C_Z = 0
C_XBC = C_Z + SSD_W
C_DT = C_XBC + CONV_CH
C_Q = C_DT + HEADS_S
C_K = C_Q + HEADS_A * HD
C_V = C_K + KV_A * HD
C_QI = C_V + KV_A * HD
C_KI = C_QI + HEADS_I * HD_I
C_WI = C_KI + HD_I
W_KW = HD_I + HEADS_I
W_SMALL = W_KW + HEADS_S
HEADS_F = 16
F = 4 * D
HALF = F // 2
UP = HALF // 512
DOWN = D // 512
HT = HALF // P

F32 = mybir.dt.float32
F32R = mybir.dt.float32r
BF16 = mybir.dt.bfloat16
ALU = mybir.AluOpType
ACT = mybir.ActivationFunctionType
AX = mybir.AxisListType.X
SCALE = HD ** -0.5


def hybrid_then_fox(nc, x, g_mix, w_in, conv_w, conv_b, dt_bias, a_log, d_skip, g_ssd, g_q, g_k,
                    g_kidx, w_out, g_mlp, w_up, w_down, norm_g, mlp_w1, mlp_w2, fox_w_in, fox_b_f,
                    fox_w_out, out):
    ctx = ExitStack()
    with ctx:
        def sem(name):
            return ctx.enter_context(nc.semaphore(name))

        def sb(name, shape, dt=F32, scope=ctx):
            return scope.enter_context(nc.sbuf_tensor(name, shape, dt))

        X = sb("X", [P, NT, D])
        XH = sb("XH", [P, KT, TOK], F32R)
        XL = sb("XL", [P, KT, TOK], F32R)
        raw = sb("raw", [P, 4, 4, 512])
        wh = sb("wh", [P, 2, 4, 512], F32R)
        wl = sb("wl", [P, 2, 4, 512], F32R)
        G = sb("G", [P, D])
        ident = sb("ident", [P, P])
        junk = sb("junk", [P, 512], BF16)
        ssq = sb("ssq", [P, NT, 4])
        rstd = sb("rstd", [P, NT])

        with ExitStack() as mix:
            Z = sb("Z", [P, NT, SSD_W], F32, mix)
            U = sb("U", [P, CONV_CH // P, TAPS - 1 + TOK], F32, mix)
            SM = sb("SM", [P, NT, W_SMALL], F32, mix)
            VB = sb("VB", [P, 3 * HEADS_S + HD_I], F32, mix)
            PR = sb("PR", [TAPS * 12 + 14, P], F32, mix)
            PC = sb("PC", [P, TAPS * 12 + 14], F32, mix)
            GS = sb("GS", [P, SSD_W], F32, mix)
            SQS = sb("SQS", [P, 64], F32, mix)
            DTS = sb("DTS", [P, 10, NT * HEADS_S], F32, mix)
            FMm = sb("FMm", [P, 3 * P], F32, mix)
            with ExitStack() as n:
                XN0 = sb("XN0", [P, NT, D], F32, n)
            with ExitStack() as a:
                QI = sb("QI", [P, HEADS_I // 2, TOK], F32, a)
                K = sb("K", [P, NT, KV_A * HD], F32, a)
                Q = sb("Q", [P, NT, HEADS_A * HD], F32, a)
                V = sb("V", [P, NT, KV_A * HD], F32, a)
                KI2 = sb("KI2", [P, NT, 2 * HD_I], F32, a)
                KIT = sb("KIT", [P, TOK], F32, a)
                SC = sb("SC", [P, 3 * P], F32, a)
                WK = sb("WK", [P, TOK], F32, a)
                M8 = sb("M8", [P, 8], F32, a)
                GT = sb("GT", [P, TOK], F32, a)
                EQ = sb("EQ", [P, TOK], F32, a)
                CS = sb("CS", [P, TOK], F32, a)
                R = sb("R", [P, 2, 512], F32, a)
                MK = sb("MK", [P, 3 * P], F32, a)
                Lm = sb("Lm", [P, 2, 3 * P], F32, a)
                PTm = sb("PTm", [P, 2, 3 * P], F32, a)
                QT = sb("QT", [P, HEADS_A, TOK], F32, a)
                KTt = sb("KTt", [P, KV_A, TOK], F32, a)
            with ExitStack() as b:
                XC = sb("XC", [P, CONV_CH // P, TOK], F32, b)
                XS = sb("XS", [P, NT, SSD_W], F32, b)
                XD = sb("XD", [P, NT, SSD_W], F32, b)
                BM = sb("BM", [P, NT, GROUPS * STATE], F32, b)
                E = sb("E", [P, HEADS_S, P], F32, b)
                Y = sb("Y", [P, NT, SSD_W], F32, b)
                ST = sb("ST", [P, GROUPS, 512], F32, b)
                CB = sb("CB", [P, NT * GROUPS, P], F32, b)
                Um = sb("Um", [P, P], F32, b)
                Vm = sb("Vm", [P, P], F32, b)
        HB = sb("HB", [P, NT, D])
        with ExitStack() as n:
            XN1 = sb("XN1", [P, NT, D], F32, n)
        with ExitStack() as fox:
            FQ = sb("FQ", [P, HEADS_F, TOK], F32, fox)
            FK = sb("FK", [P, HEADS_F, TOK], F32, fox)
            FV = sb("FV", [P, NT, D], F32, fox)
            FS = sb("FS", [P, 10, NT * HEADS_F], F32, fox)
            FB = sb("FB", [P, HEADS_F], F32, fox)
            NC = sb("NC", [P, NT, HEADS_F], F32, fox)
            NCT = sb("NCT", [HEADS_F, TOK], F32, fox)
            FMf = sb("FMf", [P, 3 * P], F32, fox)
            Uf = sb("Uf", [P, P], F32, fox)
            ONE = sb("ONE", [P, P], F32, fox)
            Lf = sb("Lf", [P, 2, 3 * P], F32, fox)
            PTf = sb("PTf", [P, 2, 3 * P], F32, fox)
            G1 = sb("G1", [P, D], F32, fox)
            FST = sb("FST", [P, 64], F32, fox)
        with ExitStack() as mlp:
            hh = sb("hh", [P, HT, TOK], F32R, mlp)
            hl = sb("hl", [P, HT, TOK], F32R, mlp)
            RB = sb("RB", [P, 2, 512], F32, mlp)

        bank = [ctx.enter_context(nc.psum_tensor(f"bank{i}", [P, 512], F32)) for i in range(8)]
        acc = [[bank[0], bank[1]], [bank[2], bank[3]]]
        side = bank[4:8]

        raw_landed = [sem(f"raw_landed{i}") for i in range(4)]
        hi_ready = sem("hi_ready")
        lo_ready = sem("lo_ready")
        chunk_used = sem("chunk_used")
        acc_freed = [[sem(f"acc_freed{p}{b}") for b in range(2)] for p in range(2)]
        side_full = [sem(f"side_full{i}") for i in range(4)]
        side_free = [sem(f"side_free{i}") for i in range(4)]
        x_landed = [sem(f"x_landed{i}") for i in range(2)]
        g_landed = sem("g_landed")
        g_used = sem("g_used")
        g1_landed = sem("g1_landed")
        vec_landed = sem("vec_landed")
        gs_landed = sem("gs_landed")
        fb_landed = sem("fb_landed")
        consts_ready = sem("consts_ready")
        pool_order = sem("pool_order")
        dve_order = sem("dve_order")
        act_order = sem("act_order")
        sum_ready = sem("sum_ready")
        ssq_ready = sem("ssq_ready")
        var_ready = sem("var_ready")
        std_ready = sem("std_ready")
        xn_ready = sem("xn_ready")
        xh_ready = sem("xh_ready")
        xl_ready = sem("xl_ready")
        sq_ready = sem("sq_ready")
        hh_ready = sem("hh_ready")
        hl_ready = sem("hl_ready")
        win_act = sem("win_act")
        win_dve = sem("win_dve")
        out_stored = sem("out_stored")
        x_final = sem("x_final")
        step = {n: sem(n) for n in (
            "pc_ready", "ki_var", "ki_std", "ki_rows", "kit_ready", "relu_scores", "scores_used",
            "qk_var", "qk_std", "qk_normed", "qt_ready", "logits_ready", "exp_ready", "probs_ready",
            "pt_ready", "oh_ready", "ol_ready", "conv_start", "conv_done", "silu_done", "xs_ready",
            "dt_a", "dt_b", "ea_ready", "adt_ready", "cum_ready", "decay_in", "decay_out", "m_ready",
            "cb_ready", "xd_ready", "st_ready", "z_gated", "y_ready", "yss_ready", "y_var", "y_std",
            "yn_ready", "f_a", "f_b", "lf_ready", "nc_ready", "nct_ready", "post_add")}

        block = ctx.enter_context(nc.Block())

        WIN = [("qi", C_QI, 512), ("qi", C_QI + 512, 512), ("k", C_K, 512), ("small", 0, W_SMALL),
               ("xbc", C_XBC, 512), ("xbc", C_XBC + 512, 512), ("xbc", C_XBC + 1024, 512),
               ("q", C_Q, 512), ("q", C_Q + 512, 512), ("v", C_V, 512),
               ("z", C_Z, 512), ("z", C_Z + 512, 512)]
        FOX = [("fq", 0, 512), ("fs", 3 * D, HEADS_F), ("fk", D, 512), ("fv", 2 * D, 512)]
        for n in range(1, 4):
            FOX += [("fq", n * 512, 512), ("fk", D + n * 512, 512), ("fv", 2 * D + n * 512, 512)]
        TFORM = ("qi", "xbc", "fq", "fk")
        B_WIN, O_WIN = 0, 0
        B_WOUT, O_WOUT = B_WIN + len(WIN), O_WIN + len(WIN)
        B_M1, O_M1 = B_WOUT + DOWN, O_WOUT + DOWN
        B_HALF, O_HALF = UP + 2 * DOWN, UP + DOWN
        B_FOX, O_FOX = B_M1 + 2 * B_HALF, O_M1 + 2 * O_HALF
        B_FOUT, O_FOUT = B_FOX + len(FOX), O_FOX + len(FOX)
        B_M2, O_M2 = B_FOUT + DOWN, O_FOUT + DOWN
        B_END = B_M2 + 2 * B_HALF
        assert O_HALF % 2 == 0

        uses = {}

        def use(name):
            uses[name] = (len(uses) % 4, len(uses) // 4)

        for n in range(8):
            use(("xt", 0, n))
        use("params")
        use("ki")
        for g in range(12):
            use(("score", g))
        for n in range(6):
            use(("qkt", n))
        for h in range(HEADS_A + 1):
            if h < HEADS_A:
                use(("S", 0, h))
            if h > 0:
                use(("PT", 0, h - 1))
                use(("O", 0, h - 1))
        for n in range(5):
            use(("xst", n))
        for c in range(NT):
            use(("cum", c))
        use("cb")
        use(("state", 0))
        use(("state", 1))
        for c in range(NT):
            for n in range(4):
                use(("seg", c, n))
            for g in range(GROUPS):
                use(("diag", c, g))
                if c:
                    use(("off", g))
        for n in range(4):
            use(("yt", n))
        for m in (1, 2):
            for n in range(8):
                use(("xt", m, n))
        use("fcum")
        use("fct")
        for h in range(HEADS_F + 1):
            if h < HEADS_F:
                use(("S", 1, h))
            if h > 0:
                use(("PT", 1, h - 1))
                use(("O", 1, h - 1))
        for n in range(8):
            use(("xt", 3, n))

        def score_heads(g):
            t, per, n = (0, 4, g) if g < 4 else (1, 2, g - 4)
            return t, per, [n % 2 + 2 * (per * (n // 2) + i) for i in range(per)]

        def side_bank(name):
            return side[uses[name][0]]

        def wait_full(eng, name):
            b, n = uses[name]
            eng.wait_ge(side_full[b], n + 1)

        def wait_free(eng, name):
            b, n = uses[name]
            if n:
                eng.wait_ge(side_free[b], n)

        def full(ins, name):
            ins.then_inc(side_full[uses[name][0]], 1)

        def free(ins, name):
            ins.then_inc(side_free[uses[name][0]], 1)

        def bc(ap, n):
            return ap.unsqueeze(2).broadcast_to([P, ap.shape[1], n])

        def heads(ap, n):
            return ap.rearrange("p (h d) -> p h d", d=n)

        def ctr(k):
            return (slice(0, P), slice(P, 3 * P))[k]

        @block.sync
        def _(sp):
            def chunk(w, b, j, k0, col, width, n0=0):
                if not (isinstance(b, int) and b == 0):
                    sp.wait_ge(lo_ready, 4 * b + j - 3)
                src = w[k0 * P:(k0 + 4) * P, col].rearrange("(k p) n -> p k n", p=P)
                sp.dma_start(raw[:, j, :, n0:n0 + width], src).then_inc(raw_landed[j], 16)

            def panel(w, b, k0, col, width=512):
                for j in range(4):
                    chunk(w, b, j, k0 + 4 * j, slice(col, col + width), width)

            def gain(src, used):
                sp.wait_ge(g_used, used)
                sp.dma_start(G[:, :], src.unsqueeze(0).broadcast_to([P, D])).then_inc(g_landed, 16)

            def mlp(w_a, w_b, b0, next_gain, used):
                for half in range(2):
                    b = b0 + half * B_HALF
                    panel(w_a, b, 0, half * HALF)
                    if half == 0:
                        gain(next_gain, used)
                    with sp.Fori(0, UP // 2 - 1) as i:
                        for s in (1, 2):
                            for j in range(4):
                                chunk(w_a, b + 2 * i + s, j, 4 * j,
                                      bass.ds(half * HALF + 512 * (2 * i + s), 512), 512)
                    panel(w_a, b + UP - 1, 0, half * HALF + 512 * (UP - 1))
                    for n in range(DOWN):
                        for m in range(2):
                            panel(w_b, b + UP + 2 * n + m, half * HT + 16 * m, 512 * n)

            for n, (kind, col, width) in enumerate(WIN):
                if kind == "small":
                    for j in range(4):
                        sp.wait_ge(lo_ready, 4 * (B_WIN + n) + j - 3)
                        for c0, w0, n0 in ((C_KI, W_KW, 0), (C_DT, HEADS_S, W_KW)):
                            src = w_in[0, 4 * j * P:(4 * j + 4) * P, c0:c0 + w0]
                            sp.dma_start(raw[:, j, :, n0:n0 + w0],
                                         src.rearrange("(k p) n -> p k n", p=P)).then_inc(raw_landed[j], 16)
                else:
                    panel(w_in[0], B_WIN + n, 0, col)
                if n == 1:
                    gain(g_mlp[0], 1)
            for n in range(DOWN):
                panel(w_out[0], B_WOUT + n, 0, 512 * n)
            mlp(w_up[0], w_down[0], B_M1, norm_g[0, 0], 2)
            for n, (kind, col, width) in enumerate(FOX):
                panel(fox_w_in[0], B_FOX + n, 0, col, width)
                if n == 0:
                    gain(norm_g[0, 2], 3)
            for n in range(DOWN):
                panel(fox_w_out[0], B_FOUT + n, 0, 512 * n)
                if n == 0:
                    sp.dma_start(G1[:, :], norm_g[0, 1].unsqueeze(0).broadcast_to([P, D])).then_inc(g1_landed, 16)
            mlp(mlp_w1[0], mlp_w2[0], B_M2, norm_g[0, 3], 4)
            for q in range(4):
                sp.wait_ge(x_final, q + 1)
                sp.dma_start(out[0].rearrange("(t p) n -> p t n", p=P)[:, :, 512 * q:512 * q + 512],
                             X[:, :, 512 * q:512 * q + 512]).then_inc(out_stored, 16)
            sp.wait_ge(out_stored, 64)

        def landed(b, j):
            if isinstance(b, int) and b <= B_WIN + 2:
                return 16 * (b + 1)
            return 16 * (b + 2)

        @block.gpsimd
        def _(pool):
            def causal(t):
                pool.memset(t[:, :], 0.0).then_inc(pool_order, 1)

            def causal_select(t):
                for c in (0, 2 * P):
                    last = pool.affine_select(out=t[:, c:c + P], in_=t[:, c:c + P], compare_op=ALU.is_ge,
                                              fill=NEG, base=0, pattern=[[-1, P]], channel_multiplier=1)
                return last

            pool.memset(ident[:, :], 0.0).then_inc(pool_order, 1)
            causal(FMm)
            pool.memset(U[:, :, 0:TAPS - 1], 0.0).then_inc(pool_order, 1)
            pool.wait_ge(pool_order, 3)
            pool.affine_select(out=ident[:, :], in_=ident[:, :], compare_op=ALU.not_equal, fill=1.0, base=0,
                               pattern=[[-1, P]], channel_multiplier=1).then_inc(consts_ready, 1)
            causal_select(FMm).then_inc(consts_ready, 1)
            pool.dma_start(PR[0:48, :], conv_w[0].rearrange("j (i p) -> (j i) p", p=P)).then_inc(vec_landed, 16)
            pool.dma_start(PR[48:60, :], conv_b[0].rearrange("(i p) -> i p", p=P)).then_inc(vec_landed, 16)
            pool.dma_start(PR[60:61, :], g_q[0:1]).then_inc(vec_landed, 16)
            pool.dma_start(PR[61:62, :], g_k[0:1]).then_inc(vec_landed, 16)
            for c, n, v in ((0, 16, dt_bias), (16, 16, a_log), (32, 16, d_skip), (48, 64, g_kidx)):
                pool.dma_start(VB[:, c:c + n], v[0].unsqueeze(0).broadcast_to([P, n])).then_inc(vec_landed, 16)
            pool.dma_start(GS[:, :], g_ssd[0].unsqueeze(0).broadcast_to([P, SSD_W])).then_inc(gs_landed, 16)
            pool.wait_ge(step["ol_ready"], 1)
            pool.memset(Um[:, :], 1.0).then_inc(pool_order, 1)
            pool.memset(Vm[:, :], 1.0).then_inc(pool_order, 1)
            pool.wait_ge(pool_order, 5)
            pool.affine_select(out=Um[:, :], in_=Um[:, :], compare_op=ALU.is_ge, fill=0.0, base=0,
                               pattern=[[1, P]], channel_multiplier=-1)
            pool.affine_select(out=Vm[:, :], in_=Vm[:, :], compare_op=ALU.is_gt, fill=0.0, base=0,
                               pattern=[[-1, P]], channel_multiplier=1).then_inc(consts_ready, 1)
            pool.wait_ge(chunk_used, 4 * B_FOX)
            causal(FMf)
            pool.memset(Uf[:, :], 1.0).then_inc(pool_order, 1)
            pool.memset(ONE[:, :], 1.0).then_inc(pool_order, 1)
            pool.wait_ge(pool_order, 8)
            causal_select(FMf)
            pool.affine_select(out=Uf[:, :], in_=Uf[:, :], compare_op=ALU.is_ge, fill=0.0, base=0,
                               pattern=[[1, P]], channel_multiplier=-1).then_inc(consts_ready, 1)
            pool.dma_start(FB[:, :], fox_b_f[0].unsqueeze(0).broadcast_to([P, HEADS_F])).then_inc(fb_landed, 16)
            pool.wait_ge(fb_landed, 16)

        @block.scalar
        def _(act):
            order = [0]

            def after(ins):
                order[0] += 1
                ins.then_inc(act_order, 1)
                act.wait_ge(act_order, order[0])

            def hi(b, j, width=512):
                act.wait_ge(raw_landed[j], landed(b, j))
                if not (isinstance(b, int) and b == 0 and j < 2):
                    act.wait_ge(chunk_used, 4 * b + j - 1)
                act.activation(wh[:, j % 2, :, 0:width], raw[:, j, :, 0:width], ACT.Copy).then_inc(hi_ready, 1)

            def std(name_in, n_in, name_out, dst, src):
                act.wait_ge(name_in, n_in)
                act.activation(dst, src, ACT.Sqrt).then_inc(name_out, 1)

            def take_xt(m, n, dst_h=XH):
                wait_full(act, ("xt", m, n))
                act.activation(dst_h[:, 2 * n:2 * n + 2, :].rearrange("p k t -> p (k t)"),
                               side_bank(("xt", m, n))[:, :], ACT.Copy).then_inc(xh_ready, 1)

            def norm(m, b, n_root):
                std(var_ready, n_root, std_ready, rstd[:, :], rstd[:, :])
                hi(b, 1)
                for n in range(8):
                    take_xt(m, n)

            def squares(q, src, n_sum):
                act.wait_ge(sum_ready, n_sum)
                act.wait_ge(ssq_ready, n_sum)
                after(act.activation(junk[:, :], src[:, 0, 512 * q:512 * q + 512], ACT.Square,
                                     accum_out=ssq[:, 0, q:q + 1]))
                act.activation(junk[:, :], src[:, 1, 512 * q:512 * q + 512], ACT.Square,
                               accum_out=ssq[:, 1, q:q + 1]).then_inc(ssq_ready, 1)

            def attn_exp(a, h, L, st):
                act.wait_ge(step["logits_ready"], a * HEADS_A + h + 1)
                for t in range(NT):
                    ins = act.activation(L[:, h % 2, ctr(t)], L[:, h % 2, ctr(t)], ACT.Exp,
                                         bias=st[:, 4 * (h % 4) + t:4 * (h % 4) + t + 1],
                                         accum_out=st[:, 4 * (h % 4) + 2 + t:4 * (h % 4) + 3 + t])
                ins.then_inc(step["exp_ready"], 1)

            def attn_pt(a, h, PT):
                wait_full(act, ("PT", a, h))
                ins = act.activation(PT[:, h % 2, :], side_bank(("PT", a, h))[:, 0:3 * P], ACT.Copy)
                free(ins, ("PT", a, h))

            def attn_out(a, h, kt):
                wait_full(act, ("O", a, h))
                act.activation(XH[:, kt, :], side_bank(("O", a, h))[:, 0:TOK], ACT.Copy)\
                   .then_inc(step["oh_ready"], 1)

            def attention(a, n_heads, L, PT, st, kt0):
                for i in range(n_heads + 1):
                    if i < n_heads:
                        attn_exp(a, i, L, st)
                    if i > 0:
                        attn_pt(a, i - 1, PT)
                        attn_out(a, i - 1, kt0 + i - 1)

            def take(kind, o, n, b):
                act.wait_ge(chunk_used, 4 * b + 4)
                src = acc[o % 2][1]
                if kind == "qi":
                    dst = QI[:, 4 * n + 2:4 * n + 4, :].rearrange("p f t -> p (f t)")
                elif kind == "xbc":
                    dst, src = U[:, 4 * n + 2:4 * n + 4, TAPS - 1:], src[:, :].rearrange("p (f t) -> p f t", f=2)
                elif kind == "small":
                    dst, src = SM[:, 1, :], src[:, 0:W_SMALL]
                elif kind in ("k", "v"):
                    dst = {"k": K, "v": V}[kind][:, 1, :]
                elif kind in ("q", "z"):
                    dst = {"q": Q, "z": Z}[kind][:, 1, 512 * n:512 * n + 512]
                elif kind in ("fq", "fk"):
                    dst = {"fq": FQ, "fk": FK}[kind][:, 4 * n + 2:4 * n + 4, :].rearrange("p f t -> p (f t)")
                elif kind == "fv":
                    dst = FV[:, 1, 512 * n:512 * n + 512]
                else:
                    dst, src = FS[:, 0, HEADS_F:2 * HEADS_F], src[:, 0:HEADS_F]
                act.activation(dst, src if kind in ("xbc", "small", "fs") else src[:, :], ACT.Copy,
                               scale=SCALE if kind == "fq" else 1.0).then_inc(acc_freed[o % 2][1], 1)

            def mlp(b0, o0, u0, q0, src):
                def relu(u, o_par, k, b):
                    if k == 0:
                        act.wait_ge(chunk_used, 4 * b + 4)
                    act.wait_ge(hl_ready, 2 * u + k + 1)
                    act.activation(RB[:, k, :], acc[o_par][k][:, :], ACT.Relu)\
                       .then_inc(acc_freed[o_par][k], 1)

                def high(u, k, tile):
                    act.wait_ge(sq_ready, 2 * u + k + 1)
                    act.activation(hh[:, tile, :], RB[:, k, :].rearrange("p (f t) -> p f t", f=2), ACT.Copy)\
                       .then_inc(hh_ready, 1)

                def hidden(j, u, o_par, b, tile0):
                    if j < 2:
                        relu(u, o_par, j, b)
                    if j in (1, 2):
                        k = j - 1
                        at = tile0 + 2 * k
                        high(u, k, slice(at, at + 2) if isinstance(at, int) else bass.ds(at, 2))

                for half in range(2):
                    b, o, u = b0 + half * B_HALF, o0 + half * O_HALF, u0 + half * UP
                    for j in range(2, 4):
                        hi(b, j)
                    with act.Fori(0, UP // 2 - 1) as i:
                        for s in (1, 2):
                            for j in range(4):
                                hi(b + 2 * i + s, j)
                                hidden(j, u + 2 * i + s - 1, (o + s - 1) % 2, b + 2 * i + s - 1,
                                       4 * (2 * i + s - 1))
                    for j in range(4):
                        hi(b + UP - 1, j)
                        hidden(j, u + UP - 2, (o + UP - 2) % 2, b + UP - 2, 4 * (UP - 2))
                    for n in range(DOWN):
                        for j in range(8):
                            hi(b + UP + 2 * n + j // 4, j % 4)
                            if n == 0 and j < 3:
                                hidden(j, u + UP - 1, (o + UP - 1) % 2, b + UP - 1, 4 * (UP - 1))
                            if half == 1 and n > 0 and j == 3:
                                squares(n - 1, src, q0 + n)
                    last = b + UP + 2 * DOWN
                    if half == 0:
                        hi(last, 0)
                        hi(last, 1)

            for t in range(NT):
                act.dma_start(X[:, t, :], x[0, t * P:(t + 1) * P, :]).then_inc(x_landed[t], 16)
            act.dma_start(G[:, :], g_mix[0].unsqueeze(0).broadcast_to([P, D])).then_inc(g_landed, 16)
            hi(0, 0)
            for t in range(NT):
                act.wait_ge(x_landed[t], 16)
                for q in range(4):
                    after(act.activation(junk[:, :], X[:, t, 512 * q:512 * q + 512], ACT.Square,
                                         accum_out=ssq[:, t, q:q + 1]))
            act.nop().then_inc(ssq_ready, 1)
            norm(0, 0, 1)
            seen = {}
            prev = None
            for n, (kind, col, width) in enumerate(WIN):
                for j in range(4):
                    if n or j >= 2:
                        hi(B_WIN + n, j, width)
                    if j == 0 and prev:
                        take(*prev)
                    if n == 1 and j == 1:
                        wait_full(act, "params")
                        free(act.activation(PC[:, :], side_bank("params")[:, 0:62], ACT.Copy), "params")
                prev = (kind, O_WIN + n, seen.get(kind, 0), B_WIN + n)
                seen[kind] = seen.get(kind, 0) + 1
            hi(B_WOUT, 0)
            hi(B_WOUT, 1)
            take(*prev)
            act.nop().then_inc(win_act, 1)
            std(step["ki_var"], 1, step["ki_std"], SQS[:, 2:4], SQS[:, 0:2])
            wait_full(act, "ki")
            ins = act.activation(KIT[:, :], side_bank("ki")[:, 0:TOK], ACT.Copy)
            free(ins, "ki")
            for g in range(12):
                wait_full(act, ("score", g))
                if g >= 2:
                    act.wait_ge(step["scores_used"], g - 1)
                ins = act.activation(R[:, g % 2, :], side_bank(("score", g))[:, :], ACT.Relu)
                free(ins, ("score", g))
            std(step["qk_var"], 1, step["qk_std"], SQS[:, 32:56], SQS[:, 8:32])
            for n in range(6):
                wait_full(act, ("qkt", n))
                dst = QT[:, 2 * n:2 * n + 2, :] if n < 4 else KTt[:, 2 * n - 8:2 * n - 6, :]
                ins = act.activation(dst.rearrange("p h t -> p (h t)"), side_bank(("qkt", n))[:, :], ACT.Copy,
                                     scale=PC[:, 60:61] if n < 4 else PC[:, 61:62])
                free(ins, ("qkt", n))
            attention(0, HEADS_A, Lm, PTm, SQS, 8)
            act.wait_ge(step["ol_ready"], 1)
            for i in range(12):
                act.activation(XC[:, i, :], U[:, i, 0:TOK], ACT.Identity, scale=PC[:, i:i + 1],
                               bias=PC[:, 48 + i:49 + i]).then_inc(step["conv_start"], 1)
            act.wait_ge(step["dt_a"], 1)
            act.activation(DTS[:, 2, :], DTS[:, 1, :], ACT.Exp).then_inc(step["dt_b"], 1)
            act.activation(DTS[:, 8, 0:16], VB[:, 16:32], ACT.Exp).then_inc(step["dt_b"], 1)
            act.wait_ge(step["dt_a"], 2)
            act.activation(DTS[:, 4, :], DTS[:, 3, :], ACT.Ln).then_inc(step["dt_b"], 1)
            for n in range(3):
                act.wait_ge(step["conv_done"], 4 * n + 4)
                act.activation(XC[:, 4 * n:4 * n + 4, :], XC[:, 4 * n:4 * n + 4, :], ACT.Silu)\
                   .then_inc(step["silu_done"], 1)
            for t in range(NT):
                act.activation(Z[:, t, :], Z[:, t, :], ACT.Silu).then_inc(step["z_gated"], 1)
            for n in range(5):
                wait_full(act, ("xst", n))
                dst = XS[:, n // 2, 512 * (n % 2):512 * (n % 2) + 512] if n < 4 else BM[:, :, :].rearrange("p t n -> p (t n)")
                free(act.activation(dst, side_bank(("xst", n))[:, :], ACT.Copy), ("xst", n))
            for c in range(NT):
                wait_full(act, ("cum", c))
                ins = act.activation(DTS[:, 9 if c else 8, :], side_bank(("cum", c))[:, 0:32], ACT.Exp)
                free(ins, ("cum", c))
            for g in range(GROUPS):
                wait_full(act, ("state", g))
                free(act.activation(ST[:, g, :], side_bank(("state", g))[:, :], ACT.Copy), ("state", g))
            for c in range(NT):
                for n in range(4):
                    wait_full(act, ("seg", c, n))
                    free(act.activation(E[:, 4 * n:4 * n + 4, :].rearrange("p h l -> p (h l)"),
                                        side_bank(("seg", c, n))[:, :], ACT.Exp), ("seg", c, n))
            act.wait_ge(step["y_ready"], 1)
            for t in range(NT):
                for g in range(GROUPS):
                    ins = act.activation(junk[:, :], Y[:, t, 512 * g:512 * g + 512], ACT.Square,
                                         accum_out=SQS[:, 2 * t + g:2 * t + g + 1])
                    ins.then_inc(step["yss_ready"], 1)
                    act.wait_ge(step["yss_ready"], 2 * t + g + 1)
            std(step["y_var"], 1, step["y_std"], SQS[:, 4:8], SQS[:, 4:8])
            for n in range(4):
                wait_full(act, ("yt", n))
                act.activation(XH[:, 2 * n:2 * n + 2, :].rearrange("p k t -> p (k t)"),
                               side_bank(("yt", n))[:, :], ACT.Copy).then_inc(xh_ready, 1)
            for n in range(DOWN):
                for j in range(4):
                    if n or j >= 2:
                        hi(B_WOUT + n, j)
                    if n and j == 2:
                        squares(n - 1, X, n)
            hi(B_M1, 0)
            squares(3, X, 4)
            norm(1, B_M1, 2)
            mlp(B_M1, O_M1, 0, 4, X)
            hi(B_FOX, 0)
            squares(3, X, 8)
            norm(2, B_FOX, 3)
            seen = {}
            prev = None
            for n, (kind, col, width) in enumerate(FOX):
                for j in range(4):
                    if n or j >= 2:
                        hi(B_FOX + n, j, width)
                    if j == 0 and prev:
                        take(*prev)
                prev = (kind, O_FOX + n, seen.get(kind, 0), B_FOX + n)
                seen[kind] = seen.get(kind, 0) + 1
            hi(B_FOUT, 0)
            hi(B_FOUT, 1)
            take(*prev)
            act.wait_ge(step["f_a"], 1)
            act.activation(FS[:, 2, :], FS[:, 1, :], ACT.Exp).then_inc(step["f_b"], 1)
            act.wait_ge(step["f_a"], 2)
            act.activation(FS[:, 4, :], FS[:, 3, :], ACT.Ln).then_inc(step["f_b"], 1)
            wait_full(act, "fct")
            free(act.activation(NCT[:, :], side_bank("fct")[0:HEADS_F, 0:TOK], ACT.Copy), "fct")
            attention(1, HEADS_F, Lf, PTf, FST, 0)
            for n in range(DOWN):
                for j in range(4):
                    if n or j >= 2:
                        hi(B_FOUT + n, j)
                    if n and j == 2:
                        squares(n - 1, HB, 8 + n)
            hi(B_M2, 0)
            squares(3, HB, 12)
            std(var_ready, 4, std_ready, rstd[:, :], rstd[:, :])
            for q in range(4):
                squares(q, X, 13 + q)
            norm(3, B_M2, 5)
            mlp(B_M2, O_M2, 2 * UP, 16, HB)
            squares(3, HB, 20)
            std(var_ready, 6, std_ready, rstd[:, :], rstd[:, :])

        @block.vector
        def _(dve):
            order = [0]

            def after(ins):
                order[0] += 1
                ins.then_inc(dve_order, 1)
                dve.wait_ge(dve_order, order[0])

            def lo(b, j, width=512):
                dve.wait_ge(hi_ready, 4 * b + j + 1)
                dve.tensor_tensor(wl[:, j % 2, :, 0:width], raw[:, j, :, 0:width],
                                  wh[:, j % 2, :, 0:width].bitcast(F32), ALU.subtract).then_inc(lo_ready, 1)

            def low_xt(name, n, sem_n):
                dve.wait_ge(xh_ready, sem_n)
                bk = side_bank(name)[:, :]
                dst = slice(2 * n, 2 * n + 2)
                ins = dve.tensor_tensor(XL[:, dst, :].rearrange("p k t -> p (k t)"), bk,
                                        XH[:, dst, :].bitcast(F32).rearrange("p k t -> p (k t)"), ALU.subtract)
                free(ins, name)

            def root(n_ssq, n_root):
                dve.wait_ge(ssq_ready, n_ssq)
                after(dve.tensor_reduce(rstd[:, :], ssq[:, :, :], AX, ALU.add))
                dve.tensor_scalar(rstd[:, :], rstd[:, :], 1.0 / D, EPS, ALU.mult, ALU.add).then_inc(var_ready, 1)
                dve.wait_ge(std_ready, n_root)
                after(dve.reciprocal(rstd[:, :], rstd[:, :]))

            def norm(m, n_ssq, n_root, n_g, n_xh, b):
                root(n_ssq, n_root)
                dve.wait_ge(g_landed, 16 * n_g)

                def quarter(q):
                    cols = slice(512 * q, 512 * q + 512)
                    for t in range(NT):
                        ins = dve.scalar_tensor_tensor(out=(XN1 if m else XN0)[:, t, cols], in0=X[:, t, cols],
                                                       scalar=rstd[:, t:t + 1], in1=G[:, cols],
                                                       op0=ALU.mult, op1=ALU.mult)
                        if q == 3 and t == 1:
                            ins.then_inc(g_used, 1)
                        else:
                            ins.then_inc(xn_ready, 1)
                quarter(0)
                quarter(1)
                lo(b, 1)
                for n in range(4):
                    low_xt(("xt", m, n), n, n_xh + n + 1)
                quarter(2)
                low_xt(("xt", m, 4), 4, n_xh + 5)
                quarter(3)
                for n in range(5, 8):
                    low_xt(("xt", m, n), n, n_xh + n + 1)

            def log1p_exp(T, ready, done, n0):
                dve.wait_ge(done, n0 + 1)
                dve.tensor_scalar(T[:, 3, :], T[:, 2, :], 1.0, None, ALU.add).then_inc(ready, 1)
                dve.wait_ge(ready, 2)
                after(dve.tensor_scalar(T[:, 5, :], T[:, 3, :], -1.0, None, ALU.add))
                after(dve.tensor_scalar(T[:, 6, :], T[:, 5, :], 0.0, None, ALU.is_equal))
                after(dve.tensor_tensor(T[:, 5, :], T[:, 5, :], T[:, 6, :], ALU.add))
                after(dve.reciprocal(T[:, 5, :], T[:, 5, :]))
                after(dve.tensor_tensor(T[:, 5, :], T[:, 5, :], T[:, 2, :], ALU.mult))
                dve.wait_ge(done, n0 + 2)
                after(dve.tensor_tensor(T[:, 5, :], T[:, 5, :], T[:, 4, :], ALU.mult))
                after(dve.tensor_tensor(T[:, 6, :], T[:, 6, :], T[:, 2, :], ALU.mult))
                after(dve.tensor_tensor(T[:, 6, :], T[:, 6, :], T[:, 5, :], ALU.add))

            def add_panel(o, b, q, dst, first):
                dve.wait_ge(chunk_used, 4 * b + 4)
                cols = slice(512 * q, 512 * q + 512)
                for t in range(NT):
                    if first:
                        ins = dve.tensor_copy(dst[:, t, cols], acc[o % 2][t][:, :])
                    else:
                        ins = dve.tensor_tensor(dst[:, t, cols], acc[o % 2][t][:, :], dst[:, t, cols], ALU.add)
                    ins.then_inc(acc_freed[o % 2][t], 1)

            def take(kind, o, n, b):
                dve.wait_ge(chunk_used, 4 * b + 4)
                src = acc[o % 2][0]
                if kind == "qi":
                    dst = QI[:, 4 * n:4 * n + 2, :].rearrange("p f t -> p (f t)")
                elif kind == "xbc":
                    dst = U[:, 4 * n:4 * n + 2, TAPS - 1:]
                elif kind == "small":
                    dst = SM[:, 0, :]
                elif kind in ("k", "v"):
                    dst = {"k": K, "v": V}[kind][:, 0, :]
                elif kind in ("q", "z"):
                    dst = {"q": Q, "z": Z}[kind][:, 0, 512 * n:512 * n + 512]
                elif kind in ("fq", "fk"):
                    dst = {"fq": FQ, "fk": FK}[kind][:, 4 * n:4 * n + 2, :].rearrange("p f t -> p (f t)")
                elif kind == "fv":
                    dst = FV[:, 0, 512 * n:512 * n + 512]
                else:
                    dst = FS[:, 0, 0:HEADS_F]
                if kind == "xbc":
                    ins = dve.tensor_copy(dst, src[:, :].rearrange("p (f t) -> p f t", f=2))
                elif kind == "fq":
                    ins = dve.tensor_scalar(dst, src[:, :], SCALE, None, ALU.mult)
                else:
                    ins = dve.tensor_copy(dst, src[:, 0:dst.shape[1]])
                ins.then_inc(acc_freed[o % 2][0], 1)

            def attn_logits(a, h, L, M, st):
                wait_full(dve, ("S", a, h))
                bk, s0 = side_bank(("S", a, h)), 4 * (h % 4)
                for t in range(NT):
                    ins = dve.tensor_tensor_reduce(L[:, h % 2, ctr(t)], bk[:, ctr(t)], M[:, ctr(t)], 1.0, -3e38,
                                                   ALU.add, ALU.max, st[:, s0 + t:s0 + t + 1])
                free(ins, ("S", a, h))
                dve.wait_ge(side_free[uses[("S", a, h)][0]], uses[("S", a, h)][1] + 1)
                dve.tensor_scalar(st[:, s0:s0 + 2], st[:, s0:s0 + 2], -1.0, None, ALU.mult)\
                   .then_inc(step["logits_ready"], 1)

            def attn_probs(a, h, L, st):
                s0 = 4 * (h % 4)
                dve.wait_ge(step["exp_ready"], a * HEADS_A + h + 1)
                after(dve.reciprocal(st[:, s0 + 2:s0 + 4], st[:, s0 + 2:s0 + 4]))
                for t in range(NT):
                    ins = dve.tensor_scalar(L[:, h % 2, ctr(t)], L[:, h % 2, ctr(t)],
                                            st[:, s0 + 2 + t:s0 + 3 + t], None, ALU.mult)
                ins.then_inc(step["probs_ready"], 1)

            def attn_low(a, h, kt):
                dve.wait_ge(step["oh_ready"], a * HEADS_A + h + 1)
                ins = dve.tensor_tensor(XL[:, kt, :], side_bank(("O", a, h))[:, 0:TOK],
                                        XH[:, kt, :].bitcast(F32), ALU.subtract)
                free(ins, ("O", a, h))

            def attention(a, n_heads, L, M, st, kt0):
                for i in range(n_heads + 1):
                    if i < n_heads:
                        attn_logits(a, i, L, M, st)
                        attn_probs(a, i, L, st)
                    if i > 0:
                        attn_low(a, i - 1, kt0 + i - 1)

            def mlp(b0, o0, u0, dst, fresh):
                def square(o_par, n, k):
                    dve.wait_ge(acc_freed[o_par][k], n)
                    dve.tensor_tensor(RB[:, k, :], RB[:, k, :], RB[:, k, :], ALU.mult).then_inc(sq_ready, 1)

                def low(u, k, tile):
                    dve.wait_ge(hh_ready, 2 * u + k + 1)
                    dve.tensor_tensor(hl[:, tile, :], RB[:, k, :].rearrange("p (f t) -> p f t", f=2),
                                      hh[:, tile, :].bitcast(F32), ALU.subtract).then_inc(hl_ready, 1)

                def hidden(j, u, o_par, n, tile0):
                    if j < 2:
                        square(o_par, n, j)
                    if j in (2, 3):
                        k = j - 2
                        at = tile0 + 2 * k
                        low(u, k, slice(at, at + 2) if isinstance(at, int) else bass.ds(at, 2))

                for half in range(2):
                    b, o, u = b0 + half * B_HALF, o0 + half * O_HALF, u0 + half * UP
                    for j in range(2, 4):
                        lo(b, j)
                    with dve.Fori(0, UP // 2 - 1) as i:
                        for s in (1, 2):
                            for j in range(4):
                                lo(b + 2 * i + s, j)
                                hidden(j, u + 2 * i + s - 1, (o + s - 1) % 2, i + (o + s - 1) // 2 + 1,
                                       4 * (2 * i + s - 1))
                    for j in range(4):
                        lo(b + UP - 1, j)
                        hidden(j, u + UP - 2, (o + UP - 2) % 2, (o + UP - 2) // 2 + 1, 4 * (UP - 2))
                    for n in range(DOWN):
                        for j in range(8):
                            lo(b + UP + 2 * n + j // 4, j % 4)
                            if n == 0 and j < 4:
                                hidden(j, u + UP - 1, (o + UP - 1) % 2, (o + UP - 1) // 2 + 1,
                                       4 * (UP - 1))
                            if n > 0 and j == 1:
                                add_panel(o + UP + n - 1, b + UP + 2 * n - 1, n - 1, dst, fresh and half == 0)
                                if half == 1:
                                    summed(o + UP + n - 1)
                    last = b + UP + 2 * DOWN
                    if half == 0:
                        lo(last, 0)
                        lo(last, 1)
                        add_panel(o + UP + DOWN - 1, last - 1, DOWN - 1, dst, fresh)

            def summed(o):
                for t in range(NT):
                    dve.wait_ge(acc_freed[o % 2][t], o // 2 + 1)
                dve.engine_nop().then_inc(sum_ready, 1)

            dve.wait_ge(x_landed[0], 16)
            dve.wait_ge(x_landed[1], 16)
            lo(0, 0)
            norm(0, 1, 1, 1, 0, 0)
            seen = {}
            prev = None
            for n, (kind, col, width) in enumerate(WIN):
                for j in range(4):
                    if n or j >= 2:
                        lo(B_WIN + n, j, width)
                    if j == 0 and prev:
                        take(*prev)
                prev = (kind, O_WIN + n, seen.get(kind, 0), B_WIN + n)
                seen[kind] = seen.get(kind, 0) + 1
            lo(B_WOUT, 0)
            lo(B_WOUT, 1)
            take(*prev)
            for o in (O_WOUT - 2, O_WOUT - 1):
                for t in range(NT):
                    dve.wait_ge(acc_freed[o % 2][t], o // 2 + 1)
            dve.wait_ge(vec_landed, 16 * 8)
            for t in range(NT):
                ins = dve.tensor_tensor_reduce(KI2[:, t, 0:HD_I], SM[:, t, 0:HD_I], SM[:, t, 0:HD_I], 1.0, 0.0,
                                               ALU.mult, ALU.add, SQS[:, t:t + 1])
                after(ins)
            dve.tensor_scalar(SQS[:, 0:2], SQS[:, 0:2], 1.0 / HD_I, EPS, ALU.mult, ALU.add)\
               .then_inc(step["ki_var"], 1)
            dve.wait_ge(step["ki_std"], 1)
            after(dve.reciprocal(SQS[:, 2:4], SQS[:, 2:4]))
            for t in range(NT):
                for k in range(2):
                    ins = dve.scalar_tensor_tensor(out=KI2[:, t, HD_I * k:HD_I * (k + 1)], in0=SM[:, t, 0:HD_I],
                                                   scalar=SQS[:, 2 + t:3 + t], in1=VB[:, 48:48 + HD_I],
                                                   op0=ALU.mult, op1=ALU.mult)
                    ins.then_inc(step["ki_rows"], 1)
            w_i = SM[:, :, HD_I:W_KW]
            after(dve.tensor_scalar(w_i, w_i, HEADS_I ** -0.5 * HD_I ** -0.5, None, ALU.mult))
            for g in range(12):
                t, per, hs = score_heads(g)
                b, n = uses[("score", g)]
                dve.wait_ge(side_free[b], n + 1)
                for i in range(per):
                    h, width = hs[i], P * (t + 1)
                    src, w = R[:, g % 2, width * i:width * (i + 1)], SM[:, t, HD_I + h:HD_I + h + 1]
                    if h == 0:
                        ins = dve.tensor_scalar(SC[:, ctr(t)], src, w, None, ALU.mult)
                    else:
                        ins = dve.scalar_tensor_tensor(out=SC[:, ctr(t)], in0=src, scalar=w, in1=SC[:, ctr(t)],
                                                       op0=ALU.mult, op1=ALU.add)
                    if i < per - 1:
                        after(ins)
                ins.then_inc(step["scores_used"], 1)
                dve.wait_ge(step["scores_used"], g + 1)
            dve.wait_ge(consts_ready, 2)
            after(dve.tensor_tensor(SC[:, :], SC[:, :], FMm[:, :], ALU.add))
            for t in range(NT):
                width = P * (t + 1)
                s = SC[:, ctr(t)]
                for r in range(TOPK // 8):
                    after(dve.max(M8[:, :], s if r == 0 else WK[:, 0:width]))
                    if r < TOPK // 8 - 1:
                        after(dve.match_replace(WK[:, 0:width], M8[:, :], s if r == 0 else WK[:, 0:width], -3e38))
                kth = M8[:, 7:8]
                after(dve.tensor_scalar(GT[:, 0:width], s, kth, None, ALU.is_gt, ALU.add, accum_out=SQS[:, 4:5]))
                after(dve.tensor_scalar(EQ[:, 0:width], s, kth, None, ALU.is_equal))
                after(dve.tensor_scalar(SQS[:, 4:5], SQS[:, 4:5], -1.0, float(TOPK), ALU.mult, ALU.add))
                after(dve.tensor_tensor_scan(CS[:, 0:width], EQ[:, 0:width], EQ[:, 0:width], 0.0,
                                             ALU.add, ALU.max))
                after(dve.scalar_tensor_tensor(out=EQ[:, 0:width], in0=CS[:, 0:width], scalar=SQS[:, 4:5],
                                               in1=EQ[:, 0:width], op0=ALU.is_le, op1=ALU.mult))
                after(dve.tensor_tensor(GT[:, 0:width], GT[:, 0:width], EQ[:, 0:width], ALU.add))
                after(dve.tensor_scalar(GT[:, 0:width], GT[:, 0:width], -1.0, -NEG, ALU.add, ALU.mult))
                after(dve.tensor_tensor(MK[:, ctr(t)], GT[:, 0:width], FMm[:, ctr(t)], ALU.add))
            for t in range(NT):
                for src, n, at in ((Q, HEADS_A, 8 + 8 * t), (K, KV_A, 24 + 4 * t)):
                    sq = QT[:, 0:4, :].rearrange("p h t -> p (h t)")[:, 0:n * HD]
                    after(dve.tensor_tensor(sq, src[:, t, :], src[:, t, :], ALU.mult))
                    after(dve.tensor_reduce(SQS[:, at:at + n], heads(sq, HD), AX, ALU.add))
            dve.tensor_scalar(SQS[:, 8:32], SQS[:, 8:32], 1.0 / HD, EPS, ALU.mult, ALU.add)\
               .then_inc(step["qk_var"], 1)
            dve.wait_ge(step["qk_std"], 1)
            after(dve.reciprocal(SQS[:, 32:56], SQS[:, 32:56]))
            after(dve.tensor_scalar(SQS[:, 32:48], SQS[:, 32:48], SCALE, None, ALU.mult))
            for t in range(NT):
                for src, n, at in ((Q, HEADS_A, 32 + 8 * t), (K, KV_A, 48 + 4 * t)):
                    dve.tensor_tensor(heads(src[:, t, :], HD), heads(src[:, t, :], HD),
                                      bc(SQS[:, at:at + n], HD), ALU.mult).then_inc(step["qk_normed"], 1)
            dve.wait_ge(step["qk_normed"], 4)
            attention(0, HEADS_A, Lm, MK, SQS, 8)
            b, n = uses[("O", 0, HEADS_A - 1)]
            dve.wait_ge(side_free[b], n + 1)
            dve.engine_nop().then_inc(step["ol_ready"], 1)
            for i in range(12):
                dve.wait_ge(step["conv_start"], i + 1)
                for j in range(1, TAPS):
                    ins = dve.scalar_tensor_tensor(out=XC[:, i, :], in0=U[:, i, j:j + TOK],
                                                   scalar=PC[:, 12 * j + i:12 * j + i + 1], in1=XC[:, i, :],
                                                   op0=ALU.mult, op1=ALU.add)
                    if j < TAPS - 1:
                        after(ins)
                ins.then_inc(step["conv_done"], 1)
            T = DTS
            v = T[:, 0, :].rearrange("p (t h) -> p t h", t=NT)
            after(dve.tensor_tensor(v, SM[:, :, W_KW:], VB[:, 0:16].unsqueeze(1).broadcast_to([P, NT, HEADS_S]), ALU.add))
            dve.scalar_tensor_tensor(out=T[:, 1, :], in0=T[:, 0, :], scalar=-1.0, in1=T[:, 0, :],
                                     op0=ALU.mult, op1=ALU.min).then_inc(step["dt_a"], 1)
            log1p_exp(T, step["dt_a"], step["dt_b"], 1)
            after(dve.scalar_tensor_tensor(out=T[:, 6, :], in0=T[:, 0, :], scalar=0.0, in1=T[:, 6, :],
                                           op0=ALU.max, op1=ALU.add))
            dve.scalar_tensor_tensor(out=T[:, 7, :].rearrange("p (t h) -> p t h", t=NT),
                                     in0=T[:, 6, :].rearrange("p (t h) -> p t h", t=NT), scalar=-1.0,
                                     in1=T[:, 8, 0:16].unsqueeze(1).broadcast_to([P, NT, HEADS_S]),
                                     op0=ALU.mult, op1=ALU.mult).then_inc(step["adt_ready"], 1)
            dve.wait_ge(step["adt_ready"], 1)
            dve.wait_ge(consts_ready, 3)
            for c in range(NT):
                bx, nx = uses[("xst", 2 * c + 1)]
                dve.wait_ge(side_free[uses[("xst", 2 * c)][0]], uses[("xst", 2 * c)][1] + 1)
                dve.wait_ge(side_free[bx], nx + 1)
                dve.tensor_tensor(heads(XD[:, c, :], HD_S), heads(XS[:, c, :], HD_S),
                                  bc(T[:, 6, 16 * c:16 * c + 16], HD_S), ALU.mult).then_inc(step["xd_ready"], 1)
            wait_full(dve, "cb")
            ins = dve.tensor_tensor(CB[:, :, :], side_bank("cb")[:, :].rearrange("p (g l) -> p g l", l=P),
                                    Um[:, :].unsqueeze(1).broadcast_to([P, NT * GROUPS, P]), ALU.mult)
            free(ins, "cb")
            bq, nq = uses[("cum", 0)]
            dve.wait_ge(side_free[bq], nq + 1)
            dve.wait_ge(step["xd_ready"], 1)
            dve.tensor_tensor(heads(Y[:, 0, :], HD_S), heads(XD[:, 0, :], HD_S),
                              bc(T[:, 8, 16:32], HD_S), ALU.mult).then_inc(step["st_ready"], 1)
            for c in range(NT):
                if c:
                    dve.wait_ge(side_full[uses[("diag", 0, 1)][0]], uses[("diag", 0, 1)][1] + 1)
                dve.tensor_tensor(E[:, :, :], Um[:, :].unsqueeze(1).broadcast_to([P, HEADS_S, P]),
                                  bc(T[:, 7, 16 * c:16 * c + 16], P), ALU.mult).then_inc(step["decay_in"], 1)
                dve.wait_ge(side_free[uses["cb"][0]], uses["cb"][1] + 1)
                for g in range(GROUPS):
                    for n in (2 * g, 2 * g + 1):
                        b, k = uses[("seg", c, n)]
                        dve.wait_ge(side_free[b], k + 1)
                    eg = E[:, HPG * g:HPG * (g + 1), :]
                    dve.tensor_tensor(eg, eg, CB[:, GROUPS * c + g, :].unsqueeze(1).broadcast_to([P, HPG, P]), ALU.mult)\
                       .then_inc(step["m_ready"], 1)
                if c == 0:
                    wait_full(dve, ("state", 1))
                after(dve.tensor_tensor(heads(Y[:, c, :], HD_S), heads(XS[:, c, :], HD_S),
                                        bc(VB[:, 32:48], HD_S), ALU.mult))
                for g in range(GROUPS):
                    yg = Y[:, c, 512 * g:512 * g + 512]
                    wait_full(dve, ("diag", c, g))
                    ins = dve.tensor_tensor(yg, side_bank(("diag", c, g))[:, :], yg, ALU.add)
                    free(ins, ("diag", c, g))
                    dve.wait_ge(side_free[uses[("diag", c, g)][0]], uses[("diag", c, g)][1] + 1)
                    if c:
                        wait_full(dve, ("off", g))
                        tmp = XD[:, 0, 512 * g:512 * g + 512]
                        bq, nq = uses[("cum", 1)]
                        dve.wait_ge(side_free[bq], nq + 1)
                        ins = dve.tensor_tensor(heads(tmp, HD_S), heads(side_bank(("off", g))[:, :], HD_S),
                                                bc(T[:, 9, HPG * g:HPG * (g + 1)], HD_S), ALU.mult)
                        free(ins, ("off", g))
                        dve.wait_ge(side_free[uses[("off", g)][0]], uses[("off", g)][1] + 1)
                        after(dve.tensor_tensor(yg, yg, tmp, ALU.add))
            for t in range(NT):
                dve.wait_ge(step["z_gated"], t + 1)
                ins = dve.tensor_tensor(Y[:, t, :], Y[:, t, :], Z[:, t, :], ALU.mult)
                if t == 0:
                    after(ins)
                else:
                    ins.then_inc(step["y_ready"], 1)
            dve.wait_ge(step["yss_ready"], 4)
            dve.tensor_scalar(SQS[:, 4:8], SQS[:, 0:4], 2.0 / SSD_W, EPS, ALU.mult, ALU.add)\
               .then_inc(step["y_var"], 1)
            dve.wait_ge(step["y_std"], 1)
            after(dve.reciprocal(SQS[:, 4:8], SQS[:, 4:8]))
            dve.wait_ge(gs_landed, 16)
            for g in range(GROUPS):
                for t in range(NT):
                    cols = slice(512 * g, 512 * g + 512)
                    dve.scalar_tensor_tensor(out=Y[:, t, cols], in0=Y[:, t, cols],
                                             scalar=SQS[:, 4 + 2 * t + g:5 + 2 * t + g], in1=GS[:, cols],
                                             op0=ALU.mult, op1=ALU.mult).then_inc(step["yn_ready"], 1)
            for n in range(4):
                low_xt(("yt", n), n, 8 + n + 1)
            for n in range(DOWN):
                for j in range(4):
                    if n or j >= 2:
                        lo(B_WOUT + n, j)
                    if n and j == 1:
                        add_panel(O_WOUT + n - 1, B_WOUT + n - 1, n - 1, X, False)
                        summed(O_WOUT + n - 1)
            lo(B_M1, 0)
            add_panel(O_WOUT + 3, B_WOUT + 3, 3, X, False)
            summed(O_WOUT + 3)
            norm(1, 5, 2, 2, 12, B_M1)
            for k in range(2):
                dve.memset(RB[:, k, :], 0.0).then_inc(hl_ready, 1)
            mlp(B_M1, O_M1, 0, X, False)
            lo(B_FOX, 0)
            add_panel(O_FOX - 1, B_FOX - 1, DOWN - 1, X, False)
            summed(O_FOX - 1)
            norm(2, 9, 3, 3, 20, B_FOX)
            seen = {}
            prev = None
            for n, (kind, col, width) in enumerate(FOX):
                for j in range(4):
                    if n or j >= 2:
                        lo(B_FOX + n, j, width)
                    if j == 0 and prev:
                        take(*prev)
                prev = (kind, O_FOX + n, seen.get(kind, 0), B_FOX + n)
                seen[kind] = seen.get(kind, 0) + 1
            lo(B_FOUT, 0)
            lo(B_FOUT, 1)
            take(*prev)
            for o in (O_FOX + 1,):
                for t in range(NT):
                    dve.wait_ge(acc_freed[o % 2][t], o // 2 + 1)
            dve.wait_ge(fb_landed, 16)
            T = FS
            v = T[:, 0, :].rearrange("p (t h) -> p t h", t=NT)
            after(dve.tensor_tensor(v, v, FB[:, :].unsqueeze(1).broadcast_to([P, NT, HEADS_F]), ALU.add))
            dve.scalar_tensor_tensor(out=T[:, 1, :], in0=T[:, 0, :], scalar=-1.0, in1=T[:, 0, :],
                                     op0=ALU.mult, op1=ALU.min).then_inc(step["f_a"], 1)
            log1p_exp(T, step["f_a"], step["f_b"], 0)
            after(dve.tensor_scalar(T[:, 5, :], T[:, 0, :], 0.0, None, ALU.min))
            dve.tensor_tensor(T[:, 7, :], T[:, 6, :], T[:, 5, :], ALU.subtract).then_inc(step["lf_ready"], 1)
            wait_full(dve, "fcum")
            ins = dve.tensor_copy(NC[:, :, :].rearrange("p t h -> p (t h)"), side_bank("fcum")[:, 0:32])
            free(ins, "fcum")
            dve.wait_ge(consts_ready, 4)
            attention(1, HEADS_F, Lf, FMf, FST, 0)
            for n in range(DOWN):
                for j in range(4):
                    if n or j >= 2:
                        lo(B_FOUT + n, j)
                    if n and j == 1:
                        add_panel(O_FOUT + n - 1, B_FOUT + n - 1, n - 1, HB, True)
                        summed(O_FOUT + n - 1)
            lo(B_M2, 0)
            add_panel(O_FOUT + 3, B_FOUT + 3, 3, HB, True)
            summed(O_FOUT + 3)

            def post(n_ssq, n_root, gain, final):
                root(n_ssq, n_root)
                for q in range(4):
                    cols = slice(512 * q, 512 * q + 512)
                    for t in range(NT):
                        ins = dve.scalar_tensor_tensor(out=HB[:, t, cols], in0=HB[:, t, cols],
                                                       scalar=rstd[:, t:t + 1], in1=gain[:, cols],
                                                       op0=ALU.mult, op1=ALU.mult)
                        ins.then_inc(step["post_add"], 1)
                    dve.wait_ge(step["post_add"], (8 if final else 0) + 2 * q + 2)
                    after(dve.tensor_tensor(X[:, 0, cols], X[:, 0, cols], HB[:, 0, cols], ALU.add))
                    dve.tensor_tensor(X[:, 1, cols], X[:, 1, cols], HB[:, 1, cols], ALU.add)\
                       .then_inc(x_final if final else sum_ready, 1)

            dve.wait_ge(g1_landed, 16)
            post(13, 4, G1, False)
            dve.wait_ge(sum_ready, 16)
            norm(3, 17, 5, 4, 28, B_M2)
            mlp(B_M2, O_M2, 2 * UP, HB, True)
            add_panel(O_M2 + 2 * O_HALF - 1, B_END - 1, DOWN - 1, HB, False)
            summed(O_M2 + 2 * O_HALF - 1)
            dve.wait_ge(g_landed, 16 * 5)
            post(21, 6, G, True)

        @block.tensor
        def _(pe):
            def acc_wait(o, n=None):
                n = o // 2 if n is None else n
                if not (isinstance(n, int) and n == 0):
                    for t in range(2):
                        pe.wait_ge(acc_freed[o % 2][t], n)

            def rows(b, j, o_par, first, last, k0, h=XH, l=XL, width=512):
                pe.wait_ge(lo_ready, 4 * b + j + 1)
                for kk in range(4):
                    for t in range(NT):
                        o = acc[o_par][t][:, 0:width]
                        sh, sl = (z[:, k0 + kk, t * P:(t + 1) * P] for z in (h, l))
                        mh, ml = wh[:, j % 2, kk, 0:width], wl[:, j % 2, kk, 0:width]
                        pe.matmul(o, sh, mh, start=first and kk == 0, stop=False)
                        pe.matmul(o, sh, ml, start=False, stop=False)
                        mm = pe.matmul(o, sl, mh, start=False, stop=last and kk == 3)
                mm.then_inc(chunk_used, 1)

            def cols(b, j, o_par, first, last, k0):
                pe.wait_ge(lo_ready, 4 * b + j + 1)
                for kk in range(4):
                    for f in range(4):
                        o = acc[o_par][f // 2][:, TOK * (f % 2):TOK * (f % 2 + 1)]
                        sh, sl = (z[:, j % 2, kk, f * P:(f + 1) * P] for z in (wh, wl))
                        mh, ml = XH[:, k0 + kk, :], XL[:, k0 + kk, :]
                        pe.matmul(o, sh, mh, start=first and kk == 0 and f % 2 == 0, stop=False,
                                  skip_group_check=True)
                        pe.matmul(o, sh, ml, start=False, stop=False, skip_group_check=True)
                        mm = pe.matmul(o, sl, mh, start=False, stop=last and kk == 3, skip_group_check=True)
                mm.then_inc(chunk_used, 1)

            def turn(m, n):
                wait_free(pe, ("xt", m, n))
                bk = side_bank(("xt", m, n))
                for i in range(4):
                    k, t = 2 * n + i // 2, i % 2
                    mm = pe.transpose(bk[:, i * P:(i + 1) * P], (XN1 if m else XN0)[:, t, k * P:(k + 1) * P], ident[:, :])
                full(mm, ("xt", m, n))

            def turn_quarter(m, q):
                if q < 3:
                    pe.wait_ge(xn_ready, 7 * m + 2 * q + 2)
                else:
                    pe.wait_ge(xn_ready, 7 * m + 7)
                    pe.wait_ge(g_used, m + 1)
                turn(m, 2 * q)
                turn(m, 2 * q + 1)

            def xt_wait(m, j, extra):
                for n in (2 * j, 2 * j + 1):
                    b, k = uses[("xt", m, n)]
                    pe.wait_ge(side_free[b], k + 1)

            def first_panel(form, m, b, o):
                turn_quarter(m, 0)
                turn_quarter(m, 1)
                for j in range(4):
                    if j == 0:
                        acc_wait(o)
                    xt_wait(m, j, 0)
                    form(b, j, o % 2, j == 0, j == 3, 4 * j)
                    if j < 2:
                        turn_quarter(m, j + 2)

            def panel(form, b, o, width=512):
                acc_wait(o)
                for j in range(4):
                    if form is cols:
                        cols(b, j, o % 2, j == 0, j == 3, 4 * j)
                    else:
                        rows(b, j, o % 2, j == 0, j == 3, 4 * j, width=width)

            def mlp(m, b0, o0, u0):
                for half in range(2):
                    b, o, u = b0 + half * B_HALF, o0 + half * O_HALF, u0 + half * UP
                    if half == 0:
                        first_panel(cols, m, b, o)
                    else:
                        panel(cols, b, o)
                    with pe.Fori(0, UP // 2 - 1) as i:
                        for s in (1, 2):
                            for k in range(2):
                                pe.wait_ge(acc_freed[(o + s) % 2][k], i + (o + s) // 2)
                            for j in range(4):
                                cols(b + 2 * i + s, j, (o + s) % 2, j == 0, j == 3, 4 * j)
                    panel(cols, b + UP - 1, o + UP - 1)
                    for n in range(DOWN):
                        on = o + UP + n
                        acc_wait(on)
                        for j in range(8):
                            if n == 0:
                                pe.wait_ge(hl_ready, 2 * (u + j) + 4)
                            rows(b + UP + 2 * n + j // 4, j % 4, on % 2, j == 0, j == 7, 4 * j, hh, hl)

            def attn_scores(a, h):
                wait_free(pe, ("S", a, h))
                bk = side_bank(("S", a, h))
                q, k = (FQ[:, h, :], FK[:, h, :]) if a else (QT[:, h, :], KTt[:, h // (HEADS_A // KV_A), :])
                for t in range(NT):
                    mm = pe.matmul(bk[:, ctr(t)], q[:, t * P:(t + 1) * P], k[:, 0:(t + 1) * P],
                                   start=True, stop=not a)
                    if a:
                        mm = pe.matmul(bk[:, ctr(t)], ident[0:HEADS_F, h:h + 1].broadcast_to([HEADS_F, P]),
                                       NCT[:, 0:(t + 1) * P], start=False, stop=True)
                full(mm, ("S", a, h))

            def attn_turn(a, h, L):
                pe.wait_ge(step["probs_ready"], a * HEADS_A + h + 1)
                wait_free(pe, ("PT", a, h))
                bk = side_bank(("PT", a, h))
                for i in range(3):
                    mm = pe.transpose(bk[:, i * P:(i + 1) * P], L[:, h % 2, i * P:(i + 1) * P], ident[:, :])
                full(mm, ("PT", a, h))

            def attn_values(a, h, PT):
                b, n = uses[("PT", a, h)]
                pe.wait_ge(side_free[b], n + 1)
                wait_free(pe, ("O", a, h))
                bk = side_bank(("O", a, h))
                vs = FV if a else V
                kv = h if a else h // (HEADS_A // KV_A)
                c = slice(kv * HD, (kv + 1) * HD)
                pe.matmul(bk[:, 0:TOK], vs[:, 0, c], PT[:, h % 2, 0:TOK], start=True, stop=False)
                mm = pe.matmul(bk[:, P:TOK], vs[:, 1, c], PT[:, h % 2, TOK:3 * P], start=False, stop=True)
                full(mm, ("O", a, h))

            def attention(a, n_heads, L, PT):
                for i in range(n_heads + 1):
                    if i < n_heads:
                        attn_scores(a, i)
                    if i > 0:
                        attn_turn(a, i - 1, L)
                        attn_values(a, i - 1, PT)

            def emptied(eng, name):
                b, n = uses[name]
                eng.wait_ge(side_free[b], n + 1)

            pe.wait_ge(consts_ready, 1)
            first_panel(cols, 0, B_WIN, O_WIN)
            pe.wait_ge(vec_landed, 16 * 8)
            wait_free(pe, "params")
            full(pe.transpose(side_bank("params")[:, 0:62], PR[:, :], ident[0:62, 0:62]), "params")
            for n, (kind, col, width) in enumerate(WIN):
                if n:
                    panel(cols if kind in TFORM else rows, B_WIN + n, O_WIN + n, width)
            pe.wait_ge(step["ki_rows"], 4)
            wait_free(pe, "ki")
            for t in range(NT):
                mm = pe.transpose(side_bank("ki")[:, t * P:(t + 1) * P], KI2[:, t, :], ident[:, :])
            full(mm, "ki")
            emptied(pe, "ki")
            for g in range(12):
                t, per, hs = score_heads(g)
                wait_free(pe, ("score", g))
                for i in range(per):
                    h, width = hs[i], P * (t + 1)
                    p0 = HD_I * (h % 2)
                    mm = pe.matmul(side_bank(("score", g))[:, width * i:width * (i + 1)],
                                   QI[p0:p0 + HD_I, h // 2, t * P:(t + 1) * P], KIT[p0:p0 + HD_I, 0:width],
                                   start=True, stop=True)
                full(mm, ("score", g))
            pe.wait_ge(step["qk_normed"], 4)
            for n in range(6):
                wait_free(pe, ("qkt", n))
                src, h0 = (Q, 2 * n) if n < 4 else (K, 2 * n - 8)
                for i in range(4):
                    h, t = h0 + i // 2, i % 2
                    mm = pe.transpose(side_bank(("qkt", n))[:, i * P:(i + 1) * P],
                                      src[:, t, h * HD:(h + 1) * HD], ident[:, :])
                full(mm, ("qkt", n))
            for n in range(6):
                emptied(pe, ("qkt", n))
            attention(0, HEADS_A, Lm, PTm)
            for n in range(5):
                pe.wait_ge(step["silu_done"], 3 if n == 4 else (n % 2) + 1)
                wait_free(pe, ("xst", n))
                for i in range(4):
                    t, k = (n // 2, 4 * (n % 2) + i) if n < 4 else (i // 2, 8 + i % 2)
                    mm = pe.transpose(side_bank(("xst", n))[:, i * P:(i + 1) * P], XC[:, k, t * P:(t + 1) * P],
                                      ident[:, :])
                full(mm, ("xst", n))
            pe.wait_ge(step["adt_ready"], 1)
            pe.wait_ge(consts_ready, 3)
            for c in range(NT):
                wait_free(pe, ("cum", c))
                adt = DTS[:, 7, 16 * c:16 * c + 16]
                pe.matmul(side_bank(("cum", c))[:, 0:16], Um[:, :], adt, start=True, stop=True)
                mm = pe.matmul(side_bank(("cum", c))[:, 16:32], Vm[:, :], adt, start=True, stop=True)
                full(mm, ("cum", c))
            wait_free(pe, "cb")
            for c in range(NT):
                for g in range(GROUPS):
                    tk = slice(c * P, (c + 1) * P)
                    mm = pe.matmul(side_bank("cb")[:, (2 * c + g) * P:(2 * c + g + 1) * P],
                                   XC[:, 8 + g, tk], XC[:, 10 + g, tk], start=True, stop=True)
            full(mm, "cb")
            pe.wait_ge(step["st_ready"], 1)
            emptied(pe, ("xst", 4))
            for g in range(GROUPS):
                wait_free(pe, ("state", g))
                full(pe.matmul(side_bank(("state", g))[:, :], BM[:, 0, g * STATE:(g + 1) * STATE],
                               Y[:, 0, 512 * g:512 * g + 512], start=True, stop=True), ("state", g))
            for c in range(NT):
                pe.wait_ge(step["decay_in"], c + 1)
                for n in range(4):
                    wait_free(pe, ("seg", c, n))
                    full(pe.matmul(side_bank(("seg", c, n))[:, :], Vm[:, :],
                                   E[:, 4 * n:4 * n + 4, :].rearrange("p h l -> p (h l)"),
                                   start=True, stop=True), ("seg", c, n))
                pe.wait_ge(step["xd_ready"], c + 1)
                for g in range(GROUPS):
                    wait_free(pe, ("diag", c, g))
                    pe.wait_ge(step["m_ready"], 2 * c + g + 1)
                    for i in range(HPG):
                        h = HPG * g + i
                        mm = pe.matmul(side_bank(("diag", c, g))[:, i * HD_S:(i + 1) * HD_S], E[:, h, :],
                                       XD[:, c, h * HD_S:(h + 1) * HD_S], start=True, stop=True)
                    full(mm, ("diag", c, g))
                    if c:
                        emptied(pe, ("state", g))
                        wait_free(pe, ("off", g))
                        full(pe.matmul(side_bank(("off", g))[:, :], XC[:, 10 + g, P:2 * P], ST[:, g, :],
                                       start=True, stop=True), ("off", g))
            for n in range(4):
                pe.wait_ge(step["yn_ready"], 2 * (n // 2) + 2)
                wait_free(pe, ("yt", n))
                for i in range(4):
                    k, t = 2 * n + i // 2, i % 2
                    mm = pe.transpose(side_bank(("yt", n))[:, i * P:(i + 1) * P], Y[:, t, k * P:(k + 1) * P],
                                      ident[:, :])
                full(mm, ("yt", n))
            for n in range(4):
                emptied(pe, ("yt", n))
            emptied(pe, ("O", 0, HEADS_A - 1))
            for n in range(DOWN):
                panel(rows, B_WOUT + n, O_WOUT + n)
            mlp(1, B_M1, O_M1, 0)
            first_panel(cols, 2, B_FOX, O_FOX)
            for n, (kind, col, width) in enumerate(FOX):
                if n:
                    panel(cols if kind in TFORM else rows, B_FOX + n, O_FOX + n, width)
            pe.wait_ge(step["lf_ready"], 1)
            pe.wait_ge(consts_ready, 4)
            wait_free(pe, "fcum")
            bk = side_bank("fcum")
            pe.matmul(bk[:, 0:16], Uf[:, :], FS[:, 7, 0:16], start=True, stop=True)
            pe.matmul(bk[:, 16:32], ONE[:, :], FS[:, 7, 0:16], start=True, stop=False)
            full(pe.matmul(bk[:, 16:32], Uf[:, :], FS[:, 7, 16:32], start=False, stop=True), "fcum")
            emptied(pe, "fcum")
            wait_free(pe, "fct")
            for t in range(NT):
                mm = pe.transpose(side_bank("fct")[0:HEADS_F, t * P:(t + 1) * P], NC[:, t, :], ident[:, :])
            full(mm, "fct")
            emptied(pe, "fct")
            for o in (O_FOUT - 1, O_FOUT - 2):
                acc_wait(o, o // 2 + 1)
            attention(1, HEADS_F, Lf, PTf)
            emptied(pe, ("O", 1, HEADS_F - 1))
            for n in range(DOWN):
                panel(rows, B_FOUT + n, O_FOUT + n)
            mlp(3, B_M2, O_M2, 2 * UP)


_INS = ['x', 'g_mix', 'w_in', 'conv_w', 'conv_b', 'dt_bias', 'a_log', 'd_skip', 'g_ssd', 'g_q', 'g_k', 'g_kidx',
        'w_out', 'g_mlp', 'w_up', 'w_down', 'norm_g_2', 'mlp_w1_2', 'mlp_w2_2', 'fox_w_in_2', 'fox_b_f_2',
        'fox_w_out_2']


def kernel(**inputs):
    import numpy as np
    import concourse.bacc as bacc
    from concourse.bass_utils import run_bass_kernel_spmd

    nc = bacc.Bacc("TRN2", target_bir_lowering=False, num_devices=1)
    arrays, args = {}, []
    for name in _INS:
        a = np.ascontiguousarray(inputs[name])
        arrays[f"in_{name}_dram"] = a
        args.append(nc.dram_tensor(f"in_{name}_dram", a.shape, mybir.dt.from_np(a.dtype),
                                   kind="ExternalInput").ap())
    args.append(nc.dram_tensor("out_dram", (1, TOK, D), F32, kind="ExternalOutput").ap())
    hybrid_then_fox(nc, *args)
    return run_bass_kernel_spmd(nc, [arrays], core_ids=[0]).results[0]["out_dram"]
```

```python
from contextlib import ExitStack

import concourse.bass as bass
from concourse import mybir

P = 128
TOK = 256
NT = TOK // P
D = 2048
KT = D // P
EPS = 1e-6
NEG = -1e30

SSD_W, HEADS_S, HD_S, GROUPS, STATE, TAPS = 1024, 16, 64, 2, 128, 4
HPG = HEADS_S // GROUPS
CONV_CH = SSD_W + 2 * GROUPS * STATE
HEADS_A, KV_A, HD = 8, 4, 128
HEADS_I, HD_I = 16, 64
TOPK = 64
C_Z = 0
C_XBC = C_Z + SSD_W
C_DT = C_XBC + CONV_CH
C_Q = C_DT + HEADS_S
C_K = C_Q + HEADS_A * HD
C_V = C_K + KV_A * HD
C_QI = C_V + KV_A * HD
C_KI = C_QI + HEADS_I * HD_I
C_WI = C_KI + HD_I
W_KW = HD_I + HEADS_I
W_SMALL = W_KW + HEADS_S
HEADS_F = 16
F = 4 * D
HALF = F // 2
UP = HALF // 512
DOWN = D // 512
HT = HALF // P

F32 = mybir.dt.float32
F32R = mybir.dt.float32r
BF16 = mybir.dt.bfloat16
ALU = mybir.AluOpType
ACT = mybir.ActivationFunctionType
AX = mybir.AxisListType.X
SCALE = HD ** -0.5


def hybrid_then_fox(nc, x, g_mix, w_in, conv_w, conv_b, dt_bias, a_log, d_skip, g_ssd, g_q, g_k,
                    g_kidx, w_out, g_mlp, w_up, w_down, norm_g, mlp_w1, mlp_w2, fox_w_in, fox_b_f,
                    fox_w_out, out):
    ctx = ExitStack()
    with ctx:
        def sem(name):
            return ctx.enter_context(nc.semaphore(name))

        def sb(name, shape, dt=F32, scope=ctx):
            return scope.enter_context(nc.sbuf_tensor(name, shape, dt))

        X = sb("X", [P, NT, D])
        XH = sb("XH", [P, KT, TOK], F32R)
        XL = sb("XL", [P, KT, TOK], F32R)
        raw = sb("raw", [P, 4, 4, 512])
        wh = sb("wh", [P, 2, 4, 512], F32R)
        wl = sb("wl", [P, 2, 4, 512], F32R)
        G = sb("G", [P, D])
        ident = sb("ident", [P, P])
        junk = sb("junk", [P, 512], BF16)
        ssq = sb("ssq", [P, NT, 4])
        rstd = sb("rstd", [P, NT])

        arena = -(-nc.sbuf_base // 32) * 32

        def region(start, *layers):
            end = start
            for layer in layers:
                at = start
                for name, shape, dt in layer:
                    T[name] = nc.alloc_sbuf_tensor_at(name, shape, dt, offset=at)
                    size = 2 if dt == BF16 else 4
                    for n in shape[1:]:
                        size *= n
                    at += -(-size // 32) * 32
                end = max(end, at)
            assert end <= nc.sbuf_usable_end
            return end

        T = {}
        at = region(arena, [("SM", [P, NT, W_SMALL], F32), ("VB", [P, 3 * HEADS_S + HD_I], F32),
                            ("PR", [TAPS * 12 + 14, P], F32), ("PC", [P, TAPS * 12 + 14], F32),
                            ("SQS", [P, 96], F32), ("DTS", [P, 10, NT * HEADS_S], F32),
                            ("FMm", [P, 3 * P], F32), ("Um", [P, P], F32), ("Vm", [P, P], F32),
                            ("MK", [P, 3 * P], F32), ("CB", [P, NT * GROUPS, P], F32),
                            ("BM", [P, NT, GROUPS * STATE], F32), ("Y", [P, NT, SSD_W], F32),
                            ("XD", [P, NT, SSD_W], F32)])
        at2 = region(at, [("E", [P, HEADS_S, P], F32)], [("GS", [P, SSD_W], F32)])
        at3 = region(at2, [("XC", [P, CONV_CH // P, TOK], F32)], [("PTm", [P, HEADS_A, 3 * P], F32)])
        region(at, [("XN0", [P, NT, D], F32)])
        at = region(at3, [("XDD", [P, SSD_W], F32)], [("ST", [P, GROUPS, 512], F32)])
        at = region(at, [("U", [P, CONV_CH // P, TAPS - 1 + TOK], F32)],
                    [("Q", [P, NT, HEADS_A * HD], F32), ("K", [P, NT, KV_A * HD], F32)],
                    [("Z", [P, NT, SSD_W], F32)])
        at = region(at, [("QI", [P, HEADS_I // 2, TOK], F32), ("R", [P, 2, 512], F32)],
                    [("QT", [P, HEADS_A, TOK], F32), ("KTt", [P, KV_A, TOK], F32)])
        at = region(at, [("KI2", [P, NT, 2 * HD_I], F32), ("KIT", [P, TOK], F32), ("SC", [P, 3 * P], F32),
                         ("WK", [P, TOK], F32), ("GT", [P, TOK], F32), ("EQ", [P, TOK], F32),
                         ("CS", [P, TOK], F32), ("M8", [P, 8], F32)],
                    [("Lm", [P, 4, 3 * P], F32), ("V", [P, NT, KV_A * HD], F32)])
        at = region(arena, [("HB", [P, NT, D], F32)], [("FQ", [P, HEADS_F, TOK], F32)])
        region(at, [("hh", [P, HT, TOK], F32R), ("hl", [P, HT, TOK], F32R), ("RB", [P, 2, 512], F32)])
        at = region(at, [("XN1", [P, NT, D], F32)], [("FK", [P, HEADS_F, TOK], F32)], [("G1", [P, D], F32)])
        region(at, [("FV", [P, NT, D], F32), ("PTf", [P, HEADS_F, 3 * P], F32), ("Lf", [P, 2, 3 * P], F32),
                    ("FS", [P, 10, NT * HEADS_F], F32), ("FB", [P, HEADS_F], F32),
                    ("NCB", [P, NT, HEADS_F], BF16), ("NC", [P, NT, 3 * HEADS_F], F32),
                    ("NCT", [3 * HEADS_F, TOK], BF16), ("OH", [3 * HEADS_F, HEADS_F], BF16),
                    ("FMf", [P, 3 * P], F32), ("Uf", [P, P], F32), ("ONE", [P, P], F32),
                    ("FST", [P, 16], F32)])
        SM, VB, PR, PC, SQS, DTS, FMm, Um, Vm, MK = (T[n] for n in "SM VB PR PC SQS DTS FMm Um Vm MK".split())
        CB, BM, Y, XD, E, GS, XC, PTm, XN0, XDD, ST = (T[n] for n in "CB BM Y XD E GS XC PTm XN0 XDD ST".split())
        U, Q, K, Z, QI, R, QT, KTt, KI2, KIT = (T[n] for n in "U Q K Z QI R QT KTt KI2 KIT".split())
        SC, WK, GT, EQ, CS, M8, Lm, V = (T[n] for n in "SC WK GT EQ CS M8 Lm V".split())
        HB, FQ, hh, hl, RB, XN1, FK, G1, FV, PTf = (T[n] for n in "HB FQ hh hl RB XN1 FK G1 FV PTf".split())
        Lf, FS, FB, NCB, NC, NCT, OH, FMf, Uf, ONE = (T[n] for n in "Lf FS FB NCB NC NCT OH FMf Uf ONE".split())
        FST = T["FST"]

        bank = [ctx.enter_context(nc.psum_tensor(f"bank{i}", [P, 512], F32)) for i in range(8)]
        acc = [[bank[0], bank[1]], [bank[2], bank[3]]]
        side = bank[4:8]

        raw_landed = [sem(f"raw_landed{i}") for i in range(4)]
        hi_ready = sem("hi_ready")
        lo_ready = sem("lo_ready")
        chunk_used = sem("chunk_used")
        acc_freed = [[sem(f"acc_freed{p}{b}") for b in range(2)] for p in range(2)]
        side_full = [sem(f"side_full{i}") for i in range(4)]
        side_free = [sem(f"side_free{i}") for i in range(4)]
        x_landed = [sem(f"x_landed{i}") for i in range(2)]
        g_landed = sem("g_landed")
        g_used = sem("g_used")
        g1_landed = sem("g1_landed")
        vec_landed = sem("vec_landed")
        gs_landed = sem("gs_landed")
        fb_landed = sem("fb_landed")
        consts_ready = sem("consts_ready")
        pool_order = sem("pool_order")
        dve_order = sem("dve_order")
        act_order = sem("act_order")
        sum_ready = sem("sum_ready")
        ssq_ready = sem("ssq_ready")
        var_ready = sem("var_ready")
        std_ready = sem("std_ready")
        xn_ready = sem("xn_ready")
        xh_ready = sem("xh_ready")
        xl_ready = sem("xl_ready")
        sq_ready = sem("sq_ready")
        hh_ready = sem("hh_ready")
        hl_ready = sem("hl_ready")
        out_stored = sem("out_stored")
        x_final = sem("x_final")
        step = {n: sem(n) for n in (
            "pc_ready", "ki_var", "ki_std", "ki_rows", "kit_ready", "relu_scores", "scores_used",
            "qk_var", "qk_std", "qk_normed", "qt_ready", "logits_ready", "exp_ready", "probs_ready",
            "pt_ready", "oh_ready", "ol_ready", "conv_start", "conv_done", "silu_done", "xs_ready",
            "dt_a", "dt_b", "ea_ready", "adt_ready", "cum_ready", "decay_in", "decay_out", "m_ready",
            "cb_ready", "xd_ready", "st_ready", "z_gated", "y_ready", "yss_ready", "y_var", "y_std",
            "yn_ready", "skip_ready", "fl_ready", "f_a", "f_b", "lf_ready", "nc_ready", "nct_ready", "post_add")}

        block = ctx.enter_context(nc.Block())

        WIN = [("qi", C_QI, 512), ("qi", C_QI + 512, 512), ("small", 0, W_SMALL),
               ("xbc", C_XBC, 512), ("xbc", C_XBC + 512, 512), ("xbc", C_XBC + 1024, 512),
               ("k", C_K, 512), ("q", C_Q, 512), ("q", C_Q + 512, 512),
               ("z", C_Z, 512), ("z", C_Z + 512, 512), ("v", C_V, 512)]
        FOX = [("fq", 0, 512), ("fk", D, 512), ("fs", 3 * D, HEADS_F)]
        for n in range(1, 4):
            FOX += [("fq", n * 512, 512), ("fk", D + n * 512, 512)]
        FOX += [("fv", 2 * D + n * 512, 512) for n in range(4)]
        TFORM = ("qi", "xbc", "fq", "fk")
        B_WIN, O_WIN = 0, 0
        B_WOUT, O_WOUT = B_WIN + len(WIN), O_WIN + len(WIN)
        B_M1, O_M1 = B_WOUT + DOWN, O_WOUT + DOWN
        B_HALF, O_HALF = UP + 2 * DOWN, UP + DOWN
        B_FOX, O_FOX = B_M1 + 2 * B_HALF, O_M1 + 2 * O_HALF
        B_FOUT, O_FOUT = B_FOX + len(FOX), O_FOX + len(FOX)
        B_M2, O_M2 = B_FOUT + DOWN, O_FOUT + DOWN
        B_END = B_M2 + 2 * B_HALF
        assert O_HALF % 2 == 0

        uses = {}

        def use(name):
            uses[name] = (len(uses) % 4, len(uses) // 4)

        MIX_AT = {4: ["params"], 14: ["ki"], 15: [("score", 0), ("score", 1)],
                  16: [("cum", 0), ("cum", 1), ("score", 2), ("score", 3)],
                  21: [("seg", 0, 0), ("seg", 0, 1)], 22: [("seg", 0, 2), ("seg", 0, 3)],
                  29: [("xst", 0), ("xst", 1)], 30: [("xst", 2), ("xst", 3)], 31: [("xst", 4), "cb"],
                  34: [("diag", 0, 0), ("diag", 0, 1)],
                  36: [("state", 0), ("state", 1), ("seg", 1, 0), ("seg", 1, 1)],
                  37: [("seg", 1, 2), ("seg", 1, 3)],
                  38: [("qkt", n) for n in range(3)], 39: [("qkt", n) for n in range(3, 6)],
                  40: [("diag", 1, 0), ("diag", 1, 1)],
                  41: [("off", 0), ("off", 1), ("S", 0, 0)], 42: [("S", 0, 1)],
                  43: [("S", 0, 2), ("S", 0, 3), ("PT", 0, 0)], 44: [("S", 0, 4), ("S", 0, 5), ("PT", 0, 1)],
                  45: [("S", 0, 6), ("S", 0, 7), ("PT", 0, 2), ("PT", 0, 3)],
                  46: [("PT", 0, 4), ("PT", 0, 5)],
                  48: [("yt", 0), ("yt", 1)], 49: [("PT", 0, 6), ("PT", 0, 7), ("yt", 2), ("yt", 3)],
                  50: [("O", 0, n) for n in range(4)], 51: [("O", 0, n) for n in range(4, 8)]}
        for g in range(4, 12, 2):
            MIX_AT[15 + g // 2] = [("score", g), ("score", g + 1)]
        FOX_S, FOX_PT = 19, 21
        FOX_O = {0: 41, 1: 42, 2: 43, 3: 44, 4: 45, 5: 46, 6: 47, 7: 48, 8: 49, 9: 50, 10: 51, 11: 51}
        FOX_AT = {n: [] for n in range(54)}
        FOX_AT[14].append("fcum")
        FOX_AT[17].append("fct")
        for h in range(HEADS_F):
            FOX_AT[FOX_S + 2 * h].append(("S", 1, h))
            FOX_AT[FOX_PT + 2 * h].append(("PT", 1, h))
        for h in range(HEADS_F):
            FOX_AT[FOX_O.get(h, 52 if h < 14 else 53)].append(("O", 1, h))
        for n in range(8):
            use(("xt", 0, n))
        for n in sorted(MIX_AT):
            for u in MIX_AT[n]:
                use(u)
        for m in (1, 2):
            for n in range(8):
                use(("xt", m, n))
        for n in sorted(FOX_AT):
            for u in FOX_AT[n]:
                use(u)
        for n in range(8):
            use(("xt", 3, n))

        def score_heads(g):
            t, per, n = (0, 4, g) if g < 4 else (1, 2, g - 4)
            return t, per, [n % 2 + 2 * (per * (n // 2) + i) for i in range(per)]

        def side_bank(name):
            return side[uses[name][0]]

        def wait_full(eng, name):
            b, n = uses[name]
            eng.wait_ge(side_full[b], n + 1)

        def wait_emptied(eng, name):
            b, n = uses[name]
            eng.wait_ge(side_free[b], n + 1)

        def wait_free(eng, name):
            b, n = uses[name]
            if n:
                eng.wait_ge(side_free[b], n)

        def full(ins, name):
            ins.then_inc(side_full[uses[name][0]], 1)

        def free(ins, name):
            ins.then_inc(side_free[uses[name][0]], 1)

        def bc(ap, n):
            return ap.unsqueeze(2).broadcast_to([P, ap.shape[1], n])

        def heads(ap, n):
            return ap.rearrange("p (h d) -> p h d", d=n)

        def ctr(k):
            return (slice(0, P), slice(P, 3 * P))[k]

        @block.sync
        def _(sp):
            def chunk(w, b, j, k0, col, width, n0=0):
                if not (isinstance(b, int) and b == 0):
                    sp.wait_ge(lo_ready, 4 * b + j - 3)
                src = w[k0 * P:(k0 + 4) * P, col].rearrange("(k p) n -> p k n", p=P)
                sp.dma_start(raw[:, j, :, n0:n0 + width], src).then_inc(raw_landed[j], 16)

            def panel(w, b, k0, col, width=512):
                for j in range(4):
                    chunk(w, b, j, k0 + 4 * j, slice(col, col + width), width)

            def gain(src, used):
                sp.wait_ge(g_used, used)
                sp.dma_start(G[:, :], src.unsqueeze(0).broadcast_to([P, D])).then_inc(g_landed, 16)

            def mlp(w_a, w_b, b0, next_gain, used):
                for half in range(2):
                    b = b0 + half * B_HALF
                    panel(w_a, b, 0, half * HALF)
                    if half == 0:
                        gain(next_gain, used)
                    with sp.Fori(0, UP // 2 - 1) as i:
                        for s in (1, 2):
                            for j in range(4):
                                chunk(w_a, b + 2 * i + s, j, 4 * j,
                                      bass.ds(half * HALF + 512 * (2 * i + s), 512), 512)
                    panel(w_a, b + UP - 1, 0, half * HALF + 512 * (UP - 1))
                    for n in range(DOWN):
                        for m in range(2):
                            panel(w_b, b + UP + 2 * n + m, half * HT + 16 * m, 512 * n)

            for n, (kind, col, width) in enumerate(WIN):
                if kind == "small":
                    for j in range(4):
                        sp.wait_ge(lo_ready, 4 * (B_WIN + n) + j - 3)
                        for c0, w0, n0 in ((C_KI, W_KW, 0), (C_DT, HEADS_S, W_KW)):
                            src = w_in[0, 4 * j * P:(4 * j + 4) * P, c0:c0 + w0]
                            sp.dma_start(raw[:, j, :, n0:n0 + w0],
                                         src.rearrange("(k p) n -> p k n", p=P)).then_inc(raw_landed[j], 16)
                else:
                    panel(w_in[0], B_WIN + n, 0, col)
                if n == 1:
                    gain(g_mlp[0], 1)
            for n in range(DOWN):
                panel(w_out[0], B_WOUT + n, 0, 512 * n)
            mlp(w_up[0], w_down[0], B_M1, norm_g[0, 0], 2)
            for n, (kind, col, width) in enumerate(FOX):
                panel(fox_w_in[0], B_FOX + n, 0, col, width)
                if n == 0:
                    gain(norm_g[0, 2], 3)
            for n in range(DOWN):
                panel(fox_w_out[0], B_FOUT + n, 0, 512 * n)
                if n == 0:
                    sp.dma_start(G1[:, :], norm_g[0, 1].unsqueeze(0).broadcast_to([P, D])).then_inc(g1_landed, 16)
            mlp(mlp_w1[0], mlp_w2[0], B_M2, norm_g[0, 3], 4)
            for q in range(4):
                sp.wait_ge(x_final, q + 1)
                sp.dma_start(out[0].rearrange("(t p) n -> p t n", p=P)[:, :, 512 * q:512 * q + 512],
                             X[:, :, 512 * q:512 * q + 512]).then_inc(out_stored, 16)
            sp.wait_ge(out_stored, 64)

        def landed(b, j):
            if isinstance(b, int) and b <= B_WIN + 1:
                return 16 * (b + 1)
            return 16 * (b + 2)

        @block.gpsimd
        def _(pool):
            def causal(t):
                pool.memset(t[:, :], 0.0).then_inc(pool_order, 1)

            def causal_select(t):
                for c in (0, 2 * P):
                    last = pool.affine_select(out=t[:, c:c + P], in_=t[:, c:c + P], compare_op=ALU.is_ge,
                                              fill=NEG, base=0, pattern=[[-1, P]], channel_multiplier=1)
                return last

            pool.memset(ident[:, :], 0.0).then_inc(pool_order, 1)
            causal(FMm)
            pool.memset(U[:, :, 0:TAPS - 1], 0.0).then_inc(pool_order, 1)
            pool.memset(Um[:, :], 1.0).then_inc(pool_order, 1)
            pool.memset(Vm[:, :], 1.0).then_inc(pool_order, 1)
            pool.wait_ge(pool_order, 5)
            pool.affine_select(out=ident[:, :], in_=ident[:, :], compare_op=ALU.not_equal, fill=1.0, base=0,
                               pattern=[[-1, P]], channel_multiplier=1).then_inc(consts_ready, 1)
            causal_select(FMm).then_inc(consts_ready, 1)
            pool.affine_select(out=Um[:, :], in_=Um[:, :], compare_op=ALU.is_ge, fill=0.0, base=0,
                               pattern=[[1, P]], channel_multiplier=-1)
            pool.affine_select(out=Vm[:, :], in_=Vm[:, :], compare_op=ALU.is_gt, fill=0.0, base=0,
                               pattern=[[-1, P]], channel_multiplier=1).then_inc(consts_ready, 1)
            pool.dma_start(PR[0:48, :], conv_w[0].rearrange("j (i p) -> (j i) p", p=P)).then_inc(vec_landed, 16)
            pool.dma_start(PR[48:60, :], conv_b[0].rearrange("(i p) -> i p", p=P)).then_inc(vec_landed, 16)
            pool.dma_start(PR[60:61, :], g_q[0:1]).then_inc(vec_landed, 16)
            pool.dma_start(PR[61:62, :], g_k[0:1]).then_inc(vec_landed, 16)
            for c, n, v in ((0, 16, dt_bias), (16, 16, a_log), (32, 16, d_skip), (48, 64, g_kidx)):
                pool.dma_start(VB[:, c:c + n], v[0].unsqueeze(0).broadcast_to([P, n])).then_inc(vec_landed, 16)
            wait_full(pool, ("diag", 1, 1))
            pool.dma_start(GS[:, :], g_ssd[0].unsqueeze(0).broadcast_to([P, SSD_W])).then_inc(gs_landed, 16)
            pool.wait_ge(chunk_used, 4 * B_FOX)
            causal(FMf)
            pool.memset(Uf[:, :], 1.0).then_inc(pool_order, 1)
            pool.memset(ONE[:, :], 1.0).then_inc(pool_order, 1)
            pool.memset(OH[:, :], 0.0).then_inc(pool_order, 1)
            pool.wait_ge(pool_order, 9)
            causal_select(FMf)
            for k in range(3):
                pool.affine_select(out=OH[:, :], in_=OH[:, :], compare_op=ALU.not_equal, fill=1.0,
                                   base=-HEADS_F * k, pattern=[[-1, HEADS_F]], channel_multiplier=1)\
                    .then_inc(pool_order, 1)
                pool.wait_ge(pool_order, 10 + k)
            pool.affine_select(out=Uf[:, :], in_=Uf[:, :], compare_op=ALU.is_ge, fill=0.0, base=0,
                               pattern=[[1, P]], channel_multiplier=-1).then_inc(consts_ready, 1)
            pool.dma_start(FB[:, :], fox_b_f[0].unsqueeze(0).broadcast_to([P, HEADS_F])).then_inc(fb_landed, 16)
            pool.wait_ge(fb_landed, 16)

        @block.scalar
        def _(act):
            order = [0]

            def after(ins):
                order[0] += 1
                ins.then_inc(act_order, 1)
                act.wait_ge(act_order, order[0])

            def hi(b, j, width=512):
                act.wait_ge(raw_landed[j], landed(b, j))
                if not (isinstance(b, int) and b == 0 and j < 2):
                    act.wait_ge(chunk_used, 4 * b + j - 1)
                act.activation(wh[:, j % 2, :, 0:width], raw[:, j, :, 0:width], ACT.Copy).then_inc(hi_ready, 1)

            def std(name_in, n_in, name_out, dst, src):
                act.wait_ge(name_in, n_in)
                act.activation(dst, src, ACT.Sqrt).then_inc(name_out, 1)

            def take_xt(m, n, dst_h=XH):
                wait_full(act, ("xt", m, n))
                act.activation(dst_h[:, 2 * n:2 * n + 2, :].rearrange("p k t -> p (k t)"),
                               side_bank(("xt", m, n))[:, :], ACT.Copy).then_inc(xh_ready, 1)

            def norm(m, b, n_root):
                std(var_ready, n_root, std_ready, rstd[:, :], rstd[:, :])
                hi(b, 1)
                for n in range(8):
                    take_xt(m, n)

            def squares(q, src, n_sum):
                act.wait_ge(sum_ready, n_sum)
                act.wait_ge(ssq_ready, n_sum)
                after(act.activation(junk[:, :], src[:, 0, 512 * q:512 * q + 512], ACT.Square,
                                     accum_out=ssq[:, 0, q:q + 1]))
                act.activation(junk[:, :], src[:, 1, 512 * q:512 * q + 512], ACT.Square,
                               accum_out=ssq[:, 1, q:q + 1]).then_inc(ssq_ready, 1)

            def attn_exp(a, h, L, st):
                act.wait_ge(step["logits_ready"], a * HEADS_A + h + 1)
                s0 = 4 * (h % 4)
                for t in range(NT):
                    ins = act.activation(L[:, h % L.shape[1], ctr(t)], L[:, h % L.shape[1], ctr(t)], ACT.Exp,
                                         bias=st[:, s0 + t:s0 + t + 1], accum_out=st[:, s0 + 2 + t:s0 + 3 + t])
                ins.then_inc(step["exp_ready"], 1)

            def attn_pt(a, h, PT):
                wait_full(act, ("PT", a, h))
                free(act.activation(PT[:, h, :], side_bank(("PT", a, h))[:, 0:3 * P], ACT.Copy), ("PT", a, h))

            def take(kind, o, n, b):
                act.wait_ge(chunk_used, 4 * b + 4)
                if kind == "k":
                    act.wait_ge(step["conv_done"], 12)
                elif kind == "z" and n == 0:
                    wait_full(act, ("qkt", 5))
                src = acc[o % 2][1]
                if kind == "qi":
                    dst = QI[:, 4 * n + 2:4 * n + 4, :].rearrange("p f t -> p (f t)")
                elif kind == "xbc":
                    dst, src = U[:, 4 * n + 2:4 * n + 4, TAPS - 1:], src[:, :].rearrange("p (f t) -> p f t", f=2)
                elif kind == "small":
                    dst, src = SM[:, 1, :], src[:, 0:W_SMALL]
                elif kind in ("k", "v"):
                    dst = {"k": K, "v": V}[kind][:, 1, :]
                elif kind in ("q", "z"):
                    dst = {"q": Q, "z": Z}[kind][:, 1, 512 * n:512 * n + 512]
                elif kind in ("fq", "fk"):
                    dst = {"fq": FQ, "fk": FK}[kind][:, 4 * n + 2:4 * n + 4, :].rearrange("p f t -> p (f t)")
                elif kind == "fv":
                    dst = FV[:, 1, 512 * n:512 * n + 512]
                else:
                    dst, src = FS[:, 0, HEADS_F:2 * HEADS_F], src[:, 0:HEADS_F]
                act.activation(dst, src if kind in ("xbc", "small", "fs") else src[:, :], ACT.Copy,
                               scale=SCALE if kind == "fq" else 1.0).then_inc(acc_freed[o % 2][1], 1)

            def mlp(b0, o0, u0, q0, src):
                def relu(u, o_par, k, b):
                    if k == 0:
                        act.wait_ge(chunk_used, 4 * b + 4)
                    act.wait_ge(hl_ready, 2 * u + k + 1)
                    act.activation(RB[:, k, :], acc[o_par][k][:, :], ACT.Relu)\
                       .then_inc(acc_freed[o_par][k], 1)

                def high(u, k, tile):
                    act.wait_ge(sq_ready, 2 * u + k + 1)
                    act.activation(hh[:, tile, :], RB[:, k, :].rearrange("p (f t) -> p f t", f=2), ACT.Copy)\
                       .then_inc(hh_ready, 1)

                def hidden(j, u, o_par, b, tile0):
                    if j < 2:
                        relu(u, o_par, j, b)
                    if j in (1, 2):
                        k = j - 1
                        at = tile0 + 2 * k
                        high(u, k, slice(at, at + 2) if isinstance(at, int) else bass.ds(at, 2))

                for half in range(2):
                    b, o, u = b0 + half * B_HALF, o0 + half * O_HALF, u0 + half * UP
                    for j in range(2, 4):
                        hi(b, j)
                    with act.Fori(0, UP // 2 - 1) as i:
                        for s in (1, 2):
                            for j in range(4):
                                hi(b + 2 * i + s, j)
                                hidden(j, u + 2 * i + s - 1, (o + s - 1) % 2, b + 2 * i + s - 1,
                                       4 * (2 * i + s - 1))
                    for j in range(4):
                        hi(b + UP - 1, j)
                        hidden(j, u + UP - 2, (o + UP - 2) % 2, b + UP - 2, 4 * (UP - 2))
                    for n in range(DOWN):
                        for j in range(8):
                            hi(b + UP + 2 * n + j // 4, j % 4)
                            if n == 0 and j < 3:
                                hidden(j, u + UP - 1, (o + UP - 1) % 2, b + UP - 1, 4 * (UP - 1))
                            if half == 1 and n > 0 and j == 3:
                                squares(n - 1, src, q0 + n)
                    last = b + UP + 2 * DOWN
                    if half == 0:
                        hi(last, 0)
                        hi(last, 1)

            for t in range(NT):
                act.dma_start(X[:, t, :], x[0, t * P:(t + 1) * P, :]).then_inc(x_landed[t], 16)
            act.dma_start(G[:, :], g_mix[0].unsqueeze(0).broadcast_to([P, D])).then_inc(g_landed, 16)
            hi(0, 0)
            for t in range(NT):
                act.wait_ge(x_landed[t], 16)
                for q in range(4):
                    after(act.activation(junk[:, :], X[:, t, 512 * q:512 * q + 512], ACT.Square,
                                         accum_out=ssq[:, t, q:q + 1]))
            act.nop().then_inc(ssq_ready, 1)
            norm(0, 0, 1)

            def dt_logs(T, asked, told, n0):
                act.wait_ge(asked, 1)
                act.activation(T[:, 2, :], T[:, 1, :], ACT.Exp).then_inc(told, 1)
                act.wait_ge(asked, 2)
                act.activation(T[:, 4, :], T[:, 3, :], ACT.Ln).then_inc(told, 1)

            def conv_start(i):
                wait_emptied(act, "params")
                o = O_WIN + 3 + i // 4
                for t in range(NT):
                    act.wait_ge(acc_freed[o % 2][t], o // 2 + 1)
                act.wait_ge(consts_ready, 2)
                act.activation(XC[:, i, :], U[:, i, 0:TOK], ACT.Identity, scale=PC[:, i:i + 1],
                               bias=PC[:, 48 + i:49 + i]).then_inc(step["conv_start"], 1)

            def silu(n):
                act.wait_ge(step["conv_done"], 4 * n + 4)
                act.activation(XC[:, 4 * n:4 * n + 4, :], XC[:, 4 * n:4 * n + 4, :], ACT.Silu)\
                   .then_inc(step["silu_done"], 1)

            def decay(c, n):
                wait_full(act, ("seg", c, n))
                free(act.activation(E[:, 4 * n:4 * n + 4, :].rearrange("p h l -> p (h l)"),
                                    side_bank(("seg", c, n))[:, :], ACT.Exp), ("seg", c, n))

            def turned(n):
                wait_full(act, ("qkt", n))
                dst = QT[:, 2 * n:2 * n + 2, :] if n < 4 else KTt[:, 2 * n - 8:2 * n - 6, :]
                free(act.activation(dst.rearrange("p h t -> p (h t)"), side_bank(("qkt", n))[:, :], ACT.Copy,
                                    scale=PC[:, 60:61] if n < 4 else PC[:, 61:62]), ("qkt", n))

            def gate(g):
                for t in range(NT):
                    o = O_WIN + 9 + g
                    act.wait_ge(acc_freed[o % 2][t], o // 2 + 1)
                    act.activation(Z[:, t, 512 * g:512 * g + 512], Z[:, t, 512 * g:512 * g + 512], ACT.Silu)\
                       .then_inc(step["z_gated"], 1)

            def gated_squares(g):
                act.wait_ge(step["y_ready"], g + 1)
                for t in range(NT):
                    act.activation(junk[:, :], Y[:, t, 512 * g:512 * g + 512], ACT.Square,
                                   accum_out=SQS[:, 56 + 2 * t + g:57 + 2 * t + g]).then_inc(step["yss_ready"], 1)
                    act.wait_ge(step["yss_ready"], 2 * g + t + 1)

            def mix_side(n):
                if n == 6:
                    wait_full(act, "params")
                    free(act.activation(PC[:, :], side_bank("params")[:, 0:62], ACT.Copy), "params")
                if n == 13:
                    std(step["ki_var"], 1, step["ki_std"], SQS[:, 2:4], SQS[:, 0:2])
                if n == 14:
                    act.activation(DTS[:, 8, 0:16], VB[:, 16:32], ACT.Exp).then_inc(step["dt_b"], 1)
                    dt_logs(DTS, step["dt_a"], step["dt_b"], 1)
                if n == 15:
                    wait_full(act, "ki")
                    free(act.activation(KIT[:, :], side_bank("ki")[:, 0:TOK], ACT.Copy), "ki")
                if 17 <= n <= 22:
                    for g in (2 * n - 34, 2 * n - 33):
                        wait_full(act, ("score", g))
                        if g >= 2:
                            act.wait_ge(step["scores_used"], g - 1)
                        free(act.activation(R[:, g % 2, :], side_bank(("score", g))[:, :], ACT.Relu), ("score", g))
                        if g == 1:
                            for c in range(NT):
                                wait_full(act, ("cum", c))
                                free(act.activation(DTS[:, 9 if c else 8, :], side_bank(("cum", c))[:, 0:32],
                                                    ACT.Exp), ("cum", c))
                if 17 <= n <= 27:
                    conv_start(n - 17)
                if n == 27:
                    conv_start(11)
                if n in (23, 24):
                    decay(0, 2 * n - 46)
                    decay(0, 2 * n - 45)
                if n in (25, 26, 29):
                    silu({25: 0, 26: 1, 29: 2}[n])
                if n == 33:
                    wait_full(act, ("xst", 4))
                    free(act.activation(BM[:, :, :].rearrange("p t n -> p (t n)"), side_bank(("xst", 4))[:, :],
                                        ACT.Copy), ("xst", 4))
                if n == 37:
                    std(step["qk_var"], 1, step["qk_std"], SQS[:, 32:56], SQS[:, 8:32])
                if n == 38:
                    for g in range(GROUPS):
                        wait_full(act, ("state", g))
                        free(act.activation(ST[:, g, :], side_bank(("state", g))[:, :], ACT.Copy), ("state", g))
                if n in (38, 39):
                    decay(1, 2 * n - 76)
                    decay(1, 2 * n - 75)
                if n in (40, 41):
                    for k in range(3 * (n - 40), 3 * (n - 40) + 3):
                        turned(k)
                if n == 41:
                    gate(0)
                for h in {43: (0,), 44: (1,), 45: (2, 3), 46: (4, 5), 47: (6, 7)}.get(n, ()):
                    attn_exp(0, h, Lm, SQS[:, 64:80])
                for h in {45: (0,), 46: (1,), 47: (2, 3)}.get(n, ()):
                    attn_pt(0, h, PTm)
                if n == 45:
                    gate(1)
                if n == 46:
                    gated_squares(0)

            def fox_side(n):
                if n == 13:
                    dt_logs(FS, step["f_a"], step["f_b"], 0)
                if n == 19:
                    wait_full(act, "fct")
                    free(act.activation(NCT[:, :], side_bank("fct")[0:3 * HEADS_F, 0:TOK], ACT.Copy), "fct")
                if n >= 21 and n % 2 == 1:
                    attn_exp(1, (n - 21) // 2, Lf, FST)
                if n >= 23 and n % 2 == 1:
                    attn_pt(1, (n - 23) // 2, PTf)
                for h in range(12):
                    if n == FOX_O[h] + 2:
                        fox_out(h)

            def fox_out(h):
                wait_full(act, ("O", 1, h))
                free(act.activation(FQ[:, h, :], side_bank(("O", 1, h))[:, 0:TOK], ACT.Copy), ("O", 1, h))

            def fox_high(n):
                for h in (2 * n, 2 * n + 1):
                    wait_emptied(act, ("O", 1, h))
                act.activation(XH[:, 2 * n:2 * n + 2, :], FQ[:, 2 * n:2 * n + 2, :], ACT.Copy).then_inc(xh_ready, 1)

            seen = {}
            prev = None
            for n, (kind, col, width) in enumerate(WIN):
                for j in range(4):
                    if n or j >= 2:
                        hi(B_WIN + n, j, width)
                    if prev and j == (1 if prev[0] == "z" else 0):
                        take(*prev)
                    mix_side(4 * n + j)
                prev = (kind, O_WIN + n, seen.get(kind, 0), B_WIN + n)
                seen[kind] = seen.get(kind, 0) + 1
            hi(B_WOUT, 0)
            for h in (4, 5):
                attn_pt(0, h, PTm)
            take(*prev)
            gated_squares(1)
            std(step["y_var"], 1, step["y_std"], SQS[:, 60:64], SQS[:, 60:64])

            def y_high(n):
                wait_full(act, ("yt", n))
                act.activation(XH[:, 2 * n:2 * n + 2, :].rearrange("p k t -> p (k t)"),
                               side_bank(("yt", n))[:, :], ACT.Copy).then_inc(xh_ready, 1)

            def o_high(h):
                wait_full(act, ("O", 0, h))
                act.activation(XH[:, 8 + h, :], side_bank(("O", 0, h))[:, 0:TOK], ACT.Copy)\
                   .then_inc(step["oh_ready"], 1)

            y_high(0)
            y_high(1)
            hi(B_WOUT, 1)
            for h in (6, 7):
                attn_pt(0, h, PTm)
            y_high(2)
            y_high(3)
            for n in range(DOWN):
                for j in range(4):
                    if n or j >= 2:
                        hi(B_WOUT + n, j)
                    if n == 0 and j >= 2:
                        for h in range(4 * j - 8, 4 * j - 4):
                            o_high(h)
                    if n and j == 2:
                        squares(n - 1, X, n)
            hi(B_M1, 0)
            squares(3, X, 4)
            norm(1, B_M1, 2)
            mlp(B_M1, O_M1, 0, 4, X)
            hi(B_FOX, 0)
            squares(3, X, 8)
            norm(2, B_FOX, 3)
            seen = {}
            prev = None
            for n, (kind, col, width) in enumerate(FOX):
                for j in range(4):
                    if n or j >= 2:
                        hi(B_FOX + n, j, width)
                    if j == 0 and prev:
                        take(*prev)
                    fox_side(4 * n + j)
                prev = (kind, O_FOX + n, seen.get(kind, 0), B_FOX + n)
                seen[kind] = seen.get(kind, 0) + 1
            hi(B_FOUT, 0)
            take(*prev)
            attn_pt(1, 15, PTf)
            for h in (9, 10, 11):
                fox_out(h)
            fox_high(0)
            fox_high(1)
            hi(B_FOUT, 1)
            for n in range(2, 6):
                fox_high(n)
            for n in range(DOWN):
                for j in range(4):
                    if n or j >= 2:
                        hi(B_FOUT + n, j)
                    if n == 0 and j >= 2:
                        for h in (2 * j + 8, 2 * j + 9):
                            fox_out(h)
                        fox_high(j + 4)
                    if n and j == 2:
                        squares(n - 1, HB, 8 + n)
            hi(B_M2, 0)
            squares(3, HB, 12)
            std(var_ready, 4, std_ready, rstd[:, :], rstd[:, :])
            for q in range(4):
                squares(q, X, 13 + q)
            norm(3, B_M2, 5)
            mlp(B_M2, O_M2, 2 * UP, 16, HB)
            squares(3, HB, 20)
            std(var_ready, 6, std_ready, rstd[:, :], rstd[:, :])

        @block.vector
        def _(dve):
            order = [0]

            def after(ins):
                order[0] += 1
                ins.then_inc(dve_order, 1)
                dve.wait_ge(dve_order, order[0])

            def lo(b, j, width=512):
                dve.wait_ge(hi_ready, 4 * b + j + 1)
                dve.tensor_tensor(wl[:, j % 2, :, 0:width], raw[:, j, :, 0:width],
                                  wh[:, j % 2, :, 0:width].bitcast(F32), ALU.subtract).then_inc(lo_ready, 1)

            def low_xt(name, n, sem_n):
                dve.wait_ge(xh_ready, sem_n)
                bk = side_bank(name)[:, :]
                dst = slice(2 * n, 2 * n + 2)
                ins = dve.tensor_tensor(XL[:, dst, :].rearrange("p k t -> p (k t)"), bk,
                                        XH[:, dst, :].bitcast(F32).rearrange("p k t -> p (k t)"), ALU.subtract)
                free(ins, name)

            def root(n_ssq, n_root):
                dve.wait_ge(ssq_ready, n_ssq)
                after(dve.tensor_reduce(rstd[:, :], ssq[:, :, :], AX, ALU.add))
                dve.tensor_scalar(rstd[:, :], rstd[:, :], 1.0 / D, EPS, ALU.mult, ALU.add).then_inc(var_ready, 1)
                dve.wait_ge(std_ready, n_root)
                after(dve.reciprocal(rstd[:, :], rstd[:, :]))

            def norm(m, n_ssq, n_root, n_g, n_xh, b):
                root(n_ssq, n_root)
                dve.wait_ge(g_landed, 16 * n_g)

                def quarter(q):
                    cols = slice(512 * q, 512 * q + 512)
                    for t in range(NT):
                        ins = dve.scalar_tensor_tensor(out=(XN1 if m else XN0)[:, t, cols], in0=X[:, t, cols],
                                                       scalar=rstd[:, t:t + 1], in1=G[:, cols],
                                                       op0=ALU.mult, op1=ALU.mult)
                        if q == 3 and t == 1:
                            ins.then_inc(g_used, 1)
                        else:
                            ins.then_inc(xn_ready, 1)
                quarter(0)
                quarter(1)
                lo(b, 1)
                for n in range(4):
                    low_xt(("xt", m, n), n, n_xh + n + 1)
                quarter(2)
                low_xt(("xt", m, 4), 4, n_xh + 5)
                quarter(3)
                for n in range(5, 8):
                    low_xt(("xt", m, n), n, n_xh + n + 1)

            def log1p_exp(T, ready, done, n0):
                dve.wait_ge(done, n0 + 1)
                dve.tensor_scalar(T[:, 3, :], T[:, 2, :], 1.0, None, ALU.add).then_inc(ready, 1)
                dve.wait_ge(ready, 2)
                after(dve.tensor_scalar(T[:, 5, :], T[:, 3, :], -1.0, None, ALU.add))
                after(dve.tensor_scalar(T[:, 6, :], T[:, 5, :], 0.0, None, ALU.is_equal))
                after(dve.tensor_tensor(T[:, 5, :], T[:, 5, :], T[:, 6, :], ALU.add))
                after(dve.reciprocal(T[:, 5, :], T[:, 5, :]))
                after(dve.tensor_tensor(T[:, 5, :], T[:, 5, :], T[:, 2, :], ALU.mult))
                dve.wait_ge(done, n0 + 2)
                after(dve.tensor_tensor(T[:, 5, :], T[:, 5, :], T[:, 4, :], ALU.mult))
                after(dve.tensor_tensor(T[:, 6, :], T[:, 6, :], T[:, 2, :], ALU.mult))
                after(dve.tensor_tensor(T[:, 6, :], T[:, 6, :], T[:, 5, :], ALU.add))

            def add_panel(o, b, q, dst, first):
                dve.wait_ge(chunk_used, 4 * b + 4)
                cols = slice(512 * q, 512 * q + 512)
                for t in range(NT):
                    if first:
                        ins = dve.tensor_copy(dst[:, t, cols], acc[o % 2][t][:, :])
                    else:
                        ins = dve.tensor_tensor(dst[:, t, cols], acc[o % 2][t][:, :], dst[:, t, cols], ALU.add)
                    ins.then_inc(acc_freed[o % 2][t], 1)

            def take(kind, o, n, b):
                dve.wait_ge(chunk_used, 4 * b + 4)
                if kind == "z" and n == 0:
                    wait_full(dve, ("qkt", 5))
                src = acc[o % 2][0]
                if kind == "qi":
                    dst = QI[:, 4 * n:4 * n + 2, :].rearrange("p f t -> p (f t)")
                elif kind == "xbc":
                    dst = U[:, 4 * n:4 * n + 2, TAPS - 1:]
                elif kind == "small":
                    dst = SM[:, 0, :]
                elif kind in ("k", "v"):
                    dst = {"k": K, "v": V}[kind][:, 0, :]
                elif kind in ("q", "z"):
                    dst = {"q": Q, "z": Z}[kind][:, 0, 512 * n:512 * n + 512]
                elif kind in ("fq", "fk"):
                    dst = {"fq": FQ, "fk": FK}[kind][:, 4 * n:4 * n + 2, :].rearrange("p f t -> p (f t)")
                elif kind == "fv":
                    dst = FV[:, 0, 512 * n:512 * n + 512]
                else:
                    dst = FS[:, 0, 0:HEADS_F]
                if kind == "xbc":
                    ins = dve.tensor_copy(dst, src[:, :].rearrange("p (f t) -> p f t", f=2))
                elif kind == "fq":
                    ins = dve.tensor_scalar(dst, src[:, :], SCALE, None, ALU.mult)
                else:
                    ins = dve.tensor_copy(dst, src[:, 0:dst.shape[1]])
                ins.then_inc(acc_freed[o % 2][0], 1)

            def attn_logits(a, h, L, M, st):
                if h >= L.shape[1]:
                    wait_full(dve, ("PT", a, h - L.shape[1]))
                wait_full(dve, ("S", a, h))
                bk, s0 = side_bank(("S", a, h)), 4 * (h % 4)
                for t in range(NT):
                    ins = dve.tensor_tensor_reduce(L[:, h % L.shape[1], ctr(t)], bk[:, ctr(t)], M[:, ctr(t)], 1.0, -3e38,
                                                   ALU.add, ALU.max, st[:, s0 + t:s0 + t + 1])
                free(ins, ("S", a, h))
                dve.wait_ge(side_free[uses[("S", a, h)][0]], uses[("S", a, h)][1] + 1)
                dve.tensor_scalar(st[:, s0:s0 + 2], st[:, s0:s0 + 2], -1.0, None, ALU.mult)\
                   .then_inc(step["logits_ready"], 1)

            def attn_probs(a, h, L, st):
                s0 = 4 * (h % 4)
                dve.wait_ge(step["exp_ready"], a * HEADS_A + h + 1)
                after(dve.reciprocal(st[:, s0 + 2:s0 + 4], st[:, s0 + 2:s0 + 4]))
                for t in range(NT):
                    ins = dve.tensor_scalar(L[:, h % L.shape[1], ctr(t)], L[:, h % L.shape[1], ctr(t)],
                                            st[:, s0 + 2 + t:s0 + 3 + t], None, ALU.mult)
                ins.then_inc(step["probs_ready"], 1)

            def attn_low(h):
                dve.wait_ge(step["oh_ready"], h + 1)
                ins = dve.tensor_tensor(XL[:, 8 + h, :], side_bank(("O", 0, h))[:, 0:TOK],
                                        XH[:, 8 + h, :].bitcast(F32), ALU.subtract)
                free(ins, ("O", 0, h))

            def mlp(b0, o0, u0, dst, fresh):
                def square(o_par, n, k):
                    dve.wait_ge(acc_freed[o_par][k], n)
                    dve.tensor_tensor(RB[:, k, :], RB[:, k, :], RB[:, k, :], ALU.mult).then_inc(sq_ready, 1)

                def low(u, k, tile):
                    dve.wait_ge(hh_ready, 2 * u + k + 1)
                    dve.tensor_tensor(hl[:, tile, :], RB[:, k, :].rearrange("p (f t) -> p f t", f=2),
                                      hh[:, tile, :].bitcast(F32), ALU.subtract).then_inc(hl_ready, 1)

                def hidden(j, u, o_par, n, tile0):
                    if j < 2:
                        square(o_par, n, j)
                    if j in (2, 3):
                        k = j - 2
                        at = tile0 + 2 * k
                        low(u, k, slice(at, at + 2) if isinstance(at, int) else bass.ds(at, 2))

                for half in range(2):
                    b, o, u = b0 + half * B_HALF, o0 + half * O_HALF, u0 + half * UP
                    for j in range(2, 4):
                        lo(b, j)
                    with dve.Fori(0, UP // 2 - 1) as i:
                        for s in (1, 2):
                            for j in range(4):
                                lo(b + 2 * i + s, j)
                                hidden(j, u + 2 * i + s - 1, (o + s - 1) % 2, i + (o + s - 1) // 2 + 1,
                                       4 * (2 * i + s - 1))
                    for j in range(4):
                        lo(b + UP - 1, j)
                        hidden(j, u + UP - 2, (o + UP - 2) % 2, (o + UP - 2) // 2 + 1, 4 * (UP - 2))
                    for n in range(DOWN):
                        for j in range(8):
                            lo(b + UP + 2 * n + j // 4, j % 4)
                            if n == 0 and j < 4:
                                hidden(j, u + UP - 1, (o + UP - 1) % 2, (o + UP - 1) // 2 + 1,
                                       4 * (UP - 1))
                            if n > 0 and j == 1:
                                add_panel(o + UP + n - 1, b + UP + 2 * n - 1, n - 1, dst, fresh and half == 0)
                                if half == 1:
                                    summed(o + UP + n - 1)
                    last = b + UP + 2 * DOWN
                    if half == 0:
                        lo(last, 0)
                        lo(last, 1)
                        add_panel(o + UP + DOWN - 1, last - 1, DOWN - 1, dst, fresh)

            def summed(o):
                for t in range(NT):
                    dve.wait_ge(acc_freed[o % 2][t], o // 2 + 1)
                dve.engine_nop().then_inc(sum_ready, 1)

            def index_keys():
                for o in (O_WIN + 2,):
                    for t in range(NT):
                        dve.wait_ge(acc_freed[o % 2][t], o // 2 + 1)
                dve.wait_ge(vec_landed, 16 * 8)
                for t in range(NT):
                    after(dve.tensor_tensor_reduce(KI2[:, t, 0:HD_I], SM[:, t, 0:HD_I], SM[:, t, 0:HD_I], 1.0, 0.0,
                                                   ALU.mult, ALU.add, SQS[:, t:t + 1]))
                dve.tensor_scalar(SQS[:, 0:2], SQS[:, 0:2], 1.0 / HD_I, EPS, ALU.mult, ALU.add)\
                   .then_inc(step["ki_var"], 1)
                w_i = SM[:, :, HD_I:W_KW]
                after(dve.tensor_scalar(w_i, w_i, HEADS_I ** -0.5 * HD_I ** -0.5, None, ALU.mult))
                dve.wait_ge(step["ki_std"], 1)
                after(dve.reciprocal(SQS[:, 2:4], SQS[:, 2:4]))
                for t in range(NT):
                    for k in range(2):
                        dve.scalar_tensor_tensor(out=KI2[:, t, HD_I * k:HD_I * (k + 1)], in0=SM[:, t, 0:HD_I],
                                                 scalar=SQS[:, 2 + t:3 + t], in1=VB[:, 48:48 + HD_I],
                                                 op0=ALU.mult, op1=ALU.mult).then_inc(step["ki_rows"], 1)

            def step_sizes():
                T = DTS
                v = T[:, 0, :].rearrange("p (t h) -> p t h", t=NT)
                after(dve.tensor_tensor(v, SM[:, :, W_KW:], VB[:, 0:16].unsqueeze(1).broadcast_to([P, NT, HEADS_S]),
                                        ALU.add))
                dve.scalar_tensor_tensor(out=T[:, 1, :], in0=T[:, 0, :], scalar=-1.0, in1=T[:, 0, :],
                                         op0=ALU.mult, op1=ALU.min).then_inc(step["dt_a"], 1)
                log1p_exp(T, step["dt_a"], step["dt_b"], 1)
                after(dve.scalar_tensor_tensor(out=T[:, 6, :], in0=T[:, 0, :], scalar=0.0, in1=T[:, 6, :],
                                               op0=ALU.max, op1=ALU.add))
                dve.scalar_tensor_tensor(out=T[:, 7, :].rearrange("p (t h) -> p t h", t=NT),
                                         in0=T[:, 6, :].rearrange("p (t h) -> p t h", t=NT), scalar=-1.0,
                                         in1=T[:, 8, 0:16].unsqueeze(1).broadcast_to([P, NT, HEADS_S]),
                                         op0=ALU.mult, op1=ALU.mult).then_inc(step["adt_ready"], 1)

            def score_add(g):
                t, per, hs = score_heads(g)
                wait_emptied(dve, ("score", g))
                for i in range(per):
                    h, width = hs[i], P * (t + 1)
                    src, w = R[:, g % 2, width * i:width * (i + 1)], SM[:, t, HD_I + h:HD_I + h + 1]
                    if h == 0:
                        ins = dve.tensor_scalar(SC[:, ctr(t)], src, w, None, ALU.mult)
                    else:
                        ins = dve.scalar_tensor_tensor(out=SC[:, ctr(t)], in0=src, scalar=w, in1=SC[:, ctr(t)],
                                                       op0=ALU.mult, op1=ALU.add)
                    if i < per - 1:
                        after(ins)
                ins.then_inc(step["scores_used"], 1)
                dve.wait_ge(step["scores_used"], g + 1)

            def top(t, r0, r1):
                width = P * (t + 1)
                s = SC[:, ctr(t)]
                if r0 == 0:
                    dve.wait_ge(consts_ready, 2)
                    after(dve.tensor_tensor(s, s, FMm[:, ctr(t)], ALU.add))
                for r in range(r0, r1):
                    after(dve.max(M8[:, :], s if r == 0 else WK[:, 0:width]))
                    if r < TOPK // 8 - 1:
                        after(dve.match_replace(WK[:, 0:width], M8[:, :], s if r == 0 else WK[:, 0:width], -3e38))

            def select(t):
                width = P * (t + 1)
                s = SC[:, ctr(t)]
                kth = M8[:, 7:8]
                after(dve.tensor_scalar(GT[:, 0:width], s, kth, None, ALU.is_gt, ALU.add, accum_out=SQS[:, 4:5]))
                after(dve.tensor_scalar(EQ[:, 0:width], s, kth, None, ALU.is_equal))
                after(dve.tensor_scalar(SQS[:, 4:5], SQS[:, 4:5], -1.0, float(TOPK), ALU.mult, ALU.add))
                after(dve.tensor_tensor_scan(CS[:, 0:width], EQ[:, 0:width], EQ[:, 0:width], 0.0,
                                             ALU.add, ALU.max))
                after(dve.scalar_tensor_tensor(out=EQ[:, 0:width], in0=CS[:, 0:width], scalar=SQS[:, 4:5],
                                               in1=EQ[:, 0:width], op0=ALU.is_le, op1=ALU.mult))
                after(dve.tensor_tensor(GT[:, 0:width], GT[:, 0:width], EQ[:, 0:width], ALU.add))
                after(dve.tensor_scalar(GT[:, 0:width], GT[:, 0:width], -1.0, -NEG, ALU.add, ALU.mult))
                after(dve.tensor_tensor(MK[:, ctr(t)], GT[:, 0:width], FMm[:, ctr(t)], ALU.add))

            def head_squares(src, half, at, o):
                for t in range(NT):
                    dve.wait_ge(acc_freed[o % 2][t], o // 2 + 1)
                    sq = QI[:, 2 * t:2 * t + 2, :].rearrange("p h t -> p (h t)")
                    v = src[:, t, 512 * half:512 * half + 512]
                    after(dve.tensor_tensor(sq, v, v, ALU.mult))
                    after(dve.tensor_reduce(SQS[:, at + 4 * t:at + 4 * t + 4], heads(sq, HD), AX, ALU.add))

            def qk_norm():
                dve.wait_ge(step["qk_std"], 1)
                after(dve.reciprocal(SQS[:, 32:56], SQS[:, 32:56]))
                after(dve.tensor_scalar(SQS[:, 32:48], SQS[:, 32:48], SCALE, None, ALU.mult))
                for src, half, at in ((Q, 0, 32), (Q, 1, 40), (K, 0, 48)):
                    for t in range(NT):
                        v = heads(src[:, t, 512 * half:512 * half + 512], HD)
                        dve.tensor_tensor(v, v, bc(SQS[:, at + 4 * t:at + 4 * t + 4], HD), ALU.mult)\
                           .then_inc(step["qk_normed"], 1)

            def conv_rest(i):
                dve.wait_ge(step["conv_start"], i + 1)
                for j in range(1, TAPS):
                    ins = dve.scalar_tensor_tensor(out=XC[:, i, :], in0=U[:, i, j:j + TOK],
                                                   scalar=PC[:, 12 * j + i:12 * j + i + 1], in1=XC[:, i, :],
                                                   op0=ALU.mult, op1=ALU.add)
                    if j < TAPS - 1:
                        after(ins)
                ins.then_inc(step["conv_done"], 1)

            def decay_in(c):
                if c:
                    wait_full(dve, ("diag", 0, 1))
                else:
                    dve.wait_ge(step["adt_ready"], 1)
                    dve.wait_ge(consts_ready, 3)
                dve.tensor_tensor(E[:, :, :], Um[:, :].unsqueeze(1).broadcast_to([P, HEADS_S, P]),
                                  bc(DTS[:, 7, 16 * c:16 * c + 16], P), ALU.mult).then_inc(step["decay_in"], 1)

            def inputs(c):
                for half in range(2):
                    wait_full(dve, ("xst", 2 * c + half))
                    src = heads(side_bank(("xst", 2 * c + half))[:, :], HD_S)
                    cols, h0 = slice(512 * half, 512 * half + 512), HPG * half
                    dve.tensor_tensor(heads(Y[:, c, cols], HD_S), src, bc(VB[:, 32 + h0:32 + h0 + HPG], HD_S),
                                      ALU.mult).then_inc(step["skip_ready"], 1)
                    free(dve.tensor_tensor(heads(XD[:, c, cols], HD_S), src,
                                           bc(DTS[:, 6, 16 * c + h0:16 * c + h0 + HPG], HD_S), ALU.mult),
                         ("xst", 2 * c + half))

            def maps():
                wait_full(dve, "cb")
                free(dve.tensor_tensor(CB[:, :, :], side_bank("cb")[:, :].rearrange("p (g l) -> p g l", l=P),
                                       Um[:, :].unsqueeze(1).broadcast_to([P, NT * GROUPS, P]), ALU.mult), "cb")

            def decayed(c):
                for g in range(GROUPS):
                    for n in (2 * g, 2 * g + 1):
                        wait_emptied(dve, ("seg", c, n))
                    if g == 0 and c == 0:
                        wait_emptied(dve, "cb")
                    eg = E[:, HPG * g:HPG * (g + 1), :]
                    dve.tensor_tensor(eg, eg, CB[:, GROUPS * c + g, :].unsqueeze(1).broadcast_to([P, HPG, P]),
                                      ALU.mult).then_inc(step["m_ready"], 1)

            def state_in():
                wait_emptied(dve, ("cum", 0))
                for half in range(2):
                    wait_emptied(dve, ("xst", half))
                dve.tensor_tensor(heads(XDD[:, :], HD_S), heads(XD[:, 0, :], HD_S),
                                  bc(DTS[:, 8, 16:32], HD_S), ALU.mult).then_inc(step["st_ready"], 1)

            def own_part(c):
                dve.wait_ge(step["skip_ready"], 2 * c + 2)
                for g in range(GROUPS):
                    yg = Y[:, c, 512 * g:512 * g + 512]
                    wait_full(dve, ("diag", c, g))
                    free(dve.tensor_tensor(yg, side_bank(("diag", c, g))[:, :], yg, ALU.add), ("diag", c, g))

            def state_part():
                wait_emptied(dve, ("cum", 1))
                for g in range(GROUPS):
                    yg, tmp = Y[:, 1, 512 * g:512 * g + 512], XD[:, 0, 512 * g:512 * g + 512]
                    wait_emptied(dve, ("diag", 1, g))
                    wait_full(dve, ("off", g))
                    free(dve.tensor_tensor(heads(tmp, HD_S), heads(side_bank(("off", g))[:, :], HD_S),
                                           bc(DTS[:, 9, HPG * g:HPG * (g + 1)], HD_S), ALU.mult), ("off", g))
                    wait_emptied(dve, ("off", g))
                    after(dve.tensor_tensor(yg, yg, tmp, ALU.add))

            def gated(g):
                cols = slice(512 * g, 512 * g + 512)
                dve.wait_ge(step["z_gated"], 2 * g + 2)
                wait_emptied(dve, ("diag", 0, g))
                after(dve.tensor_tensor(Y[:, 0, cols], Y[:, 0, cols], Z[:, 0, cols], ALU.mult))
                dve.tensor_tensor(Y[:, 1, cols], Y[:, 1, cols], Z[:, 1, cols], ALU.mult)\
                   .then_inc(step["y_ready"], 1)

            def gated_norm(g):
                for t in range(NT):
                    cols = slice(512 * g, 512 * g + 512)
                    dve.scalar_tensor_tensor(out=Y[:, t, cols], in0=Y[:, t, cols],
                                             scalar=SQS[:, 60 + 2 * t + g:61 + 2 * t + g], in1=GS[:, cols],
                                             op0=ALU.mult, op1=ALU.mult).then_inc(step["yn_ready"], 1)

            def mix_side(n):
                st = SQS[:, 64:80]
                if n == 13:
                    index_keys()
                if n == 14:
                    step_sizes()
                if n == 15:
                    decay_in(0)
                if 17 <= n <= 22:
                    score_add(2 * n - 34)
                    score_add(2 * n - 33)
                if 17 <= n <= 27:
                    conv_rest(n - 17)
                if n == 27:
                    conv_rest(11)
                if n in (23, 24):
                    top(0, 4 * (n - 23), 4 * (n - 22))
                if n == 24:
                    select(0)
                if 25 <= n <= 28:
                    top(1, 2 * (n - 25), 2 * (n - 24))
                if n == 29:
                    select(1)
                if n == 30:
                    head_squares(K, 0, 24, O_WIN + 6)
                if n in (31, 32):
                    inputs(n - 31)
                if n == 33:
                    head_squares(Q, 0, 8, O_WIN + 7)
                if n == 34:
                    maps()
                    decayed(0)
                if n == 35:
                    state_in()
                if n == 36:
                    own_part(0)
                    decay_in(1)
                if n == 37:
                    head_squares(Q, 1, 16, O_WIN + 8)
                    dve.tensor_scalar(SQS[:, 8:32], SQS[:, 8:32], 1.0 / HD, EPS, ALU.mult, ALU.add)\
                       .then_inc(step["qk_var"], 1)
                if n == 38:
                    qk_norm()
                if n == 40:
                    decayed(1)
                if n == 42:
                    own_part(1)
                if n == 43:
                    state_part()
                for h in {43: (0,), 44: (1,), 45: (2, 3), 46: (4, 5), 47: (6, 7)}.get(n, ()):
                    attn_logits(0, h, Lm, MK, st)
                for h in {44: (0,), 45: (1,), 46: (2, 3), 47: (4, 5)}.get(n, ()):
                    attn_probs(0, h, Lm, st)
                if n in (44, 46):
                    gated((n - 44) // 2)

            def fox_logs():
                o = O_FOX + 2
                for t in range(NT):
                    dve.wait_ge(acc_freed[o % 2][t], o // 2 + 1)
                dve.wait_ge(fb_landed, 16)
                T = FS
                v = T[:, 0, :].rearrange("p (t h) -> p t h", t=NT)
                after(dve.tensor_tensor(v, v, FB[:, :].unsqueeze(1).broadcast_to([P, NT, HEADS_F]), ALU.add))
                dve.scalar_tensor_tensor(out=T[:, 1, :], in0=T[:, 0, :], scalar=-1.0, in1=T[:, 0, :],
                                         op0=ALU.mult, op1=ALU.min).then_inc(step["f_a"], 1)
                log1p_exp(T, step["f_a"], step["f_b"], 0)
                after(dve.tensor_scalar(T[:, 5, :], T[:, 0, :], 0.0, None, ALU.min))
                dve.tensor_tensor(T[:, 7, :], T[:, 6, :], T[:, 5, :], ALU.subtract).then_inc(step["lf_ready"], 1)

            def fox_parts():
                wait_full(dve, "fcum")
                src = side_bank("fcum")[:, 0:32].rearrange("p (t h) -> p t h", t=NT)
                p0, p1, p2 = (NC[:, :, HEADS_F * k:HEADS_F * (k + 1)] for k in range(3))
                after(dve.tensor_copy(NCB[:, :, :], src))
                after(dve.tensor_copy(p0, NCB[:, :, :]))
                free(dve.tensor_tensor(p2, src, p0, ALU.subtract), "fcum")
                wait_emptied(dve, "fcum")
                after(dve.tensor_copy(NCB[:, :, :], p2))
                after(dve.tensor_copy(p1, NCB[:, :, :]))
                dve.tensor_tensor(p2, p2, p1, ALU.subtract).then_inc(step["nc_ready"], 1)

            def fox_side(n):
                if n == 13:
                    fox_logs()
                if n == 16:
                    fox_parts()
                if n == 20:
                    dve.wait_ge(consts_ready, 4)
                if n >= 21 and n % 2 == 1:
                    attn_logits(1, (n - 21) // 2, Lf, FMf, FST)
                if n >= 22 and n % 2 == 0:
                    attn_probs(1, (n - 22) // 2, Lf, FST)

            dve.wait_ge(x_landed[0], 16)
            dve.wait_ge(x_landed[1], 16)
            lo(0, 0)
            norm(0, 1, 1, 1, 0, 0)
            seen = {}
            prev = None
            for n, (kind, col, width) in enumerate(WIN):
                for j in range(4):
                    if n or j >= 2:
                        lo(B_WIN + n, j, width)
                    if prev and j == (1 if prev[0] == "z" else 0):
                        take(*prev)
                    mix_side(4 * n + j)
                prev = (kind, O_WIN + n, seen.get(kind, 0), B_WIN + n)
                seen[kind] = seen.get(kind, 0) + 1
            lo(B_WOUT, 0)
            take(*prev)
            dve.wait_ge(step["yss_ready"], 4)
            dve.tensor_scalar(SQS[:, 60:64], SQS[:, 56:60], 2.0 / SSD_W, EPS, ALU.mult, ALU.add)\
               .then_inc(step["y_var"], 1)
            dve.wait_ge(step["y_std"], 1)
            after(dve.reciprocal(SQS[:, 60:64], SQS[:, 60:64]))
            dve.wait_ge(gs_landed, 16)
            gated_norm(0)
            gated_norm(1)
            low_xt(("yt", 0), 0, 9)
            low_xt(("yt", 1), 1, 10)
            lo(B_WOUT, 1)
            for h in (6, 7):
                attn_probs(0, h, Lm, SQS[:, 64:80])
            low_xt(("yt", 2), 2, 11)
            low_xt(("yt", 3), 3, 12)
            for n in range(DOWN):
                for j in range(4):
                    if n or j >= 2:
                        lo(B_WOUT + n, j)
                    if n == 0 and j >= 2:
                        for h in range(4 * j - 8, 4 * j - 4):
                            attn_low(h)
                    if n and j == 1:
                        add_panel(O_WOUT + n - 1, B_WOUT + n - 1, n - 1, X, False)
                        summed(O_WOUT + n - 1)
            lo(B_M1, 0)
            add_panel(O_WOUT + 3, B_WOUT + 3, 3, X, False)
            summed(O_WOUT + 3)
            norm(1, 5, 2, 2, 12, B_M1)
            for k in range(2):
                dve.memset(RB[:, k, :], 0.0).then_inc(hl_ready, 1)
            mlp(B_M1, O_M1, 0, X, False)
            lo(B_FOX, 0)
            add_panel(O_FOX - 1, B_FOX - 1, DOWN - 1, X, False)
            summed(O_FOX - 1)
            norm(2, 9, 3, 3, 20, B_FOX)
            seen = {}
            prev = None
            for n, (kind, col, width) in enumerate(FOX):
                for j in range(4):
                    if n or j >= 2:
                        lo(B_FOX + n, j, width)
                    if j == 0 and prev:
                        take(*prev)
                    fox_side(4 * n + j)
                prev = (kind, O_FOX + n, seen.get(kind, 0), B_FOX + n)
                seen[kind] = seen.get(kind, 0) + 1
            def fox_low(n):
                dve.wait_ge(xh_ready, 28 + n + 1)
                pair = slice(2 * n, 2 * n + 2)
                dve.tensor_tensor(XL[:, pair, :], FQ[:, pair, :], XH[:, pair, :].bitcast(F32), ALU.subtract)\
                   .then_inc(step["fl_ready"], 1)

            lo(B_FOUT, 0)
            attn_probs(1, 15, Lf, FST)
            take(*prev)
            fox_low(0)
            fox_low(1)
            lo(B_FOUT, 1)
            for n in range(2, 6):
                fox_low(n)
            for n in range(DOWN):
                for j in range(4):
                    if n or j >= 2:
                        lo(B_FOUT + n, j)
                    if n == 0 and j >= 2:
                        fox_low(j + 4)
                    if n and j == 1:
                        add_panel(O_FOUT + n - 1, B_FOUT + n - 1, n - 1, HB, True)
                        summed(O_FOUT + n - 1)
            lo(B_M2, 0)
            add_panel(O_FOUT + 3, B_FOUT + 3, 3, HB, True)
            summed(O_FOUT + 3)

            def post(n_ssq, n_root, gain, final):
                root(n_ssq, n_root)
                for q in range(4):
                    cols = slice(512 * q, 512 * q + 512)
                    for t in range(NT):
                        ins = dve.scalar_tensor_tensor(out=HB[:, t, cols], in0=HB[:, t, cols],
                                                       scalar=rstd[:, t:t + 1], in1=gain[:, cols],
                                                       op0=ALU.mult, op1=ALU.mult)
                        ins.then_inc(step["post_add"], 1)
                    dve.wait_ge(step["post_add"], (8 if final else 0) + 2 * q + 2)
                    after(dve.tensor_tensor(X[:, 0, cols], X[:, 0, cols], HB[:, 0, cols], ALU.add))
                    dve.tensor_tensor(X[:, 1, cols], X[:, 1, cols], HB[:, 1, cols], ALU.add)\
                       .then_inc(x_final if final else sum_ready, 1)

            dve.wait_ge(g1_landed, 16)
            post(13, 4, G1, False)
            dve.wait_ge(sum_ready, 16)
            norm(3, 17, 5, 4, 36, B_M2)
            mlp(B_M2, O_M2, 2 * UP, HB, True)
            add_panel(O_M2 + 2 * O_HALF - 1, B_END - 1, DOWN - 1, HB, False)
            summed(O_M2 + 2 * O_HALF - 1)
            dve.wait_ge(g_landed, 16 * 5)
            post(21, 6, G, True)

        @block.tensor
        def _(pe):
            def acc_wait(o, n=None):
                n = o // 2 if n is None else n
                if not (isinstance(n, int) and n == 0):
                    for t in range(2):
                        pe.wait_ge(acc_freed[o % 2][t], n)

            def rows(b, j, o_par, first, last, k0, h=XH, l=XL, width=512):
                pe.wait_ge(lo_ready, 4 * b + j + 1)
                for kk in range(4):
                    for t in range(NT):
                        o = acc[o_par][t][:, 0:width]
                        sh, sl = (z[:, k0 + kk, t * P:(t + 1) * P] for z in (h, l))
                        mh, ml = wh[:, j % 2, kk, 0:width], wl[:, j % 2, kk, 0:width]
                        pe.matmul(o, sh, mh, start=first and kk == 0, stop=False)
                        pe.matmul(o, sh, ml, start=False, stop=False)
                        mm = pe.matmul(o, sl, mh, start=False, stop=last and kk == 3)
                mm.then_inc(chunk_used, 1)

            def cols(b, j, o_par, first, last, k0):
                pe.wait_ge(lo_ready, 4 * b + j + 1)
                for kk in range(4):
                    for f in range(4):
                        o = acc[o_par][f // 2][:, TOK * (f % 2):TOK * (f % 2 + 1)]
                        sh, sl = (z[:, j % 2, kk, f * P:(f + 1) * P] for z in (wh, wl))
                        mh, ml = XH[:, k0 + kk, :], XL[:, k0 + kk, :]
                        pe.matmul(o, sh, mh, start=first and kk == 0 and f % 2 == 0, stop=False,
                                  skip_group_check=True)
                        pe.matmul(o, sh, ml, start=False, stop=False, skip_group_check=True)
                        mm = pe.matmul(o, sl, mh, start=False, stop=last and kk == 3, skip_group_check=True)
                mm.then_inc(chunk_used, 1)

            def turn(m, n):
                wait_free(pe, ("xt", m, n))
                bk = side_bank(("xt", m, n))
                for i in range(4):
                    k, t = 2 * n + i // 2, i % 2
                    mm = pe.transpose(bk[:, i * P:(i + 1) * P], (XN1 if m else XN0)[:, t, k * P:(k + 1) * P], ident[:, :])
                full(mm, ("xt", m, n))

            def turn_quarter(m, q):
                if q < 3:
                    pe.wait_ge(xn_ready, 7 * m + 2 * q + 2)
                else:
                    pe.wait_ge(xn_ready, 7 * m + 7)
                    pe.wait_ge(g_used, m + 1)
                turn(m, 2 * q)
                turn(m, 2 * q + 1)

            def xt_wait(m, j, extra):
                for n in (2 * j, 2 * j + 1):
                    b, k = uses[("xt", m, n)]
                    pe.wait_ge(side_free[b], k + 1)

            def first_panel(form, m, b, o):
                turn_quarter(m, 0)
                turn_quarter(m, 1)
                for j in range(4):
                    if j == 0:
                        acc_wait(o)
                    xt_wait(m, j, 0)
                    form(b, j, o % 2, j == 0, j == 3, 4 * j)
                    if j < 2:
                        turn_quarter(m, j + 2)

            def panel(form, b, o, width=512, plan={}, slot=0):
                acc_wait(o)
                for j in range(4):
                    if form is cols:
                        cols(b, j, o % 2, j == 0, j == 3, 4 * j)
                    else:
                        rows(b, j, o % 2, j == 0, j == 3, 4 * j, width=width)
                    side_work(plan, slot + j)

            def mlp(m, b0, o0, u0):
                for half in range(2):
                    b, o, u = b0 + half * B_HALF, o0 + half * O_HALF, u0 + half * UP
                    if half == 0:
                        first_panel(cols, m, b, o)
                    else:
                        panel(cols, b, o)
                    with pe.Fori(0, UP // 2 - 1) as i:
                        for s in (1, 2):
                            for k in range(2):
                                pe.wait_ge(acc_freed[(o + s) % 2][k], i + (o + s) // 2)
                            for j in range(4):
                                cols(b + 2 * i + s, j, (o + s) % 2, j == 0, j == 3, 4 * j)
                    panel(cols, b + UP - 1, o + UP - 1)
                    for n in range(DOWN):
                        on = o + UP + n
                        acc_wait(on)
                        for j in range(8):
                            if n == 0:
                                pe.wait_ge(hl_ready, 2 * (u + j) + 4)
                            rows(b + UP + 2 * n + j // 4, j % 4, on % 2, j == 0, j == 7, 4 * j, hh, hl)

            def attn_scores(a, h):
                bk = side_bank(("S", a, h))
                q, k = (FQ[:, h, :], FK[:, h, :]) if a else (QT[:, h, :], KTt[:, h // (HEADS_A // KV_A), :])
                for t in range(NT):
                    mm = pe.matmul(bk[:, ctr(t)], q[:, t * P:(t + 1) * P], k[:, 0:(t + 1) * P],
                                   start=True, stop=not a)
                    if a:
                        mm = pe.matmul(bk[:, ctr(t)], OH[:, h:h + 1].broadcast_to([3 * HEADS_F, P]),
                                       NCT[:, 0:(t + 1) * P], start=False, stop=True)
                return mm

            def attn_turn(a, h, L):
                pe.wait_ge(step["probs_ready"], a * HEADS_A + h + 1)
                bk = side_bank(("PT", a, h))
                for i in range(3):
                    mm = pe.transpose(bk[:, i * P:(i + 1) * P], L[:, h % L.shape[1], i * P:(i + 1) * P], ident[:, :])
                return mm

            def attn_values(a, h, PT):
                wait_emptied(pe, ("PT", a, h))
                o = (O_FOX + 9 + h // 4) if a else (O_WIN + 11)
                if not a or h % 4 == 0:
                    for t in range(NT):
                        pe.wait_ge(acc_freed[o % 2][t], o // 2 + 1)
                bk = side_bank(("O", a, h))
                vs = FV if a else V
                kv = h if a else h // (HEADS_A // KV_A)
                c = slice(kv * HD, (kv + 1) * HD)
                pe.matmul(bk[:, 0:TOK], vs[:, 0, c], PT[:, h, 0:TOK], start=True, stop=False)
                return pe.matmul(bk[:, P:TOK], vs[:, 1, c], PT[:, h, TOK:3 * P], start=False, stop=True)

            def index_scores(g):
                t, per, hs = score_heads(g)
                for i in range(per):
                    h, width = hs[i], P * (t + 1)
                    p0 = HD_I * (h % 2)
                    mm = pe.matmul(side_bank(("score", g))[:, width * i:width * (i + 1)],
                                   QI[p0:p0 + HD_I, h // 2, t * P:(t + 1) * P], KIT[p0:p0 + HD_I, 0:width],
                                   start=True, stop=True)
                return mm

            def turn4(name, blocks):
                for i, blk in enumerate(blocks):
                    mm = pe.transpose(side_bank(name)[:, i * P:(i + 1) * P], blk, ident[:, :])
                return mm

            def fill(name):
                wait_free(pe, name)
                bk = side_bank(name)
                kind = name if isinstance(name, str) else name[0]
                if kind == "params":
                    pe.wait_ge(vec_landed, 16 * 8)
                    mm = pe.transpose(bk[:, 0:62], PR[:, :], ident[0:62, 0:62])
                elif kind == "ki":
                    pe.wait_ge(step["ki_rows"], 4)
                    mm = turn4(name, [KI2[:, t, :] for t in range(NT)])
                elif kind == "score":
                    if name[1] == 0:
                        wait_emptied(pe, "ki")
                    mm = index_scores(name[1])
                elif kind == "cum":
                    c = name[1]
                    pe.wait_ge(step["adt_ready"], 1)
                    pe.wait_ge(consts_ready, 3)
                    adt = DTS[:, 7, 16 * c:16 * c + 16]
                    pe.matmul(bk[:, 0:16], Um[:, :], adt, start=True, stop=True)
                    mm = pe.matmul(bk[:, 16:32], Vm[:, :], adt, start=True, stop=True)
                elif kind == "seg":
                    c, n = name[1:]
                    pe.wait_ge(step["decay_in"], c + 1)
                    mm = pe.matmul(bk[:, :], Vm[:, :], E[:, 4 * n:4 * n + 4, :].rearrange("p h l -> p (h l)"),
                                   start=True, stop=True)
                elif kind == "xst":
                    n = name[1]
                    pe.wait_ge(step["silu_done"], 3 if n == 4 else (n % 2) + 1)
                    where = [(n // 2, 4 * (n % 2) + i) if n < 4 else (i // 2, 8 + i % 2) for i in range(4)]
                    mm = turn4(name, [XC[:, k, t * P:(t + 1) * P] for t, k in where])
                elif kind == "cb":
                    for c in range(NT):
                        for g in range(GROUPS):
                            tk = slice(c * P, (c + 1) * P)
                            mm = pe.matmul(bk[:, (2 * c + g) * P:(2 * c + g + 1) * P],
                                           XC[:, 8 + g, tk], XC[:, 10 + g, tk], start=True, stop=True)
                elif kind == "state":
                    g = name[1]
                    pe.wait_ge(step["st_ready"], 1)
                    wait_emptied(pe, ("xst", 4))
                    mm = pe.matmul(bk[:, :], BM[:, 0, g * STATE:(g + 1) * STATE], XDD[:, 512 * g:512 * g + 512],
                                   start=True, stop=True)
                elif kind == "diag":
                    c, g = name[1:]
                    wait_emptied(pe, ("xst", 2 * c + g))
                    pe.wait_ge(step["m_ready"], 2 * c + g + 1)
                    for i in range(HPG):
                        h = HPG * g + i
                        mm = pe.matmul(bk[:, i * HD_S:(i + 1) * HD_S], E[:, h, :],
                                       XD[:, c, h * HD_S:(h + 1) * HD_S], start=True, stop=True)
                elif kind == "off":
                    g = name[1]
                    wait_emptied(pe, ("state", g))
                    mm = pe.matmul(bk[:, :], XC[:, 10 + g, P:2 * P], ST[:, g, :], start=True, stop=True)
                elif kind == "qkt":
                    n = name[1]
                    pe.wait_ge(step["qk_normed"], 6 if n >= 4 else 4 if n >= 2 else 2)
                    src, h0 = (Q, 2 * n) if n < 4 else (K, 2 * n - 8)
                    mm = turn4(name, [src[:, i % 2, (h0 + i // 2) * HD:(h0 + i // 2 + 1) * HD] for i in range(4)])
                elif kind == "yt":
                    n = name[1]
                    pe.wait_ge(step["yn_ready"], 2 * (n // 2) + 2)
                    mm = turn4(name, [Y[:, i % 2, (2 * n + i // 2) * P:(2 * n + i // 2 + 1) * P] for i in range(4)])
                elif kind == "S":
                    a, h = name[1:]
                    if a:
                        wait_emptied(pe, "fct")
                        pe.wait_ge(consts_ready, 4)
                        o = O_FOX + (1 if h < 4 else 2 + 2 * (h // 4))
                        for t in range(NT):
                            for x in (o, o - 1):
                                pe.wait_ge(acc_freed[x % 2][t], x // 2 + 1)
                    elif h == 0:
                        for n in range(6):
                            wait_emptied(pe, ("qkt", n))
                    mm = attn_scores(a, h)
                elif kind == "PT":
                    mm = attn_turn(name[1], name[2], Lf if name[1] else Lm)
                elif kind == "O":
                    mm = attn_values(name[1], name[2], PTf if name[1] else PTm)
                elif kind == "fcum":
                    pe.wait_ge(step["lf_ready"], 1)
                    pe.wait_ge(consts_ready, 4)
                    pe.matmul(bk[:, 0:16], Uf[:, :], FS[:, 7, 0:16], start=True, stop=True)
                    pe.matmul(bk[:, 16:32], ONE[:, :], FS[:, 7, 0:16], start=True, stop=False)
                    mm = pe.matmul(bk[:, 16:32], Uf[:, :], FS[:, 7, 16:32], start=False, stop=True)
                else:
                    pe.wait_ge(step["nc_ready"], 1)
                    for t in range(NT):
                        mm = pe.transpose(bk[0:3 * HEADS_F, t * P:(t + 1) * P], NC[:, t, :], ident[:, :])
                full(mm, name)

            def side_work(plan, n):
                for name in plan.get(n, ()):
                    fill(name)

            pe.wait_ge(consts_ready, 1)
            first_panel(cols, 0, B_WIN, O_WIN)
            for n, (kind, col, width) in enumerate(WIN):
                if n:
                    panel(cols if kind in TFORM else rows, B_WIN + n, O_WIN + n, width, MIX_AT, 4 * n)
            side_work(MIX_AT, 48)
            acc_wait(O_WOUT)
            for j in range(4):
                if j == 1:
                    side_work(MIX_AT, 49)
                elif j > 1:
                    side_work(MIX_AT, 48 + j)
                for n in ((("yt", 2 * j), ("yt", 2 * j + 1)) if j < 2 else
                          [("O", 0, h) for h in range(4 * j - 8, 4 * j - 4)]):
                    wait_emptied(pe, n)
                rows(B_WOUT, j, O_WOUT % 2, j == 0, j == 3, 4 * j)
            for n in range(1, DOWN):
                panel(rows, B_WOUT + n, O_WOUT + n)
            mlp(1, B_M1, O_M1, 0)
            first_panel(cols, 2, B_FOX, O_FOX)
            for n, (kind, col, width) in enumerate(FOX):
                if n:
                    panel(cols if kind in TFORM else rows, B_FOX + n, O_FOX + n, width, FOX_AT, 4 * n)
            acc_wait(O_FOUT)
            for j in range(4):
                pe.wait_ge(step["fl_ready"], 2 * j + 2)
                rows(B_FOUT, j, O_FOUT % 2, j == 0, j == 3, 4 * j)
                if j < 2:
                    side_work(FOX_AT, 52 + j)
            for n in range(1, DOWN):
                panel(rows, B_FOUT + n, O_FOUT + n)
            mlp(3, B_M2, O_M2, 2 * UP)


_INS = ['x', 'g_mix', 'w_in', 'conv_w', 'conv_b', 'dt_bias', 'a_log', 'd_skip', 'g_ssd', 'g_q', 'g_k', 'g_kidx',
        'w_out', 'g_mlp', 'w_up', 'w_down', 'norm_g_2', 'mlp_w1_2', 'mlp_w2_2', 'fox_w_in_2', 'fox_b_f_2',
        'fox_w_out_2']


def kernel(**inputs):
    import numpy as np
    import concourse.bacc as bacc
    from concourse.bass_utils import run_bass_kernel_spmd

    nc = bacc.Bacc("TRN2", target_bir_lowering=False, num_devices=1)
    arrays, args = {}, []
    for name in _INS:
        a = np.ascontiguousarray(inputs[name])
        arrays[f"in_{name}_dram"] = a
        args.append(nc.dram_tensor(f"in_{name}_dram", a.shape, mybir.dt.from_np(a.dtype),
                                   kind="ExternalInput").ap())
    args.append(nc.dram_tensor("out_dram", (1, TOK, D), F32, kind="ExternalOutput").ap())
    hybrid_then_fox(nc, *args)
    return run_bass_kernel_spmd(nc, [arrays], core_ids=[0]).results[0]["out_dram"]
```

```python
from contextlib import ExitStack

import concourse.bass as bass
from concourse import mybir

P = 128
TOK = 256
NT = TOK // P
D = 2048
KT = D // P
EPS = 1e-6
NEG = -1e30

SSD_W, HEADS_S, HD_S, GROUPS, STATE, TAPS = 1024, 16, 64, 2, 128, 4
HPG = HEADS_S // GROUPS
CONV_CH = SSD_W + 2 * GROUPS * STATE
HEADS_A, KV_A, HD = 8, 4, 128
HEADS_I, HD_I = 16, 64
TOPK = 64
C_Z = 0
C_XBC = C_Z + SSD_W
C_DT = C_XBC + CONV_CH
C_Q = C_DT + HEADS_S
C_K = C_Q + HEADS_A * HD
C_V = C_K + KV_A * HD
C_QI = C_V + KV_A * HD
C_KI = C_QI + HEADS_I * HD_I
C_WI = C_KI + HD_I
W_KW = HD_I + HEADS_I
W_SMALL = W_KW + HEADS_S
HEADS_F = 16
F = 4 * D
HALF = F // 2
UP = HALF // 512
DOWN = D // 512
HT = HALF // P

F32 = mybir.dt.float32
F32R = mybir.dt.float32r
BF16 = mybir.dt.bfloat16
ALU = mybir.AluOpType
ACT = mybir.ActivationFunctionType
AX = mybir.AxisListType.X
SCALE = HD ** -0.5


def hybrid_then_fox(nc, x, g_mix, w_in, conv_w, conv_b, dt_bias, a_log, d_skip, g_ssd, g_q, g_k,
                    g_kidx, w_out, g_mlp, w_up, w_down, norm_g, mlp_w1, mlp_w2, fox_w_in, fox_b_f,
                    fox_w_out, out):
    ctx = ExitStack()
    with ctx:
        def sem(name):
            return ctx.enter_context(nc.semaphore(name))

        def sb(name, shape, dt=F32):
            return ctx.enter_context(nc.sbuf_tensor(name, shape, dt))

        X = sb("X", [P, NT, D])
        XH = sb("XH", [P, KT, TOK], F32R)
        XL = sb("XL", [P, KT, TOK], F32R)
        wh = sb("wh", [P, 4, 4, 512], F32R)
        G = sb("G", [P, D])
        ident = sb("ident", [P, P])
        junk = sb("junk", [P, 512], BF16)
        ssq = sb("ssq", [P, NT, 4])
        rstd = sb("rstd", [P, 6, NT])

        arena = -(-nc.sbuf_base // 32) * 32

        def region(start, *layers):
            end = start
            for layer in layers:
                at = start
                for name, shape, dt in layer:
                    T[name] = nc.alloc_sbuf_tensor_at(name, shape, dt, offset=at)
                    size = 2 if dt == BF16 else 4
                    for n in shape[1:]:
                        size *= n
                    at += -(-size // 32) * 32
                end = max(end, at)
            assert end <= nc.sbuf_usable_end
            return end

        T = {}
        arena = region(arena, [("raw", [P, 4, 4, 512], F32)], [("wl", [P, 4, 4, 512], F32R)])
        raw, wl = T["raw"], T["wl"]
        at = region(arena, [("SM", [P, NT, W_SMALL], F32), ("VB", [P, 3 * HEADS_S + HD_I], F32),
                            ("PR", [TAPS * 12 + 14, P], F32), ("PC", [P, TAPS * 12 + 14], F32),
                            ("SQS", [P, 96], F32), ("DTS", [P, 10, NT * HEADS_S], F32),
                            ("FMm", [P, 3 * P], F32), ("Um", [P, P], F32), ("Vm", [P, P], F32),
                            ("MK", [P, 3 * P], F32), ("CB", [P, NT * GROUPS, P], F32),
                            ("BM", [P, NT, GROUPS * STATE], F32), ("Y", [P, NT, SSD_W], F32),
                            ("XD", [P, NT, SSD_W], F32)])
        at2 = region(at, [("E", [P, HEADS_S, P], F32)], [("GS", [P, SSD_W], F32)])
        at3 = region(at2, [("XC", [P, CONV_CH // P, TOK], F32)], [("PTm", [P, HEADS_A, 3 * P], F32)])
        region(at, [("XN0", [P, NT, D], F32)])
        low = region(at, [("NHm", [P, KT, W_SMALL], F32R)])
        region(low, [("NRm", [P, KT, W_SMALL], F32)], [("NLm", [P, KT, W_SMALL], F32R)])
        at = region(at3, [("RCm", [P, TOK], F32), ("SMT", [W_SMALL, TOK], F32)], [("XDD", [P, SSD_W], F32)],
                    [("ST", [P, GROUPS, 512], F32)])
        at = region(at, [("U", [P, CONV_CH // P, TAPS - 1 + TOK], F32)],
                    [("Q", [P, NT, HEADS_A * HD], F32), ("K", [P, NT, KV_A * HD], F32)],
                    [("Z", [P, NT, SSD_W], F32)])
        at = region(at, [("QI", [P, HEADS_I // 2, TOK], F32), ("R", [P, 2, 512], F32)],
                    [("QT", [P, HEADS_A, TOK], F32), ("KTt", [P, KV_A, TOK], F32)])
        at = region(at, [("KI2", [P, NT, 2 * HD_I], F32), ("KIT", [P, TOK], F32), ("SC", [P, 3 * P], F32),
                         ("WK", [P, TOK], F32), ("GT", [P, TOK], F32), ("EQ", [P, TOK], F32),
                         ("CS", [P, TOK], F32), ("M8", [P, 8], F32)],
                    [("Lm", [P, 4, 3 * P], F32), ("V", [P, NT, KV_A * HD], F32)])
        at = region(arena, [("HB", [P, NT, D], F32)], [("FQ", [P, HEADS_F, TOK], F32)])
        region(at, [("hh", [P, HT, TOK], F32R), ("hl", [P, HT, TOK], F32R), ("RB", [P, 2, 512], F32)])
        region(at, [("G1", [P, D], F32), ("HG", [P, NT, D], F32), ("XG", [P, NT, D], F32)])
        at = region(at, [("FK", [P, HEADS_F, TOK], F32)])
        low = region(at, [("NHf", [P, KT, HEADS_F], F32R)])
        region(low, [("NRf", [P, KT, HEADS_F], F32)], [("NLf", [P, KT, HEADS_F], F32R)])
        region(at, [("FV", [P, NT, D], F32), ("PTf", [P, HEADS_F, 3 * P], F32), ("Lf", [P, 2, 3 * P], F32),
                    ("FS", [P, 10, NT * HEADS_F], F32), ("FB", [P, HEADS_F], F32),
                    ("NCB", [P, NT, HEADS_F], BF16), ("NC", [P, NT, 3 * HEADS_F], F32),
                    ("NCT", [3 * HEADS_F, TOK], BF16), ("OH", [3 * HEADS_F, HEADS_F], BF16),
                    ("FMf", [P, 3 * P], F32), ("Uf", [P, P], F32), ("ONE", [P, P], F32),
                    ("FST", [P, 16], F32), ("RCf", [P, TOK], F32), ("FTT", [HEADS_F, TOK], F32)])
        SM, VB, PR, PC, SQS, DTS, FMm, Um, Vm, MK = (T[n] for n in "SM VB PR PC SQS DTS FMm Um Vm MK".split())
        CB, BM, Y, XD, E, GS, XC, PTm, XN0, XDD, ST = (T[n] for n in "CB BM Y XD E GS XC PTm XN0 XDD ST".split())
        U, Q, K, Z, QI, R, QT, KTt, KI2, KIT = (T[n] for n in "U Q K Z QI R QT KTt KI2 KIT".split())
        SC, WK, GT, EQ, CS, M8, Lm, V = (T[n] for n in "SC WK GT EQ CS M8 Lm V".split())
        HB, FQ, hh, hl, RB, HG, XG, FK, G1, FV, PTf = (T[n] for n in "HB FQ hh hl RB HG XG FK G1 FV PTf".split())
        Lf, FS, FB, NCB, NC, NCT, OH, FMf, Uf, ONE = (T[n] for n in "Lf FS FB NCB NC NCT OH FMf Uf ONE".split())
        FST = T["FST"]
        narrow = {0: (T["NHm"], T["NRm"], T["NLm"]), 2: (T["NHf"], T["NRf"], T["NLf"])}
        SMT, FTT = T["SMT"], T["FTT"]
        RCm, RCf = T["RCm"], T["RCf"]

        bank = [ctx.enter_context(nc.psum_tensor(f"bank{i}", [P, 512], F32)) for i in range(8)]
        acc = [[bank[0], bank[1]], [bank[2], bank[3]]]
        side = bank[4:8]

        raw_landed = [sem(f"raw_landed{i}") for i in range(4)]
        hi_ready = sem("hi_ready")
        lo_ready = sem("lo_ready")
        chunk_used = sem("chunk_used")
        acc_freed = [[sem(f"acc_freed{p}{b}") for b in range(2)] for p in range(2)]
        side_full = [sem(f"side_full{i}") for i in range(4)]
        side_free = [sem(f"side_free{i}") for i in range(4)]
        x_landed = [sem(f"x_landed{i}") for i in range(4)]
        g_landed = sem("g_landed")
        narrow_landed = sem("narrow_landed")
        narrow_high = sem("narrow_high")
        narrow_low = sem("narrow_low")
        g1_landed = sem("g1_landed")
        vec_landed = sem("vec_landed")
        gs_landed = sem("gs_landed")
        fb_landed = sem("fb_landed")
        consts_ready = sem("consts_ready")
        pool_order = sem("pool_order")
        dve_order = sem("dve_order")
        act_order = sem("act_order")
        sum_ready = sem("sum_ready")
        ssq_ready = sem("ssq_ready")
        var_ready = sem("var_ready")
        std_ready = sem("std_ready")
        xn_ready = sem("xn_ready")
        xh_ready = sem("xh_ready")
        sq_ready = sem("sq_ready")
        hh_ready = sem("hh_ready")
        hl_ready = sem("hl_ready")
        out_stored = sem("out_stored")
        x_final = sem("x_final")
        step = {n: sem(n) for n in (
            "ki_var", "ki_std", "ki_rows", "scores_used",
            "qk_var", "qk_std", "qk_normed", "logits_ready", "exp_ready", "probs_ready",
            "oh_ready", "conv_start", "conv_done", "silu_done",
            "dt_a", "dt_b", "adt_ready", "decay_in", "m_ready",
            "st_ready", "z_gated", "y_ready", "yss_ready", "y_var", "y_std",
            "yn_ready", "skip_ready", "fl_ready", "f_a", "f_b", "lf_ready", "nc_ready", "rs_ready", "hg_ready",
            "hb_gained")}

        block = ctx.enter_context(nc.Block())

        WIN = [("qi", C_QI), ("qi", C_QI + 512),
               ("xbc", C_XBC), ("xbc", C_XBC + 512), ("xbc", C_XBC + 1024),
               ("k", C_K), ("q", C_Q), ("q", C_Q + 512),
               ("z", C_Z), ("z", C_Z + 512), ("v", C_V)]
        FOX = [("fq", 0), ("fk", D)]
        for n in range(1, 4):
            FOX += [("fq", n * 512), ("fk", D + n * 512)]
        FOX += [("fv", 2 * D + n * 512) for n in range(4)]
        TFORM = ("qi", "xbc", "fq", "fk")
        B_WIN, O_WIN = 0, 0
        B_WOUT, O_WOUT = B_WIN + len(WIN), O_WIN + len(WIN)
        B_M1, O_M1 = B_WOUT + DOWN, O_WOUT + DOWN
        B_HALF, O_HALF = UP + 2 * DOWN, UP + DOWN
        B_FOX, O_FOX = B_M1 + 2 * B_HALF, O_M1 + 2 * O_HALF
        B_FOUT, O_FOUT = B_FOX + len(FOX), O_FOX + len(FOX)
        B_M2, O_M2 = B_FOUT + DOWN, O_FOUT + DOWN
        B_END = B_M2 + 2 * B_HALF
        assert O_HALF % 2 == 0

        uses = {}

        def use(name):
            uses[name] = (len(uses) % 4, len(uses) // 4)

        MIX_AT = {4: ["params"], 7: [("narrow", 0)], 8: [("narrow_rows", 0), ("rbc", 0)], 10: ["ki"],
                  11: [("score", 0), ("score", 1)],
                  12: [("cum", 0), ("cum", 1), ("score", 2), ("score", 3)],
                  17: [("seg", 0, 0), ("seg", 0, 1)], 18: [("seg", 0, 2), ("seg", 0, 3)],
                  25: [("xst", 0), ("xst", 1)], 26: [("xst", 2), ("xst", 3)], 27: [("xst", 4), "cb"],
                  30: [("diag", 0, 0), ("diag", 0, 1)],
                  32: [("state", 0), ("state", 1), ("seg", 1, 0), ("seg", 1, 1)],
                  33: [("seg", 1, 2), ("seg", 1, 3)],
                  34: [("qkt", n) for n in range(3)], 35: [("qkt", n) for n in range(3, 6)],
                  36: [("diag", 1, 0), ("diag", 1, 1)],
                  37: [("off", 0), ("off", 1), ("S", 0, 0), ("S", 0, 1)], 38: [("S", 0, 2), ("S", 0, 3)],
                  39: [("S", 0, 4), ("S", 0, 5)], 40: [("PT", 0, 0), ("PT", 0, 1), ("S", 0, 6), ("S", 0, 7)],
                  41: [("PT", 0, 2), ("PT", 0, 3)], 
                  44: [("yt", n) for n in range(4)],
                  43: [("PT", 0, 4), ("PT", 0, 5)], 45: [("PT", 0, 6), ("PT", 0, 7)] + [("O", 0, n) for n in range(4)],
                  46: [("O", 0, n) for n in range(4, 8)]}
        for g in range(4, 12, 2):
            MIX_AT[11 + g // 2] = [("score", g), ("score", g + 1)]
        FOX_S, FOX_PT = 15, 17
        FOX_O = {h: min(37 + h, 47) for h in range(12)}
        FOX_AT = {n: [] for n in range(50)}
        FOX_AT[3].append(("rbc", 2))
        FOX_AT[7].append(("narrow", 2))
        FOX_AT[8].append(("narrow_rows", 2))
        FOX_AT[10].append("fcum")
        FOX_AT[13].append("fct")
        for h in range(HEADS_F):
            FOX_AT[FOX_S + 2 * h].append(("S", 1, h))
            FOX_AT[FOX_PT + 2 * h].append(("PT", 1, h))
        for h in range(HEADS_F):
            FOX_AT[FOX_O.get(h, 48 if h < 14 else 49)].append(("O", 1, h))
        for n in range(8):
            use(("xt", 0, n))
        for n in sorted(MIX_AT):
            for u in MIX_AT[n]:
                use(u)
        for m in (1, 2):
            for n in range(8):
                use(("xt", m, n))
        for n in sorted(FOX_AT):
            for u in FOX_AT[n]:
                use(u)
        for n in range(8):
            use(("xt", 3, n))

        def score_heads(g):
            t, per, n = (0, 4, g) if g < 4 else (1, 2, g - 4)
            return t, per, [n % 2 + 2 * (per * (n // 2) + i) for i in range(per)]

        def ahead(part, b, n):
            if n > 2:
                part(b + n // 4, n % 4)

        def side_bank(name):
            return side[uses[name][0]]

        def wait_full(eng, name):
            b, n = uses[name]
            eng.wait_ge(side_full[b], n + 1)

        def wait_emptied(eng, name):
            b, n = uses[name]
            eng.wait_ge(side_free[b], n + 1)

        def wait_free(eng, name):
            b, n = uses[name]
            if n:
                eng.wait_ge(side_free[b], n)

        def full(ins, name):
            ins.then_inc(side_full[uses[name][0]], 1)

        def free(ins, name):
            ins.then_inc(side_free[uses[name][0]], 1)

        def bc(ap, n):
            return ap.unsqueeze(2).broadcast_to([P, ap.shape[1], n])

        def heads(ap, n):
            return ap.rearrange("p (h d) -> p h d", d=n)

        def ctr(k):
            return (slice(0, P), slice(P, 3 * P))[k]

        @block.sync
        def _(sp):
            def chunk(w, b, j, k0, col):
                if not (isinstance(b, int) and b == 0):
                    sp.wait_ge(chunk_used, 4 * b + j - 3)
                src = w[k0 * P:(k0 + 4) * P, col].rearrange("(k p) n -> p k n", p=P)
                sp.dma_start(raw[:, j, :, :], src).then_inc(raw_landed[j], 16)

            def panel(w, b, k0, col):
                for j in range(4):
                    chunk(w, b, j, k0 + 4 * j, slice(col, col + 512))

            def narrow_weights(w, dst, col, width, n0):
                sp.dma_start(dst[:, :, n0:n0 + width], w[:, col:col + width].rearrange("(k p) n -> p k n", p=P))\
                  .then_inc(narrow_landed, 16)

            def gain(src, used):
                sp.wait_ge(xn_ready, 4 * used)
                sp.dma_start(G[:, :], src.unsqueeze(0).broadcast_to([P, D])).then_inc(g_landed, 16)

            def mlp(w_a, w_b, b0, next_gain, used):
                for half in range(2):
                    b = b0 + half * B_HALF
                    panel(w_a, b, 0, half * HALF)
                    if half == 0:
                        gain(next_gain, used)
                    with sp.Fori(0, UP // 2 - 1) as i:
                        for s in (1, 2):
                            for j in range(4):
                                chunk(w_a, b + 2 * i + s, j, 4 * j,
                                      bass.ds(half * HALF + 512 * (2 * i + s), 512))
                    panel(w_a, b + UP - 1, 0, half * HALF + 512 * (UP - 1))
                    for n in range(DOWN):
                        for m in range(2):
                            panel(w_b, b + UP + 2 * n + m, half * HT + 16 * m, 512 * n)

            for q in range(4):
                cols = slice(512 * q, 512 * q + 512)
                sp.dma_start(X[:, :, cols], x[0].rearrange("(t p) n -> p t n", p=P)[:, :, cols])\
                   .then_inc(x_landed[q], 16)
                sp.dma_start(G[:, cols], g_mix[0:1, cols].broadcast_to([P, 512])).then_inc(x_landed[q], 16)
                if q < 3:
                    chunk(w_in[0], 0, q, 4 * q, slice(C_QI, C_QI + 512))
            chunk(w_in[0], 0, 3, 12, slice(C_QI, C_QI + 512))
            for n in range(1, len(WIN)):
                for j in range(4):
                    chunk(w_in[0], B_WIN + n, j, 4 * j, slice(WIN[n][1], WIN[n][1] + 512))
                    if n == 1 and j == 1:
                        wait_full(sp, ("xt", 0, 7))
                        narrow_weights(w_in[0], narrow[0][1], C_KI, W_KW, 0)
                        narrow_weights(w_in[0], narrow[0][1], C_DT, HEADS_S, W_KW)
                if n == 1:
                    gain(g_mlp[0], 1)
            for n in range(DOWN):
                panel(w_out[0], B_WOUT + n, 0, 512 * n)
            mlp(w_up[0], w_down[0], B_M1, norm_g[0, 0], 2)
            for n, (kind, col) in enumerate(FOX):
                panel(fox_w_in[0], B_FOX + n, 0, col)
                if n == 0:
                    narrow_weights(fox_w_in[0], narrow[2][1], 3 * D, HEADS_F, 0)
                    gain(norm_g[0, 2], 3)
            for n in range(DOWN):
                panel(fox_w_out[0], B_FOUT + n, 0, 512 * n)
                if n == 0:
                    sp.dma_start(G1[:, :], norm_g[0, 1].unsqueeze(0).broadcast_to([P, D])).then_inc(g1_landed, 16)
            mlp(mlp_w1[0], mlp_w2[0], B_M2, norm_g[0, 3], 4)
            for q in range(4):
                sp.wait_ge(x_final, q + 1)
                sp.dma_start(out[0].rearrange("(t p) n -> p t n", p=P)[:, :, 512 * q:512 * q + 512],
                             X[:, :, 512 * q:512 * q + 512]).then_inc(out_stored, 16)
            sp.wait_ge(out_stored, 64)

        def landed(b, j):
            return 16 * (b + 1)

        @block.gpsimd
        def _(pool):
            def causal(t):
                pool.memset(t[:, :], 0.0).then_inc(pool_order, 1)

            def causal_select(t):
                for c in (0, 2 * P):
                    last = pool.affine_select(out=t[:, c:c + P], in_=t[:, c:c + P], compare_op=ALU.is_ge,
                                              fill=NEG, base=0, pattern=[[-1, P]], channel_multiplier=1)
                return last

            pool.memset(ident[:, :], 0.0).then_inc(pool_order, 1)
            causal(FMm)
            pool.memset(U[:, :, 0:TAPS - 1], 0.0).then_inc(pool_order, 1)
            pool.memset(Um[:, :], 1.0).then_inc(pool_order, 1)
            pool.memset(Vm[:, :], 1.0).then_inc(pool_order, 1)
            pool.wait_ge(pool_order, 5)
            pool.affine_select(out=ident[:, :], in_=ident[:, :], compare_op=ALU.not_equal, fill=1.0, base=0,
                               pattern=[[-1, P]], channel_multiplier=1).then_inc(consts_ready, 1)
            causal_select(FMm).then_inc(consts_ready, 1)
            pool.affine_select(out=Um[:, :], in_=Um[:, :], compare_op=ALU.is_ge, fill=0.0, base=0,
                               pattern=[[1, P]], channel_multiplier=-1)
            pool.affine_select(out=Vm[:, :], in_=Vm[:, :], compare_op=ALU.is_gt, fill=0.0, base=0,
                               pattern=[[-1, P]], channel_multiplier=1).then_inc(consts_ready, 1)
            pool.dma_start(PR[0:48, :], conv_w[0].rearrange("j (i p) -> (j i) p", p=P)).then_inc(vec_landed, 16)
            pool.dma_start(PR[48:60, :], conv_b[0].rearrange("(i p) -> i p", p=P)).then_inc(vec_landed, 16)
            pool.dma_start(PR[60:61, :], g_q[0:1]).then_inc(vec_landed, 16)
            pool.dma_start(PR[61:62, :], g_k[0:1]).then_inc(vec_landed, 16)
            for c, n, v in ((0, 16, dt_bias), (16, 16, a_log), (32, 16, d_skip), (48, 64, g_kidx)):
                pool.dma_start(VB[:, c:c + n], v[0].unsqueeze(0).broadcast_to([P, n])).then_inc(vec_landed, 16)
            wait_full(pool, ("diag", 1, 1))
            pool.dma_start(GS[:, :], g_ssd[0].unsqueeze(0).broadcast_to([P, SSD_W])).then_inc(gs_landed, 16)
            pool.wait_ge(chunk_used, 4 * B_FOX)
            causal(FMf)
            pool.memset(Uf[:, :], 1.0).then_inc(pool_order, 1)
            pool.memset(ONE[:, :], 1.0).then_inc(pool_order, 1)
            pool.memset(OH[:, :], 0.0).then_inc(pool_order, 1)
            pool.wait_ge(pool_order, 9)
            causal_select(FMf)
            for k in range(3):
                pool.affine_select(out=OH[:, :], in_=OH[:, :], compare_op=ALU.not_equal, fill=1.0,
                                   base=-HEADS_F * k, pattern=[[-1, HEADS_F]], channel_multiplier=1)\
                    .then_inc(pool_order, 1)
                pool.wait_ge(pool_order, 10 + k)
            pool.affine_select(out=Uf[:, :], in_=Uf[:, :], compare_op=ALU.is_ge, fill=0.0, base=0,
                               pattern=[[1, P]], channel_multiplier=-1).then_inc(consts_ready, 1)
            pool.dma_start(FB[:, :], fox_b_f[0].unsqueeze(0).broadcast_to([P, HEADS_F])).then_inc(fb_landed, 16)
            pool.wait_ge(fb_landed, 16)

        @block.scalar
        def _(act):
            order = [0]

            def after(ins):
                order[0] += 1
                ins.then_inc(act_order, 1)
                act.wait_ge(act_order, order[0])

            def hi(b, j):
                act.wait_ge(raw_landed[j], landed(b, j))
                act.activation(wh[:, j, :, :], raw[:, j, :, :], ACT.Copy).then_inc(hi_ready, 1)

            def std(name_in, n_in, name_out, dst, src):
                act.wait_ge(name_in, n_in)
                act.activation(dst, src, ACT.Sqrt).then_inc(name_out, 1)

            def take_quarter(m, q):
                if m == 1:
                    act.wait_ge(chunk_used, 4 * (B_WOUT + DOWN - 1) + q + 1)
                for n in (2 * q, 2 * q + 1):
                    wait_full(act, ("xt", m, n))
                    act.activation(XH[:, 2 * n:2 * n + 2, :].rearrange("p k t -> p (k t)"),
                                   side_bank(("xt", m, n))[:, :], ACT.Copy).then_inc(xh_ready, 1)

            def root(m, n):
                std(var_ready, n, std_ready, rstd[:, m, :], rstd[:, m, :])

            def late_norm(m, b):
                hi(b, 0)
                if m == 1:
                    take_quarter(m, 2)
                hi(b, 1)
                squares(m - 1, 3)
                hi(b, 2)
                take_quarter(m, 3)

            def square_sums(which, q, src):
                act.wait_ge(ssq_ready, 4 * which + q + 1)
                after(act.activation(junk[:, :], src[0], ACT.Square, accum_out=ssq[:, 0, q:q + 1]))
                act.activation(junk[:, :], src[1], ACT.Square, accum_out=ssq[:, 1, q:q + 1]).then_inc(ssq_ready, 1)

            def squares(which, q):
                if which == 2:
                    act.wait_ge(chunk_used, 4 * (B_FOUT + q) + 4)
                    square_sums(which, q, [acc[(O_FOUT + q) % 2][t][:, :] for t in range(NT)])
                else:
                    act.wait_ge(sum_ready, 4 * (which - which // 3) + q + 1)
                    src = HB if which == 4 else X
                    square_sums(which, q, [src[:, t, 512 * q:512 * q + 512] for t in range(NT)])

            def attn_exp(a, h, L, st):
                act.wait_ge(step["logits_ready"], a * HEADS_A + h + 1)
                s0 = 4 * (h % 4)
                for t in range(NT):
                    ins = act.activation(L[:, h % L.shape[1], ctr(t)], L[:, h % L.shape[1], ctr(t)], ACT.Exp,
                                         bias=st[:, s0 + t:s0 + t + 1], accum_out=st[:, s0 + 2 + t:s0 + 3 + t])
                ins.then_inc(step["exp_ready"], 1)

            def attn_pt(a, h, PT):
                wait_full(act, ("PT", a, h))
                free(act.activation(PT[:, h, :], side_bank(("PT", a, h))[:, 0:3 * P], ACT.Copy), ("PT", a, h))

            def take(kind, o, n, b):
                if kind in ("xbc", "fq", "fk"):
                    return
                act.wait_ge(chunk_used, 4 * b + 4)
                if kind == "k":
                    act.wait_ge(step["conv_done"], 12)
                elif kind == "z" and n == 0:
                    wait_full(act, ("qkt", 5))
                src = acc[o % 2][1]
                rows_root = rstd[:, 0, 1:2]
                if kind == "qi":
                    dst, rows_root = QI[:, 4 * n + 2:4 * n + 4, :].rearrange("p f t -> p (f t)"), 1.0
                elif kind in ("k", "v"):
                    dst = {"k": K, "v": V}[kind][:, 1, :]
                elif kind in ("q", "z"):
                    dst = {"q": Q, "z": Z}[kind][:, 1, 512 * n:512 * n + 512]
                else:
                    dst, rows_root = FV[:, 1, 512 * n:512 * n + 512], rstd[:, 2, 1:2]
                if kind in ("k", "q", "z", "v", "fv"):
                    act.wait_ge(step["rs_ready"], 2 if kind == "fv" else 1)
                act.activation(dst, src[0:dst.shape[0], 0:dst.shape[1]], ACT.Copy, scale=rows_root)\
                   .then_inc(acc_freed[o % 2][1], 1)

            def mlp(b0, o0, u0, which):
                def relu(u, o_par, k, b):
                    if k == 0:
                        act.wait_ge(chunk_used, 4 * b + 4)
                    act.wait_ge(hl_ready, 2 * u + k + 1)
                    act.activation(RB[:, k, :], acc[o_par][k][:, :], ACT.Relu)\
                       .then_inc(acc_freed[o_par][k], 1)

                def high(u, k, tile):
                    act.wait_ge(sq_ready, 2 * u + k + 1)
                    act.activation(hh[:, tile, :], RB[:, k, :].rearrange("p (f t) -> p f t", f=2), ACT.Copy)\
                       .then_inc(hh_ready, 1)

                def hidden(j, u, o_par, b, tile0):
                    if j < 2:
                        relu(u, o_par, j, b)
                    if j in (1, 2):
                        k = j - 1
                        at = tile0 + 2 * k
                        high(u, k, slice(at, at + 2) if isinstance(at, int) else bass.ds(at, 2))

                for half in range(2):
                    b, o, u = b0 + half * B_HALF, o0 + half * O_HALF, u0 + half * UP
                    for j in range(2 if half else 3, 4):
                        hi(b, j)
                    with act.Fori(0, UP // 2 - 1) as i:
                        for s in (1, 2):
                            for j in range(4):
                                hi(b + 2 * i + s, j)
                                hidden(j, u + 2 * i + s - 1, (o + s - 1) % 2, b + 2 * i + s - 1,
                                       4 * (2 * i + s - 1))
                    for j in range(4):
                        hi(b + UP - 1, j)
                        hidden(j, u + UP - 2, (o + UP - 2) % 2, b + UP - 2, 4 * (UP - 2))
                    for n in range(DOWN):
                        for j in range(8):
                            hi(b + UP + 2 * n + j // 4, j % 4)
                            if n == 0 and j < 3:
                                hidden(j, u + UP - 1, (o + UP - 1) % 2, b + UP - 1, 4 * (UP - 1))
                            if which == 4 and half == 0 and n == 0 and 3 <= j < 7:
                                squares(3, j - 3)
                            if half == 1 and n > 0 and j == 3:
                                squares(which, n - 1)
                            if half == 1 and n > 0 and j == 5 and which == 1:
                                take_quarter(2, n - 1)
                    last = b + UP + 2 * DOWN
                    if half == 0:
                        hi(last, 0)
                        hi(last, 1)

            take_quarter(0, 0)
            hi(0, 0)
            take_quarter(0, 1)
            hi(0, 1)
            take_quarter(0, 2)
            hi(0, 2)
            take_quarter(0, 3)

            def first_squares(q):
                act.wait_ge(x_landed[q], 32)
                for t in range(NT):
                    ins = act.activation(junk[:, :], X[:, t, 512 * q:512 * q + 512], ACT.Square,
                                         accum_out=ssq[:, t, q:q + 1])
                    if t < NT - 1 or q < 3:
                        after(ins)
                if q == 3:
                    ins.then_inc(ssq_ready, 1)

            def dt_logs(T, asked, told):
                act.wait_ge(asked, 1)
                act.activation(T[:, 2, :], T[:, 1, :], ACT.Exp).then_inc(told, 1)
                act.wait_ge(asked, 2)
                act.activation(T[:, 4, :], T[:, 3, :], ACT.Ln).then_inc(told, 1)

            def narrow_hi(m):
                h, came, l = narrow[m]
                act.wait_ge(narrow_landed, 48 if m else 32)
                act.activation(h[:, :, :], came[:, :, :], ACT.Copy).then_inc(narrow_high, 1)

            def narrow_out(m):
                wait_full(act, ("narrow", m))
                dst = FTT if m else SMT
                free(act.activation(dst[:, :], side_bank(("narrow", m))[0:dst.shape[0], 0:TOK], ACT.Copy),
                     ("narrow", m))

            def conv_start(i):
                wait_emptied(act, "params")
                o = O_WIN + 2 + i // 4
                for t in range(NT):
                    act.wait_ge(acc_freed[o % 2][t], o // 2 + 1)
                act.wait_ge(consts_ready, 2)
                act.activation(XC[:, i, :], U[:, i, 0:TOK], ACT.Identity, scale=PC[:, i:i + 1],
                               bias=PC[:, 48 + i:49 + i]).then_inc(step["conv_start"], 1)

            def silu(n):
                act.wait_ge(step["conv_done"], 4 * n + 4)
                act.activation(XC[:, 4 * n:4 * n + 4, :], XC[:, 4 * n:4 * n + 4, :], ACT.Silu)\
                   .then_inc(step["silu_done"], 1)

            def decay(c, n):
                wait_full(act, ("seg", c, n))
                free(act.activation(E[:, 4 * n:4 * n + 4, :].rearrange("p h l -> p (h l)"),
                                    side_bank(("seg", c, n))[:, :], ACT.Exp), ("seg", c, n))

            def turned(n):
                wait_full(act, ("qkt", n))
                dst = QT[:, 2 * n:2 * n + 2, :] if n < 4 else KTt[:, 2 * n - 8:2 * n - 6, :]
                free(act.activation(dst.rearrange("p h t -> p (h t)"), side_bank(("qkt", n))[:, :], ACT.Copy,
                                    scale=PC[:, 60:61] if n < 4 else PC[:, 61:62]), ("qkt", n))

            def gate(g):
                for t in range(NT):
                    o = O_WIN + 8 + g
                    act.wait_ge(acc_freed[o % 2][t], o // 2 + 1)
                    act.activation(Z[:, t, 512 * g:512 * g + 512], Z[:, t, 512 * g:512 * g + 512], ACT.Silu)\
                       .then_inc(step["z_gated"], 1)

            def gated_squares(g):
                act.wait_ge(step["y_ready"], g + 1)
                for t in range(NT):
                    act.activation(junk[:, :], Y[:, t, 512 * g:512 * g + 512], ACT.Square,
                                   accum_out=SQS[:, 56 + 2 * t + g:57 + 2 * t + g]).then_inc(step["yss_ready"], 1)
                    act.wait_ge(step["yss_ready"], 2 * g + t + 1)

            def mix_side(n):
                if n in (3, 4):
                    first_squares(2 * n - 6)
                    first_squares(2 * n - 5)
                if n == 6:
                    root(0, 1)
                if n == 6:
                    narrow_hi(0)
                if n == 8:
                    narrow_out(0)
                if n == 10:
                    wait_full(act, ("rbc", 0))
                    free(act.activation(RCm[:, :], side_bank(("rbc", 0))[:, 0:TOK], ACT.Copy), ("rbc", 0))
                if n == 6:
                    wait_full(act, "params")
                    free(act.activation(PC[:, :], side_bank("params")[:, 0:62], ACT.Copy), "params")
                if n == 9:
                    std(step["ki_var"], 1, step["ki_std"], SQS[:, 2:4], SQS[:, 0:2])
                if n == 10:
                    act.activation(DTS[:, 8, 0:16], VB[:, 16:32], ACT.Exp).then_inc(step["dt_b"], 1)
                    dt_logs(DTS, step["dt_a"], step["dt_b"])
                if n == 11:
                    wait_full(act, "ki")
                    free(act.activation(KIT[:, :], side_bank("ki")[:, 0:TOK], ACT.Copy), "ki")
                if 13 <= n <= 18:
                    for g in (2 * n - 26, 2 * n - 25):
                        wait_full(act, ("score", g))
                        if g >= 2:
                            act.wait_ge(step["scores_used"], g - 1)
                        free(act.activation(R[:, g % 2, :], side_bank(("score", g))[:, :], ACT.Relu), ("score", g))
                        if g == 1:
                            for c in range(NT):
                                wait_full(act, ("cum", c))
                                free(act.activation(DTS[:, 9 if c else 8, :], side_bank(("cum", c))[:, 0:32],
                                                    ACT.Exp), ("cum", c))
                if 13 <= n <= 23:
                    conv_start(n - 13)
                if n == 23:
                    conv_start(11)
                if n in (19, 20):
                    decay(0, 2 * n - 38)
                    decay(0, 2 * n - 37)
                if n in (21, 22, 25):
                    silu({21: 0, 22: 1, 25: 2}[n])
                if n == 29:
                    wait_full(act, ("xst", 4))
                    free(act.activation(BM[:, :, :].rearrange("p t n -> p (t n)"), side_bank(("xst", 4))[:, :],
                                        ACT.Copy), ("xst", 4))
                if n == 33:
                    std(step["qk_var"], 1, step["qk_std"], SQS[:, 32:56], SQS[:, 8:32])
                if n == 34:
                    for g in range(GROUPS):
                        wait_full(act, ("state", g))
                        free(act.activation(ST[:, g, :], side_bank(("state", g))[:, :], ACT.Copy), ("state", g))
                if n in (34, 35):
                    decay(1, 2 * n - 68)
                    decay(1, 2 * n - 67)
                if n in (36, 37):
                    for k in range(3 * (n - 36), 3 * (n - 36) + 3):
                        turned(k)
                if n == 37:
                    gate(0)
                if n == 43:
                    gated_squares(1)
                    std(step["y_var"], 1, step["y_std"], SQS[:, 60:64], SQS[:, 60:64])
                for h in {39: (0, 1), 40: (2, 3), 41: (4, 5), 43: (6, 7)}.get(n, ()):
                    attn_exp(0, h, Lm, SQS[:, 64:80])
                for h in {41: (0, 1), 42: (2, 3)}.get(n, ()):
                    attn_pt(0, h, PTm)
                if n == 42:
                    gate(1)
                    gated_squares(0)
                if n == 43:
                    for h in (4, 5):
                        attn_pt(0, h, PTm)

            def fox_side(n):
                if n == 3:
                    root(2, 2)
                if n == 5:
                    narrow_hi(2)
                if n == 8:
                    narrow_out(2)
                if n == 9:
                    dt_logs(FS, step["f_a"], step["f_b"])
                if n == 15:
                    wait_full(act, "fct")
                    free(act.activation(NCT[:, :], side_bank("fct")[0:3 * HEADS_F, 0:TOK], ACT.Copy), "fct")
                if n >= 17 and n % 2 == 1:
                    attn_exp(1, (n - 17) // 2, Lf, FST)
                if n >= 19 and n % 2 == 1:
                    attn_pt(1, (n - 19) // 2, PTf)
                for h in range(12):
                    if n == FOX_O[h] + 2:
                        fox_out(h)
                if n == 47:
                    fox_high(0)
                    fox_high(1)

            def fox_out(h):
                wait_full(act, ("O", 1, h))
                free(act.activation(FQ[:, h, :], side_bank(("O", 1, h))[:, 0:TOK], ACT.Copy), ("O", 1, h))

            def fox_high(n):
                act.wait_ge(chunk_used, 4 * (B_FOUT - 1) + n // 2 + 1)
                for h in (2 * n, 2 * n + 1):
                    wait_emptied(act, ("O", 1, h))
                act.activation(XH[:, 2 * n:2 * n + 2, :], FQ[:, 2 * n:2 * n + 2, :], ACT.Copy).then_inc(xh_ready, 1)

            seen = {}
            prev = None
            for n, (kind, col) in enumerate(WIN):
                for j in range(4):
                    ahead(hi, B_WIN, 4 * n + j + 1)
                    if prev and j == (1 if prev[0] == "z" else 0):
                        take(*prev)
                    mix_side(4 * n + j)
                prev = (kind, O_WIN + n, seen.get(kind, 0), B_WIN + n)
                seen[kind] = seen.get(kind, 0) + 1
            def y_high(n):
                wait_full(act, ("yt", n))
                act.activation(XH[:, 2 * n:2 * n + 2, :].rearrange("p k t -> p (k t)"),
                               side_bank(("yt", n))[:, :], ACT.Copy).then_inc(xh_ready, 1)

            def o_high(h):
                wait_full(act, ("O", 0, h))
                act.activation(XH[:, 8 + h, :], side_bank(("O", 0, h))[:, 0:TOK], ACT.Copy)\
                   .then_inc(step["oh_ready"], 1)

            y_high(0)
            y_high(1)
            take(*prev)
            hi(B_WOUT, 1)
            y_high(2)
            y_high(3)
            for h in (6, 7):
                attn_pt(0, h, PTm)
            for n in range(DOWN):
                for j in range(4):
                    if n or j >= 2:
                        hi(B_WOUT + n, j)
                    if n == 0 and j >= 2:
                        for h in range(4 * j - 8, 4 * j - 4):
                            o_high(h)
                    if n and j == 2:
                        squares(0, n - 1)
                    if n == DOWN - 1 and j >= 2:
                        take_quarter(1, j - 2)
            late_norm(1, B_M1)
            mlp(B_M1, O_M1, 0, 1)
            late_norm(2, B_FOX)
            seen = {}
            prev = None
            for n, (kind, col) in enumerate(FOX):
                for j in range(4):
                    ahead(hi, B_FOX, 4 * n + j + 1)
                    if j == 0 and prev:
                        take(*prev)
                    fox_side(4 * n + j)
                prev = (kind, O_FOX + n, seen.get(kind, 0), B_FOX + n)
                seen[kind] = seen.get(kind, 0) + 1
            take(*prev)
            attn_pt(1, 15, PTf)
            for h in (9, 10, 11):
                fox_out(h)
            hi(B_FOUT, 1)
            for n in range(2, 6):
                fox_high(n)
            for n in range(DOWN):
                for j in range(4):
                    if n or j >= 2:
                        hi(B_FOUT + n, j)
                    if n == 0 and j >= 2:
                        for h in (2 * j + 8, 2 * j + 9):
                            fox_out(h)
                        fox_high(j + 4)
                    if n and j == 1:
                        squares(2, n - 1)
            hi(B_M2, 0)
            squares(2, 3)
            root(4, 3)
            take_quarter(3, 0)
            hi(B_M2, 1)
            take_quarter(3, 1)
            take_quarter(3, 2)
            hi(B_M2, 2)
            take_quarter(3, 3)
            mlp(B_M2, O_M2, 2 * UP, 4)
            squares(4, 3)
            root(5, 4)

        @block.vector
        def _(dve):
            order = [0]

            def after(ins):
                order[0] += 1
                ins.then_inc(dve_order, 1)
                dve.wait_ge(dve_order, order[0])

            def lo(b, j):
                dve.wait_ge(hi_ready, 4 * b + j + 1)
                dve.tensor_tensor(wl[:, j, :, :], raw[:, j, :, :], wh[:, j, :, :].bitcast(F32), ALU.subtract)\
                   .then_inc(lo_ready, 1)

            def low_xt(name, n, sem_n):
                dve.wait_ge(xh_ready, sem_n)
                bk = side_bank(name)[:, :]
                dst = slice(2 * n, 2 * n + 2)
                ins = dve.tensor_tensor(XL[:, dst, :].rearrange("p k t -> p (k t)"), bk,
                                        XH[:, dst, :].bitcast(F32).rearrange("p k t -> p (k t)"), ALU.subtract)
                free(ins, name)

            def mean_square(m, n_ssq):
                dve.wait_ge(ssq_ready, n_ssq)
                after(dve.tensor_reduce(rstd[:, m, :], ssq[:, :, :], AX, ALU.add))
                return dve.tensor_scalar(rstd[:, m, :], rstd[:, m, :], 1.0 / D, EPS, ALU.mult, ALU.add)

            def inverse_square(m, n_ssq):
                after(mean_square(m, n_ssq))
                after(dve.reciprocal(rstd[:, m, :], rstd[:, m, :]))

            def inverse_root(m, n):
                dve.wait_ge(std_ready, n)
                dve.reciprocal(rstd[:, m, :], rstd[:, m, :]).then_inc(step["rs_ready"], 1)
                dve.wait_ge(step["rs_ready"], n)

            def gained(m, q):
                cols = slice(512 * q, 512 * q + 512)
                for t in range(NT):
                    ins = dve.tensor_tensor((HB if m else XN0)[:, t, cols], X[:, t, cols], G[:, cols], ALU.mult)
                ins.then_inc(xn_ready, 1)

            def low_quarter(m, q):
                for n in (2 * q, 2 * q + 1):
                    low_xt(("xt", m, n), n, (0, 12, 20, 36)[m] + n + 1)

            def late_norm(m, b, o):
                lo(b, 0)
                if m == 1:
                    low_quarter(m, 2)
                add_panel(o, b - 1, 3, X, rstd[:, 1, :] if m == 2 else None)
                summed(o)
                lo(b, 1)
                dve.wait_ge(g_landed, 16 * m)
                gained(m, 3)
                lo(b, 2)
                low_quarter(m, 3)
                if m == 1:
                    inverse_square(1, 5)
                else:
                    mean_square(2, 9).then_inc(var_ready, 1)

            def log1p_exp(T, ready, done, n0):
                dve.wait_ge(done, n0 + 1)
                dve.tensor_scalar(T[:, 3, :], T[:, 2, :], 1.0, None, ALU.add).then_inc(ready, 1)
                dve.wait_ge(ready, 2)
                after(dve.tensor_scalar(T[:, 5, :], T[:, 3, :], -1.0, None, ALU.add))
                after(dve.tensor_scalar(T[:, 6, :], T[:, 5, :], 0.0, None, ALU.is_equal))
                after(dve.tensor_tensor(T[:, 5, :], T[:, 5, :], T[:, 6, :], ALU.add))
                after(dve.reciprocal(T[:, 5, :], T[:, 5, :]))
                after(dve.tensor_tensor(T[:, 5, :], T[:, 5, :], T[:, 2, :], ALU.mult))
                dve.wait_ge(done, n0 + 2)
                after(dve.tensor_tensor(T[:, 5, :], T[:, 5, :], T[:, 4, :], ALU.mult))
                after(dve.tensor_tensor(T[:, 6, :], T[:, 6, :], T[:, 2, :], ALU.mult))
                after(dve.tensor_tensor(T[:, 6, :], T[:, 6, :], T[:, 5, :], ALU.add))

            def add_panel(o, b, q, dst, scale=None, first=False):
                dve.wait_ge(chunk_used, 4 * b + 4)
                cols = slice(512 * q, 512 * q + 512)
                for t in range(NT):
                    src = acc[o % 2][t][:, :]
                    if first:
                        ins = dve.tensor_scalar(dst[:, t, cols], src, scale[:, t:t + 1], None, ALU.mult)
                    elif scale is not None:
                        ins = dve.scalar_tensor_tensor(out=dst[:, t, cols], in0=src, scalar=scale[:, t:t + 1],
                                                       in1=dst[:, t, cols], op0=ALU.mult, op1=ALU.add)
                    else:
                        ins = dve.tensor_tensor(dst[:, t, cols], src, dst[:, t, cols], ALU.add)
                    ins.then_inc(acc_freed[o % 2][t], 1)

            def take(kind, o, n, b):
                dve.wait_ge(chunk_used, 4 * b + 4)
                if kind == "z" and n == 0:
                    wait_full(dve, ("qkt", 5))
                src = acc[o % 2][0]
                if kind == "qi":
                    dst = QI[:, 4 * n:4 * n + 2, :].rearrange("p f t -> p (f t)")
                elif kind in ("k", "v"):
                    dst = {"k": K, "v": V}[kind][:, 0, :]
                elif kind in ("q", "z"):
                    dst = {"q": Q, "z": Z}[kind][:, 0, 512 * n:512 * n + 512]
                elif kind == "fv":
                    dst = FV[:, 0, 512 * n:512 * n + 512]
                if kind in ("xbc", "fq", "fk"):
                    if kind == "xbc":
                        wait_emptied(dve, ("rbc", 0))
                    along = RCm if kind == "xbc" else RCf
                    for k in range(2):
                        f = slice(4 * n + 2 * k, 4 * n + 2 * k + 2)
                        dst = U[:, f, TAPS - 1:] if kind == "xbc" else {"fq": FQ, "fk": FK}[kind][:, f, :]
                        src = acc[o % 2][k][:, :].rearrange("p (f t) -> p f t", f=2)
                        dve.scalar_tensor_tensor(out=dst, in0=src, scalar=SCALE if kind == "fq" else 1.0,
                                                 in1=along[:, :].unsqueeze(1).broadcast_to([P, 2, TOK]),
                                                 op0=ALU.mult, op1=ALU.mult).then_inc(acc_freed[o % 2][k], 1)
                elif kind == "qi":
                    dve.tensor_copy(dst, src[:, :]).then_inc(acc_freed[o % 2][0], 1)
                else:
                    c = rstd[:, 2 if kind == "fv" else 0, 0:1]
                    dve.tensor_scalar(dst, src[:, 0:dst.shape[1]], c, None, ALU.mult)\
                       .then_inc(acc_freed[o % 2][0], 1)

            def attn_logits(a, h, L, M, st):
                if h >= L.shape[1]:
                    wait_full(dve, ("PT", a, h - L.shape[1]))
                wait_full(dve, ("S", a, h))
                bk, s0 = side_bank(("S", a, h)), 4 * (h % 4)
                for t in range(NT):
                    ins = dve.tensor_tensor_reduce(L[:, h % L.shape[1], ctr(t)], bk[:, ctr(t)], M[:, ctr(t)], 1.0,
                                                   -3e38, ALU.add, ALU.max, st[:, s0 + t:s0 + t + 1])
                free(ins, ("S", a, h))
                dve.wait_ge(side_free[uses[("S", a, h)][0]], uses[("S", a, h)][1] + 1)
                dve.tensor_scalar(st[:, s0:s0 + 2], st[:, s0:s0 + 2], -1.0, None, ALU.mult)\
                   .then_inc(step["logits_ready"], 1)

            def attn_probs(a, h, L, st):
                s0 = 4 * (h % 4)
                dve.wait_ge(step["exp_ready"], a * HEADS_A + h + 1)
                after(dve.reciprocal(st[:, s0 + 2:s0 + 4], st[:, s0 + 2:s0 + 4]))
                for t in range(NT):
                    ins = dve.tensor_scalar(L[:, h % L.shape[1], ctr(t)], L[:, h % L.shape[1], ctr(t)],
                                            st[:, s0 + 2 + t:s0 + 3 + t], None, ALU.mult)
                ins.then_inc(step["probs_ready"], 1)

            def attn_low(h):
                dve.wait_ge(step["oh_ready"], h + 1)
                ins = dve.tensor_tensor(XL[:, 8 + h, :], side_bank(("O", 0, h))[:, 0:TOK],
                                        XH[:, 8 + h, :].bitcast(F32), ALU.subtract)
                free(ins, ("O", 0, h))

            def mlp(b0, o0, u0, dst, m):
                scale = rstd[:, m, :]
                def square(o_par, n, k):
                    dve.wait_ge(acc_freed[o_par][k], n)
                    dve.tensor_tensor(RB[:, k, :], RB[:, k, :], RB[:, k, :], ALU.mult).then_inc(sq_ready, 1)

                def low(u, k, tile):
                    dve.wait_ge(hh_ready, 2 * u + k + 1)
                    dve.tensor_tensor(hl[:, tile, :], RB[:, k, :].rearrange("p (f t) -> p f t", f=2),
                                      hh[:, tile, :].bitcast(F32), ALU.subtract).then_inc(hl_ready, 1)

                def hidden(j, u, o_par, n, tile0):
                    if j < 2:
                        square(o_par, n, j)
                    if j in (2, 3):
                        k = j - 2
                        at = tile0 + 2 * k
                        low(u, k, slice(at, at + 2) if isinstance(at, int) else bass.ds(at, 2))

                for half in range(2):
                    b, o, u = b0 + half * B_HALF, o0 + half * O_HALF, u0 + half * UP
                    for j in range(2 if half else 3, 4):
                        lo(b, j)
                    with dve.Fori(0, UP // 2 - 1) as i:
                        for s in (1, 2):
                            for j in range(4):
                                lo(b + 2 * i + s, j)
                                hidden(j, u + 2 * i + s - 1, (o + s - 1) % 2, i + (o + s - 1) // 2 + 1,
                                       4 * (2 * i + s - 1))
                    for j in range(4):
                        lo(b + UP - 1, j)
                        if m == 3 and half == 0:
                            fox_added(j)
                        hidden(j, u + UP - 2, (o + UP - 2) % 2, (o + UP - 2) // 2 + 1, 4 * (UP - 2))
                    for n in range(DOWN):
                        for j in range(8):
                            lo(b + UP + 2 * n + j // 4, j % 4)
                            if n == 0 and j < 4:
                                hidden(j, u + UP - 1, (o + UP - 1) % 2, (o + UP - 1) // 2 + 1,
                                       4 * (UP - 1))
                            if n > 0 and j == 1:
                                add_panel(o + UP + n - 1, b + UP + 2 * n - 1, n - 1, dst, scale,
                                          m == 3 and half == 0)
                                if half == 1:
                                    summed(o + UP + n - 1)
                            if half == 1 and n > 0 and m == 1:
                                if j == 2:
                                    dve.wait_ge(g_landed, 16 * 2)
                                    gained(2, n - 1)
                                if j == 5:
                                    low_quarter(2, n - 1)
                            if half == 1 and n > 0 and m == 3 and j == 5:
                                last_gain(n - 1)
                            if half == 0 and n == 0 and m == 3 and j == 7:
                                inverse_square(3, 17)
                    last = b + UP + 2 * DOWN
                    if half == 0:
                        lo(last, 0)
                        lo(last, 1)
                        add_panel(o + UP + DOWN - 1, last - 1, DOWN - 1, dst, scale, m == 3)

            def summed(o):
                for t in range(NT):
                    dve.wait_ge(acc_freed[o % 2][t], o // 2 + 1)
                dve.engine_nop().then_inc(sum_ready, 1)

            def narrow_lo(m):
                h, came, l = narrow[m]
                dve.wait_ge(narrow_high, m // 2 + 1)
                dve.tensor_tensor(l[:, :, :], came[:, :, :], h[:, :, :].bitcast(F32), ALU.subtract)\
                   .then_inc(narrow_low, 1)

            def narrow_rows(m):
                wait_full(dve, ("narrow_rows", m))
                w = FTT.shape[0] if m else SMT.shape[0]
                for t in range(NT):
                    dst = FS[:, 0, t * w:(t + 1) * w] if m else SM[:, t, :]
                    ins = dve.tensor_scalar(dst, side_bank(("narrow_rows", m))[:, t * w:(t + 1) * w],
                                            rstd[:, m, t:t + 1], None, ALU.mult)
                free(ins, ("narrow_rows", m))
                wait_emptied(dve, ("narrow_rows", m))

            def index_keys():
                narrow_rows(0)
                dve.wait_ge(vec_landed, 16 * 8)
                for t in range(NT):
                    after(dve.tensor_tensor_reduce(KI2[:, t, 0:HD_I], SM[:, t, 0:HD_I], SM[:, t, 0:HD_I], 1.0, 0.0,
                                                   ALU.mult, ALU.add, SQS[:, t:t + 1]))
                dve.tensor_scalar(SQS[:, 0:2], SQS[:, 0:2], 1.0 / HD_I, EPS, ALU.mult, ALU.add)\
                   .then_inc(step["ki_var"], 1)
                for t in range(NT):
                    w_i = SM[:, t, HD_I:W_KW]
                    after(dve.tensor_scalar(w_i, w_i, rstd[:, 0, t:t + 1], HEADS_I ** -0.5 * HD_I ** -0.5,
                                            ALU.mult, ALU.mult))
                dve.wait_ge(step["ki_std"], 1)
                after(dve.reciprocal(SQS[:, 2:4], SQS[:, 2:4]))
                for t in range(NT):
                    for k in range(2):
                        dve.scalar_tensor_tensor(out=KI2[:, t, HD_I * k:HD_I * (k + 1)], in0=SM[:, t, 0:HD_I],
                                                 scalar=SQS[:, 2 + t:3 + t], in1=VB[:, 48:48 + HD_I],
                                                 op0=ALU.mult, op1=ALU.mult).then_inc(step["ki_rows"], 1)

            def step_sizes():
                T = DTS
                v = T[:, 0, :].rearrange("p (t h) -> p t h", t=NT)
                after(dve.tensor_tensor(v, SM[:, :, W_KW:], VB[:, 0:16].unsqueeze(1).broadcast_to([P, NT, HEADS_S]),
                                        ALU.add))
                dve.scalar_tensor_tensor(out=T[:, 1, :], in0=T[:, 0, :], scalar=-1.0, in1=T[:, 0, :],
                                         op0=ALU.mult, op1=ALU.min).then_inc(step["dt_a"], 1)
                log1p_exp(T, step["dt_a"], step["dt_b"], 1)
                after(dve.scalar_tensor_tensor(out=T[:, 6, :], in0=T[:, 0, :], scalar=0.0, in1=T[:, 6, :],
                                               op0=ALU.max, op1=ALU.add))
                dve.scalar_tensor_tensor(out=T[:, 7, :].rearrange("p (t h) -> p t h", t=NT),
                                         in0=T[:, 6, :].rearrange("p (t h) -> p t h", t=NT), scalar=-1.0,
                                         in1=T[:, 8, 0:16].unsqueeze(1).broadcast_to([P, NT, HEADS_S]),
                                         op0=ALU.mult, op1=ALU.mult).then_inc(step["adt_ready"], 1)

            def score_add(g):
                t, per, hs = score_heads(g)
                wait_emptied(dve, ("score", g))
                for i in range(per):
                    h, width = hs[i], P * (t + 1)
                    src, w = R[:, g % 2, width * i:width * (i + 1)], SM[:, t, HD_I + h:HD_I + h + 1]
                    if h == 0:
                        ins = dve.tensor_scalar(SC[:, ctr(t)], src, w, None, ALU.mult)
                    else:
                        ins = dve.scalar_tensor_tensor(out=SC[:, ctr(t)], in0=src, scalar=w, in1=SC[:, ctr(t)],
                                                       op0=ALU.mult, op1=ALU.add)
                    if i < per - 1:
                        after(ins)
                ins.then_inc(step["scores_used"], 1)
                dve.wait_ge(step["scores_used"], g + 1)

            def top(t, r0, r1):
                width = P * (t + 1)
                s = SC[:, ctr(t)]
                if r0 == 0:
                    dve.wait_ge(consts_ready, 2)
                    after(dve.tensor_tensor(s, s, FMm[:, ctr(t)], ALU.add))
                for r in range(r0, r1):
                    after(dve.max(M8[:, :], s if r == 0 else WK[:, 0:width]))
                    if r < TOPK // 8 - 1:
                        after(dve.match_replace(WK[:, 0:width], M8[:, :], s if r == 0 else WK[:, 0:width], -3e38))

            def select(t):
                width = P * (t + 1)
                s = SC[:, ctr(t)]
                kth = M8[:, 7:8]
                after(dve.tensor_scalar(GT[:, 0:width], s, kth, None, ALU.is_gt, ALU.add, accum_out=SQS[:, 4:5]))
                after(dve.tensor_scalar(EQ[:, 0:width], s, kth, None, ALU.is_equal))
                after(dve.tensor_scalar(SQS[:, 4:5], SQS[:, 4:5], -1.0, float(TOPK), ALU.mult, ALU.add))
                after(dve.tensor_tensor_scan(CS[:, 0:width], EQ[:, 0:width], EQ[:, 0:width], 0.0,
                                             ALU.add, ALU.max))
                after(dve.scalar_tensor_tensor(out=EQ[:, 0:width], in0=CS[:, 0:width], scalar=SQS[:, 4:5],
                                               in1=EQ[:, 0:width], op0=ALU.is_le, op1=ALU.mult))
                after(dve.tensor_tensor(GT[:, 0:width], GT[:, 0:width], EQ[:, 0:width], ALU.add))
                after(dve.tensor_scalar(GT[:, 0:width], GT[:, 0:width], -1.0, -NEG, ALU.add, ALU.mult))
                after(dve.tensor_tensor(MK[:, ctr(t)], GT[:, 0:width], FMm[:, ctr(t)], ALU.add))

            def head_squares(src, half, at, o):
                for t in range(NT):
                    dve.wait_ge(acc_freed[o % 2][t], o // 2 + 1)
                    sq = QI[:, 2 * t:2 * t + 2, :].rearrange("p h t -> p (h t)")
                    v = src[:, t, 512 * half:512 * half + 512]
                    after(dve.tensor_tensor(sq, v, v, ALU.mult))
                    after(dve.tensor_reduce(SQS[:, at + 4 * t:at + 4 * t + 4], heads(sq, HD), AX, ALU.add))

            def qk_norm():
                dve.wait_ge(step["qk_std"], 1)
                after(dve.reciprocal(SQS[:, 32:56], SQS[:, 32:56]))
                after(dve.tensor_scalar(SQS[:, 32:48], SQS[:, 32:48], SCALE, None, ALU.mult))
                for src, half, at in ((Q, 0, 32), (Q, 1, 40), (K, 0, 48)):
                    for t in range(NT):
                        v = heads(src[:, t, 512 * half:512 * half + 512], HD)
                        dve.tensor_tensor(v, v, bc(SQS[:, at + 4 * t:at + 4 * t + 4], HD), ALU.mult)\
                           .then_inc(step["qk_normed"], 1)

            def conv_rest(i):
                dve.wait_ge(step["conv_start"], i + 1)
                for j in range(1, TAPS):
                    ins = dve.scalar_tensor_tensor(out=XC[:, i, :], in0=U[:, i, j:j + TOK],
                                                   scalar=PC[:, 12 * j + i:12 * j + i + 1], in1=XC[:, i, :],
                                                   op0=ALU.mult, op1=ALU.add)
                    if j < TAPS - 1:
                        after(ins)
                ins.then_inc(step["conv_done"], 1)

            def decay_in(c):
                if c:
                    wait_full(dve, ("diag", 0, 1))
                else:
                    dve.wait_ge(step["adt_ready"], 1)
                    dve.wait_ge(consts_ready, 3)
                dve.tensor_tensor(E[:, :, :], Um[:, :].unsqueeze(1).broadcast_to([P, HEADS_S, P]),
                                  bc(DTS[:, 7, 16 * c:16 * c + 16], P), ALU.mult).then_inc(step["decay_in"], 1)

            def inputs(c):
                for half in range(2):
                    wait_full(dve, ("xst", 2 * c + half))
                    src = heads(side_bank(("xst", 2 * c + half))[:, :], HD_S)
                    cols, h0 = slice(512 * half, 512 * half + 512), HPG * half
                    dve.tensor_tensor(heads(Y[:, c, cols], HD_S), src, bc(VB[:, 32 + h0:32 + h0 + HPG], HD_S),
                                      ALU.mult).then_inc(step["skip_ready"], 1)
                    free(dve.tensor_tensor(heads(XD[:, c, cols], HD_S), src,
                                           bc(DTS[:, 6, 16 * c + h0:16 * c + h0 + HPG], HD_S), ALU.mult),
                         ("xst", 2 * c + half))

            def maps():
                wait_full(dve, "cb")
                free(dve.tensor_tensor(CB[:, :, :], side_bank("cb")[:, :].rearrange("p (g l) -> p g l", l=P),
                                       Um[:, :].unsqueeze(1).broadcast_to([P, NT * GROUPS, P]), ALU.mult), "cb")

            def decayed(c):
                for g in range(GROUPS):
                    for n in (2 * g, 2 * g + 1):
                        wait_emptied(dve, ("seg", c, n))
                    if g == 0 and c == 0:
                        wait_emptied(dve, "cb")
                    eg = E[:, HPG * g:HPG * (g + 1), :]
                    dve.tensor_tensor(eg, eg, CB[:, GROUPS * c + g, :].unsqueeze(1).broadcast_to([P, HPG, P]),
                                      ALU.mult).then_inc(step["m_ready"], 1)

            def state_in():
                wait_emptied(dve, ("cum", 0))
                for half in range(2):
                    wait_emptied(dve, ("xst", half))
                dve.tensor_tensor(heads(XDD[:, :], HD_S), heads(XD[:, 0, :], HD_S),
                                  bc(DTS[:, 8, 16:32], HD_S), ALU.mult).then_inc(step["st_ready"], 1)

            def own_part(c):
                dve.wait_ge(step["skip_ready"], 2 * c + 2)
                for g in range(GROUPS):
                    yg = Y[:, c, 512 * g:512 * g + 512]
                    wait_full(dve, ("diag", c, g))
                    free(dve.tensor_tensor(yg, side_bank(("diag", c, g))[:, :], yg, ALU.add), ("diag", c, g))

            def state_part():
                wait_emptied(dve, ("cum", 1))
                for g in range(GROUPS):
                    yg, tmp = Y[:, 1, 512 * g:512 * g + 512], XD[:, 0, 512 * g:512 * g + 512]
                    wait_emptied(dve, ("diag", 1, g))
                    wait_full(dve, ("off", g))
                    free(dve.tensor_tensor(heads(tmp, HD_S), heads(side_bank(("off", g))[:, :], HD_S),
                                           bc(DTS[:, 9, HPG * g:HPG * (g + 1)], HD_S), ALU.mult), ("off", g))
                    wait_emptied(dve, ("off", g))
                    after(dve.tensor_tensor(yg, yg, tmp, ALU.add))

            def gated(g):
                cols = slice(512 * g, 512 * g + 512)
                dve.wait_ge(step["z_gated"], 2 * g + 2)
                wait_emptied(dve, ("diag", 0, g))
                after(dve.tensor_tensor(Y[:, 0, cols], Y[:, 0, cols], Z[:, 0, cols], ALU.mult))
                dve.tensor_tensor(Y[:, 1, cols], Y[:, 1, cols], Z[:, 1, cols], ALU.mult)\
                   .then_inc(step["y_ready"], 1)

            def gated_norm(g):
                for t in range(NT):
                    cols = slice(512 * g, 512 * g + 512)
                    dve.scalar_tensor_tensor(out=Y[:, t, cols], in0=Y[:, t, cols],
                                             scalar=SQS[:, 60 + 2 * t + g:61 + 2 * t + g], in1=GS[:, cols],
                                             op0=ALU.mult, op1=ALU.mult).then_inc(step["yn_ready"], 1)

            def mix_side(n):
                st = SQS[:, 64:80]
                if n == 5:
                    mean_square(0, 1).then_inc(var_ready, 1)
                if n == 7:
                    inverse_root(0, 1)
                if n == 7:
                    narrow_lo(0)
                if n == 9:
                    index_keys()
                if n == 10:
                    step_sizes()
                if n == 11:
                    decay_in(0)
                if 13 <= n <= 18:
                    score_add(2 * n - 26)
                    score_add(2 * n - 25)
                if 13 <= n <= 23:
                    conv_rest(n - 13)
                if n == 23:
                    conv_rest(11)
                if n in (19, 20):
                    top(0, 4 * (n - 19), 4 * (n - 18))
                if n == 21:
                    select(0)
                if 22 <= n <= 25:
                    top(1, 2 * (n - 22), 2 * (n - 21))
                if n == 26:
                    select(1)
                if n == 26:
                    head_squares(K, 0, 24, O_WIN + 5)
                if n in (27, 28):
                    inputs(n - 27)
                if n == 29:
                    head_squares(Q, 0, 8, O_WIN + 6)
                if n == 30:
                    maps()
                    decayed(0)
                if n == 31:
                    state_in()
                if n == 32:
                    own_part(0)
                    decay_in(1)
                if n == 33:
                    head_squares(Q, 1, 16, O_WIN + 7)
                    dve.tensor_scalar(SQS[:, 8:32], SQS[:, 8:32], 1.0 / HD, EPS, ALU.mult, ALU.add)\
                       .then_inc(step["qk_var"], 1)
                if n == 34:
                    qk_norm()
                if n == 36:
                    decayed(1)
                if n == 38:
                    own_part(1)
                if n == 39:
                    state_part()
                if n in (40, 42):
                    gated((n - 40) // 2)
                if n == 43:
                    dve.wait_ge(step["yss_ready"], 4)
                    dve.tensor_scalar(SQS[:, 60:64], SQS[:, 56:60], 2.0 / SSD_W, EPS, ALU.mult, ALU.add)\
                       .then_inc(step["y_var"], 1)
                for h in {39: (0, 1), 40: (2, 3), 41: (4, 5), 43: (6, 7)}.get(n, ()):
                    attn_logits(0, h, Lm, MK, st)
                for h in {40: (0, 1), 41: (2, 3), 42: (4, 5)}.get(n, ()):
                    attn_probs(0, h, Lm, st)

            def fox_logs():
                narrow_rows(2)
                dve.wait_ge(fb_landed, 16)
                T = FS
                v = T[:, 0, :].rearrange("p (t h) -> p t h", t=NT)
                after(dve.tensor_tensor(v, v, FB[:, :].unsqueeze(1).broadcast_to([P, NT, HEADS_F]), ALU.add))
                dve.scalar_tensor_tensor(out=T[:, 1, :], in0=T[:, 0, :], scalar=-1.0, in1=T[:, 0, :],
                                         op0=ALU.mult, op1=ALU.min).then_inc(step["f_a"], 1)
                log1p_exp(T, step["f_a"], step["f_b"], 0)
                after(dve.tensor_scalar(T[:, 5, :], T[:, 0, :], 0.0, None, ALU.min))
                dve.tensor_tensor(T[:, 7, :], T[:, 6, :], T[:, 5, :], ALU.subtract).then_inc(step["lf_ready"], 1)

            def fox_parts():
                wait_full(dve, "fcum")
                src = side_bank("fcum")[:, 0:32].rearrange("p (t h) -> p t h", t=NT)
                p0, p1, p2 = (NC[:, :, HEADS_F * k:HEADS_F * (k + 1)] for k in range(3))
                after(dve.tensor_copy(NCB[:, :, :], src))
                after(dve.tensor_copy(p0, NCB[:, :, :]))
                free(dve.tensor_tensor(p2, src, p0, ALU.subtract), "fcum")
                wait_emptied(dve, "fcum")
                after(dve.tensor_copy(NCB[:, :, :], p2))
                after(dve.tensor_copy(p1, NCB[:, :, :]))
                dve.tensor_tensor(p2, p2, p1, ALU.subtract).then_inc(step["nc_ready"], 1)

            def columns_factor():
                wait_full(dve, ("rbc", 2))
                free(dve.tensor_copy(RCf[:, :], side_bank(("rbc", 2))[:, 0:TOK]), ("rbc", 2))
                wait_emptied(dve, ("rbc", 2))

            def fox_low(n):
                dve.wait_ge(xh_ready, 28 + n + 1)
                pair = slice(2 * n, 2 * n + 2)
                dve.tensor_tensor(XL[:, pair, :], FQ[:, pair, :], XH[:, pair, :].bitcast(F32), ALU.subtract)\
                   .then_inc(step["fl_ready"], 1)

            def fox_side(n):
                if n == 3:
                    inverse_root(2, 2)
                if n == 6:
                    narrow_lo(2)
                if n == 9:
                    fox_logs()
                if n == 12:
                    fox_parts()
                if n == 16:
                    dve.wait_ge(consts_ready, 4)
                if n >= 17 and n % 2 == 1:
                    attn_logits(1, (n - 17) // 2, Lf, FMf, FST)
                if n >= 18 and n % 2 == 0:
                    attn_probs(1, (n - 18) // 2, Lf, FST)
                if n == 47:
                    fox_low(0)
                    fox_low(1)

            def first_quarter(q):
                dve.wait_ge(x_landed[q], 32)
                gained(0, q)

            first_quarter(0)
            low_quarter(0, 0)
            lo(0, 0)
            first_quarter(1)
            low_quarter(0, 1)
            first_quarter(2)
            lo(0, 1)
            first_quarter(3)
            low_quarter(0, 2)
            lo(0, 2)
            low_quarter(0, 3)
            seen = {}
            prev = None
            for n, (kind, col) in enumerate(WIN):
                for j in range(4):
                    ahead(lo, B_WIN, 4 * n + j + 1)
                    if prev and j == (1 if prev[0] == "z" else 0):
                        take(*prev)
                    mix_side(4 * n + j)
                prev = (kind, O_WIN + n, seen.get(kind, 0), B_WIN + n)
                seen[kind] = seen.get(kind, 0) + 1
            dve.wait_ge(step["y_std"], 1)
            after(dve.reciprocal(SQS[:, 60:64], SQS[:, 60:64]))
            dve.wait_ge(gs_landed, 16)
            gated_norm(0)
            gated_norm(1)
            for h in (6, 7):
                attn_probs(0, h, Lm, SQS[:, 64:80])
            low_xt(("yt", 0), 0, 9)
            low_xt(("yt", 1), 1, 10)
            take(*prev)
            lo(B_WOUT, 1)
            low_xt(("yt", 2), 2, 11)
            low_xt(("yt", 3), 3, 12)
            for n in range(DOWN):
                for j in range(4):
                    if n or j >= 2:
                        lo(B_WOUT + n, j)
                    if n == 0 and j >= 2:
                        for h in range(4 * j - 8, 4 * j - 4):
                            attn_low(h)
                    if n and j == 1:
                        add_panel(O_WOUT + n - 1, B_WOUT + n - 1, n - 1, X)
                        summed(O_WOUT + n - 1)
                    if n and j == 2:
                        dve.wait_ge(g_landed, 16)
                        gained(1, n - 1)
                    if n == DOWN - 1 and j >= 2:
                        low_quarter(1, j - 2)
            late_norm(1, B_M1, O_WOUT + 3)
            for k in range(2):
                dve.memset(RB[:, k, :], 0.0).then_inc(hl_ready, 1)
            mlp(B_M1, O_M1, 0, X, 1)
            late_norm(2, B_FOX, O_FOX - 1)
            seen = {}
            prev = None
            for n, (kind, col) in enumerate(FOX):
                for j in range(4):
                    ahead(lo, B_FOX, 4 * n + j + 1)
                    if n == 1 and j == 0:
                        columns_factor()
                    fox_side(4 * n + j)
                    if j == 0 and prev:
                        take(*prev)
                prev = (kind, O_FOX + n, seen.get(kind, 0), B_FOX + n)
                seen[kind] = seen.get(kind, 0) + 1
            def fox_panel(q):
                cols, o = slice(512 * q, 512 * q + 512), O_FOUT + q
                dve.wait_ge(ssq_ready, 10 + q)
                if q == 0:
                    dve.wait_ge(g1_landed, 16)
                    dve.wait_ge(g_landed, 16 * 3)
                for t in range(NT):
                    dve.tensor_tensor(HB[:, t, cols], acc[o % 2][t][:, :], G1[:, cols], ALU.mult)\
                       .then_inc(acc_freed[o % 2][t], 1)

            def both_gains(q):
                cols, o = slice(512 * q, 512 * q + 512), O_FOUT + q
                for t in range(NT):
                    dve.wait_ge(acc_freed[o % 2][t], o // 2 + 1)
                    ins = dve.tensor_tensor(HG[:, t, cols], HB[:, t, cols], G[:, cols], ALU.mult)
                ins.then_inc(step["hg_ready"], 1)
                dve.wait_ge(step["hg_ready"], q + 1)

            def residual_gained(q):
                cols = slice(512 * q, 512 * q + 512)
                for t in range(NT):
                    ins = dve.tensor_tensor(XG[:, t, cols], X[:, t, cols], G[:, cols], ALU.mult)
                after(ins)

            def fox_added(q):
                cols = slice(512 * q, 512 * q + 512)
                for t in range(NT):
                    ins = dve.scalar_tensor_tensor(out=X[:, t, cols], in0=HB[:, t, cols],
                                                   scalar=rstd[:, 4, t:t + 1], in1=X[:, t, cols],
                                                   op0=ALU.mult, op1=ALU.add)
                ins.then_inc(sum_ready, 1)

            def last_gain(q):
                dve.wait_ge(ssq_ready, 18 + q)
                dve.wait_ge(g_landed, 16 * 4)
                cols = slice(512 * q, 512 * q + 512)
                for t in range(NT):
                    ins = dve.tensor_tensor(HB[:, t, cols], HB[:, t, cols], G[:, cols], ALU.mult)
                ins.then_inc(step["hb_gained"], 1)

            attn_probs(1, 15, Lf, FST)
            take(*prev)
            lo(B_FOUT, 1)
            for n in range(2, 6):
                fox_low(n)
            for n in range(DOWN):
                for j in range(4):
                    if n or j >= 2:
                        lo(B_FOUT + n, j)
                    if n == 0 and j >= 2:
                        fox_low(j + 4)
                    if n and j == 1:
                        fox_panel(n - 1)
                        both_gains(n - 1)
                    if n and j == 2:
                        residual_gained(n - 1)
                    if n == 3 and j == 3:
                        residual_gained(3)
            lo(B_M2, 0)
            mean_square(4, 13).then_inc(var_ready, 1)
            fox_panel(3)
            inverse_root(4, 3)

            def both(q):
                cols = slice(512 * q, 512 * q + 512)
                for t in range(NT):
                    ins = dve.scalar_tensor_tensor(out=HG[:, t, cols], in0=HG[:, t, cols],
                                                   scalar=rstd[:, 4, t:t + 1], in1=XG[:, t, cols],
                                                   op0=ALU.mult, op1=ALU.add)
                ins.then_inc(xn_ready, 1)

            both(0)
            both(1)
            low_quarter(3, 0)
            lo(B_M2, 1)
            low_quarter(3, 1)
            both(2)
            both_gains(3)
            both(3)
            low_quarter(3, 2)
            lo(B_M2, 2)
            low_quarter(3, 3)
            mlp(B_M2, O_M2, 2 * UP, HB, 3)
            add_panel(O_M2 + 2 * O_HALF - 1, B_END - 1, DOWN - 1, HB, rstd[:, 3, :])
            summed(O_M2 + 2 * O_HALF - 1)
            mean_square(5, 21).then_inc(var_ready, 1)
            last_gain(3)
            inverse_root(5, 4)
            dve.wait_ge(step["hb_gained"], 4)
            for q in range(4):
                cols = slice(512 * q, 512 * q + 512)
                for t in range(NT):
                    ins = dve.scalar_tensor_tensor(out=X[:, t, cols], in0=HB[:, t, cols], scalar=rstd[:, 5, t:t + 1],
                                                   in1=X[:, t, cols], op0=ALU.mult, op1=ALU.add)
                ins.then_inc(x_final, 1)

        @block.tensor
        def _(pe):
            def acc_wait(o, n=None):
                n = o // 2 if n is None else n
                if not (isinstance(n, int) and n == 0):
                    for t in range(2):
                        pe.wait_ge(acc_freed[o % 2][t], n)

            def rows(b, j, o_par, first, last, k0, h=XH, l=XL):
                pe.wait_ge(lo_ready, 4 * b + j + 1)
                for kk in range(4):
                    for t in range(NT):
                        o = acc[o_par][t][:, :]
                        sh, sl = (z[:, k0 + kk, t * P:(t + 1) * P] for z in (h, l))
                        mh, ml = wh[:, j, kk, :], wl[:, j, kk, :]
                        pe.matmul(o, sh, mh, start=first and kk == 0, stop=False)
                        pe.matmul(o, sh, ml, start=False, stop=False)
                        mm = pe.matmul(o, sl, mh, start=False, stop=last and kk == 3)
                mm.then_inc(chunk_used, 1)

            def cols(b, j, o_par, first, last, k0):
                pe.wait_ge(lo_ready, 4 * b + j + 1)
                for kk in range(4):
                    for f in range(4):
                        o = acc[o_par][f // 2][:, TOK * (f % 2):TOK * (f % 2 + 1)]
                        sh, sl = (z[:, j, kk, f * P:(f + 1) * P] for z in (wh, wl))
                        mh, ml = XH[:, k0 + kk, :], XL[:, k0 + kk, :]
                        pe.matmul(o, sh, mh, start=first and kk == 0 and f % 2 == 0, stop=False,
                                  skip_group_check=True)
                        pe.matmul(o, sh, ml, start=False, stop=False, skip_group_check=True)
                        mm = pe.matmul(o, sl, mh, start=False, stop=last and kk == 3, skip_group_check=True)
                mm.then_inc(chunk_used, 1)

            def turn_quarter(m, q):
                pe.wait_ge(xn_ready, 4 * m + q + 1)
                src = (XN0, HB, HB, HG)[m]
                for n in (2 * q, 2 * q + 1):
                    wait_free(pe, ("xt", m, n))
                    bk = side_bank(("xt", m, n))
                    for i in range(4):
                        k, t = 2 * n + i // 2, i % 2
                        mm = pe.transpose(bk[:, i * P:(i + 1) * P], src[:, t, k * P:(k + 1) * P], ident[:, :])
                    full(mm, ("xt", m, n))

            def first_panel(form, m, b, o, plan={}):
                late = m in (1, 2)
                if not late:
                    turn_quarter(m, 0)
                    turn_quarter(m, 1)
                for j in range(4):
                    if j == 0:
                        acc_wait(o)
                    wait_emptied(pe, ("xt", m, 2 * j))
                    wait_emptied(pe, ("xt", m, 2 * j + 1))
                    form(b, j, o % 2, j == 0, j == 3, 4 * j)
                    if late and j == 1:
                        turn_quarter(m, 3)
                    if not late and j < 2:
                        turn_quarter(m, j + 2)
                    side_work(plan, j)

            def panel(form, b, o, plan={}, slot=0):
                acc_wait(o)
                for j in range(4):
                    if form is cols:
                        cols(b, j, o % 2, j == 0, j == 3, 4 * j)
                    else:
                        rows(b, j, o % 2, j == 0, j == 3, 4 * j)
                    side_work(plan, slot + j)

            def mlp(m, b0, o0, u0):
                for half in range(2):
                    b, o, u = b0 + half * B_HALF, o0 + half * O_HALF, u0 + half * UP
                    if half == 0:
                        first_panel(cols, m, b, o)
                    else:
                        panel(cols, b, o)
                    with pe.Fori(0, UP // 2 - 1) as i:
                        for s in (1, 2):
                            for k in range(2):
                                pe.wait_ge(acc_freed[(o + s) % 2][k], i + (o + s) // 2)
                            for j in range(4):
                                cols(b + 2 * i + s, j, (o + s) % 2, j == 0, j == 3, 4 * j)
                    panel(cols, b + UP - 1, o + UP - 1)
                    for n in range(DOWN):
                        on = o + UP + n
                        acc_wait(on)
                        for j in range(8):
                            if n == 0:
                                pe.wait_ge(hl_ready, 2 * (u + j) + 4)
                            rows(b + UP + 2 * n + j // 4, j % 4, on % 2, j == 0, j == 7, 4 * j, hh, hl)
                            if half == 1 and m == 1 and n > 0 and j == 3:
                                turn_quarter(2, n - 1)

            def attn_scores(a, h):
                bk = side_bank(("S", a, h))
                q, k = (FQ[:, h, :], FK[:, h, :]) if a else (QT[:, h, :], KTt[:, h // (HEADS_A // KV_A), :])
                for t in range(NT):
                    mm = pe.matmul(bk[:, ctr(t)], q[:, t * P:(t + 1) * P], k[:, 0:(t + 1) * P],
                                   start=True, stop=not a)
                    if a:
                        mm = pe.matmul(bk[:, ctr(t)], OH[:, h:h + 1].broadcast_to([3 * HEADS_F, P]),
                                       NCT[:, 0:(t + 1) * P], start=False, stop=True)
                return mm

            def attn_turn(a, h, L):
                pe.wait_ge(step["probs_ready"], a * HEADS_A + h + 1)
                bk = side_bank(("PT", a, h))
                for i in range(3):
                    mm = pe.transpose(bk[:, i * P:(i + 1) * P], L[:, h % L.shape[1], i * P:(i + 1) * P], ident[:, :])
                return mm

            def attn_values(a, h, PT):
                wait_emptied(pe, ("PT", a, h))
                o = (O_FOX + 8 + h // 4) if a else (O_WIN + 10)
                if not a or h % 4 == 0:
                    for t in range(NT):
                        pe.wait_ge(acc_freed[o % 2][t], o // 2 + 1)
                bk = side_bank(("O", a, h))
                vs = FV if a else V
                kv = h if a else h // (HEADS_A // KV_A)
                c = slice(kv * HD, (kv + 1) * HD)
                pe.matmul(bk[:, 0:TOK], vs[:, 0, c], PT[:, h, 0:TOK], start=True, stop=False)
                return pe.matmul(bk[:, P:TOK], vs[:, 1, c], PT[:, h, TOK:3 * P], start=False, stop=True)

            def index_scores(g):
                t, per, hs = score_heads(g)
                for i in range(per):
                    h, width = hs[i], P * (t + 1)
                    p0 = HD_I * (h % 2)
                    mm = pe.matmul(side_bank(("score", g))[:, width * i:width * (i + 1)],
                                   QI[p0:p0 + HD_I, h // 2, t * P:(t + 1) * P], KIT[p0:p0 + HD_I, 0:width],
                                   start=True, stop=True)
                return mm

            def turn4(name, blocks):
                for i, blk in enumerate(blocks):
                    mm = pe.transpose(side_bank(name)[:, i * P:(i + 1) * P], blk, ident[:, :])
                return mm

            def fill(name):
                wait_free(pe, name)
                bk = side_bank(name)
                kind = name if isinstance(name, str) else name[0]
                if kind == "narrow":
                    m = name[1]
                    pe.wait_ge(narrow_low, m // 2 + 1)
                    h, _, l = narrow[m]
                    o = bk[0:h.shape[2], 0:TOK]
                    for k in range(KT):
                        pe.matmul(o, h[:, k, :], XH[:, k, :], start=k == 0, stop=False)
                        pe.matmul(o, h[:, k, :], XL[:, k, :], start=False, stop=False)
                        mm = pe.matmul(o, l[:, k, :], XH[:, k, :], start=False, stop=k == KT - 1)
                elif kind == "narrow_rows":
                    m = name[1]
                    src = FTT if m else SMT
                    wait_emptied(pe, ("narrow", m))
                    w = src.shape[0]
                    for t in range(NT):
                        mm = pe.transpose(bk[:, t * w:(t + 1) * w], src[:, t * P:(t + 1) * P], ident[0:w, 0:w])
                elif kind == "rbc":
                    pe.wait_ge(step["rs_ready"], 1 if name[1] == 0 else 2)
                    for t in range(NT):
                        mm = pe.matmul(bk[:, t * P:(t + 1) * P], rstd[:, name[1], t:t + 1].broadcast_to([P, P]),
                                       ident[:, :], start=True, stop=True)
                elif kind == "params":
                    pe.wait_ge(vec_landed, 16 * 8)
                    mm = pe.transpose(bk[:, 0:62], PR[:, :], ident[0:62, 0:62])
                elif kind == "ki":
                    pe.wait_ge(step["ki_rows"], 4)
                    mm = turn4(name, [KI2[:, t, :] for t in range(NT)])
                elif kind == "score":
                    if name[1] == 0:
                        wait_emptied(pe, "ki")
                    mm = index_scores(name[1])
                elif kind == "cum":
                    c = name[1]
                    pe.wait_ge(step["adt_ready"], 1)
                    pe.wait_ge(consts_ready, 3)
                    adt = DTS[:, 7, 16 * c:16 * c + 16]
                    pe.matmul(bk[:, 0:16], Um[:, :], adt, start=True, stop=True)
                    mm = pe.matmul(bk[:, 16:32], Vm[:, :], adt, start=True, stop=True)
                elif kind == "seg":
                    c, n = name[1:]
                    pe.wait_ge(step["decay_in"], c + 1)
                    mm = pe.matmul(bk[:, :], Vm[:, :], E[:, 4 * n:4 * n + 4, :].rearrange("p h l -> p (h l)"),
                                   start=True, stop=True)
                elif kind == "xst":
                    n = name[1]
                    pe.wait_ge(step["silu_done"], 3 if n == 4 else (n % 2) + 1)
                    where = [(n // 2, 4 * (n % 2) + i) if n < 4 else (i // 2, 8 + i % 2) for i in range(4)]
                    mm = turn4(name, [XC[:, k, t * P:(t + 1) * P] for t, k in where])
                elif kind == "cb":
                    for c in range(NT):
                        for g in range(GROUPS):
                            tk = slice(c * P, (c + 1) * P)
                            mm = pe.matmul(bk[:, (2 * c + g) * P:(2 * c + g + 1) * P],
                                           XC[:, 8 + g, tk], XC[:, 10 + g, tk], start=True, stop=True)
                elif kind == "state":
                    g = name[1]
                    pe.wait_ge(step["st_ready"], 1)
                    wait_emptied(pe, ("xst", 4))
                    mm = pe.matmul(bk[:, :], BM[:, 0, g * STATE:(g + 1) * STATE], XDD[:, 512 * g:512 * g + 512],
                                   start=True, stop=True)
                elif kind == "diag":
                    c, g = name[1:]
                    wait_emptied(pe, ("xst", 2 * c + g))
                    pe.wait_ge(step["m_ready"], 2 * c + g + 1)
                    for i in range(HPG):
                        h = HPG * g + i
                        mm = pe.matmul(bk[:, i * HD_S:(i + 1) * HD_S], E[:, h, :],
                                       XD[:, c, h * HD_S:(h + 1) * HD_S], start=True, stop=True)
                elif kind == "off":
                    g = name[1]
                    wait_emptied(pe, ("state", g))
                    mm = pe.matmul(bk[:, :], XC[:, 10 + g, P:2 * P], ST[:, g, :], start=True, stop=True)
                elif kind == "qkt":
                    n = name[1]
                    pe.wait_ge(step["qk_normed"], 6 if n >= 4 else 4 if n >= 2 else 2)
                    src, h0 = (Q, 2 * n) if n < 4 else (K, 2 * n - 8)
                    mm = turn4(name, [src[:, i % 2, (h0 + i // 2) * HD:(h0 + i // 2 + 1) * HD] for i in range(4)])
                elif kind == "yt":
                    n = name[1]
                    pe.wait_ge(step["yn_ready"], 2 * (n // 2) + 2)
                    mm = turn4(name, [Y[:, i % 2, (2 * n + i // 2) * P:(2 * n + i // 2 + 1) * P] for i in range(4)])
                elif kind == "S":
                    a, h = name[1:]
                    if a:
                        wait_emptied(pe, "fct")
                        pe.wait_ge(consts_ready, 4)
                        o = O_FOX + 1 + 2 * (h // 4)
                        for t in range(NT):
                            for x in (o, o - 1):
                                pe.wait_ge(acc_freed[x % 2][t], x // 2 + 1)
                    elif h == 0:
                        for n in range(6):
                            wait_emptied(pe, ("qkt", n))
                    mm = attn_scores(a, h)
                elif kind == "PT":
                    mm = attn_turn(name[1], name[2], Lf if name[1] else Lm)
                elif kind == "O":
                    mm = attn_values(name[1], name[2], PTf if name[1] else PTm)
                elif kind == "fcum":
                    pe.wait_ge(step["lf_ready"], 1)
                    pe.wait_ge(consts_ready, 4)
                    pe.matmul(bk[:, 0:16], Uf[:, :], FS[:, 7, 0:16], start=True, stop=True)
                    pe.matmul(bk[:, 16:32], ONE[:, :], FS[:, 7, 0:16], start=True, stop=False)
                    mm = pe.matmul(bk[:, 16:32], Uf[:, :], FS[:, 7, 16:32], start=False, stop=True)
                else:
                    pe.wait_ge(step["nc_ready"], 1)
                    for t in range(NT):
                        mm = pe.transpose(bk[0:3 * HEADS_F, t * P:(t + 1) * P], NC[:, t, :], ident[:, :])
                full(mm, name)

            def side_work(plan, n):
                for name in plan.get(n, ()):
                    fill(name)

            pe.wait_ge(consts_ready, 1)
            first_panel(cols, 0, B_WIN, O_WIN, MIX_AT)
            for n, (kind, col) in enumerate(WIN):
                if n:
                    panel(cols if kind in TFORM else rows, B_WIN + n, O_WIN + n, MIX_AT, 4 * n)
            side_work(MIX_AT, 44)
            acc_wait(O_WOUT)
            for j in range(4):
                if j == 1:
                    side_work(MIX_AT, 45)
                elif j > 1:
                    side_work(MIX_AT, 44 + j)
                for n in ((("yt", 2 * j), ("yt", 2 * j + 1)) if j < 2 else
                          [("O", 0, h) for h in range(4 * j - 8, 4 * j - 4)]):
                    wait_emptied(pe, n)
                rows(B_WOUT, j, O_WOUT % 2, j == 0, j == 3, 4 * j)
            for n in range(1, DOWN):
                acc_wait(O_WOUT + n)
                for j in range(4):
                    rows(B_WOUT + n, j, (O_WOUT + n) % 2, j == 0, j == 3, 4 * j)
                    if n == DOWN - 1 and j < 3:
                        turn_quarter(1, j)
            mlp(1, B_M1, O_M1, 0)
            first_panel(cols, 2, B_FOX, O_FOX, FOX_AT)
            for n, (kind, col) in enumerate(FOX):
                if n:
                    panel(cols if kind in TFORM else rows, B_FOX + n, O_FOX + n, FOX_AT, 4 * n)
            acc_wait(O_FOUT)
            for j in range(4):
                pe.wait_ge(step["fl_ready"], 2 * j + 2)
                rows(B_FOUT, j, O_FOUT % 2, j == 0, j == 3, 4 * j)
                if j < 2:
                    side_work(FOX_AT, 48 + j)
            for n in range(1, DOWN):
                panel(rows, B_FOUT + n, O_FOUT + n)
            mlp(3, B_M2, O_M2, 2 * UP)


_INS = ['x', 'g_mix', 'w_in', 'conv_w', 'conv_b', 'dt_bias', 'a_log', 'd_skip', 'g_ssd', 'g_q', 'g_k', 'g_kidx',
        'w_out', 'g_mlp', 'w_up', 'w_down', 'norm_g_2', 'mlp_w1_2', 'mlp_w2_2', 'fox_w_in_2', 'fox_b_f_2',
        'fox_w_out_2']


def kernel(**inputs):
    import numpy as np
    import concourse.bacc as bacc
    from concourse.bass_utils import run_bass_kernel_spmd

    nc = bacc.Bacc("TRN2", target_bir_lowering=False, num_devices=1)
    arrays, args = {}, []
    for name in _INS:
        a = np.ascontiguousarray(inputs[name])
        arrays[f"in_{name}_dram"] = a
        args.append(nc.dram_tensor(f"in_{name}_dram", a.shape, mybir.dt.from_np(a.dtype),
                                   kind="ExternalInput").ap())
    args.append(nc.dram_tensor("out_dram", (1, TOK, D), F32, kind="ExternalOutput").ap())
    hybrid_then_fox(nc, *args)
    return run_bass_kernel_spmd(nc, [arrays], core_ids=[0]).results[0]["out_dram"]
```
